# Optimizing a Trainium2 kernel written in Bass

```python
import math
import numpy as np
import jax
import jax.numpy as jnp
from jax import lax

D_MODEL = 1024
BATCH = 1
SEQ = 256
DEPTH = 2

GRID_W = 64
CTX_LEN = 256
ROPE_BASE = 10000.0
Q_BLOCK = 128

DA_HEADS = 4
DA_HEAD_DIM = 64
DA_QK = DA_HEADS * 2 * DA_HEAD_DIM
DA_V = DA_HEADS * 2 * DA_HEAD_DIM
DA_OUT = DA_V

MLA_HEADS = 4
MLA_Q_RANK = 256
MLA_KV_RANK = 128
MLA_NOPE = 64
MLA_ROPE = 32
MLA_V = 64
MLA_OUT = MLA_HEADS * MLA_V

HG_HEADS = 4
HG_KEY = 64
HG_VAL = 64
HG_WIDTH = HG_HEADS * HG_KEY
HG_OUT = HG_HEADS * HG_VAL
HG_CHUNK = 64

D_MIX = DA_OUT + MLA_OUT + HG_OUT
IN_SPLITS = (DA_QK, DA_QK, DA_V, MLA_Q_RANK, MLA_KV_RANK, MLA_ROPE, HG_WIDTH, HG_OUT, HG_WIDTH, HG_WIDTH, HG_OUT)
IN_COLS = sum(IN_SPLITS)

D_FF = 2816
N_EXPERTS = 8
TOP_K = 2
D_FF_EXPERT = 2816
N_DENSE = (DEPTH + 1) // 2
N_MOE = DEPTH // 2

kernel_name = "hybrid_diffattn_mla_hgrn2_moe_dit"

def rmsnorm(x, g, eps=1e-6):
    xf = x.astype(jnp.float32)
    y = xf * lax.rsqrt(jnp.mean(xf * xf, axis=-1, keepdims=True) + eps)
    return y.astype(x.dtype) * g

def modulate(h, shift, scale):
    return h * (1.0 + scale) + shift

def split_columns(p):
    out, start = [], 0
    for size in IN_SPLITS:
        out.append(p[..., start:start + size])
        start += size
    return out

def axial_rope_tables(L, rot_dim, dtype):
    rows = L // GRID_W
    row, col = jnp.meshgrid(jnp.arange(rows, dtype=jnp.float32), jnp.arange(GRID_W, dtype=jnp.float32), indexing="ij")
    row, col = row.reshape(-1), col.reshape(-1)
    n_freq = rot_dim // 4
    inv = ROPE_BASE ** (-jnp.arange(n_freq, dtype=jnp.float32) / n_freq)
    ang = jnp.concatenate([row[:, None] * inv, col[:, None] * inv], axis=-1)
    return jnp.cos(ang).astype(dtype), jnp.sin(ang).astype(dtype)

def apply_rope(x, cos, sin):
    half = x.shape[-1] // 2
    x1, x2 = x[..., :half], x[..., half:]
    return jnp.concatenate([x1 * cos - x2 * sin, x2 * cos + x1 * sin], axis=-1)

def sdpa(q, k, v, scale):
    s = jnp.einsum("bhgqd,bhgkd->bhgqk", q, k).astype(jnp.float32) * scale
    p = jax.nn.softmax(s, axis=-1).astype(v.dtype)
    return jnp.einsum("bhgqk,bhkv->bhgqv", p, v)

def blocked_attention(q, k, v, scale):
    B, H, G, L, d = q.shape
    nb = L // Q_BLOCK
    qb = jnp.moveaxis(q.reshape(B, H, G, nb, Q_BLOCK, d), 3, 0)
    ob = lax.map(lambda qi: sdpa(qi, k, v, scale), qb)
    return jnp.moveaxis(ob, 0, 3).reshape(B, H, G, L, v.shape[-1])

def diff_attention(pl, pc, lam_vec, gain, lam_init, rope, need_ctx):
    cos, sin = rope

    def heads_qk(a):
        B, L, _ = a.shape
        return a.reshape(B, L, DA_HEADS, 2, DA_HEAD_DIM).transpose(0, 2, 3, 1, 4)

    def heads_v(a):
        B, L, _ = a.shape
        return a.reshape(B, L, DA_HEADS, 2 * DA_HEAD_DIM).transpose(0, 2, 1, 3)

    lv = lam_vec.astype(jnp.float32)
    lam = jnp.exp(jnp.sum(lv[0] * lv[1])) - jnp.exp(jnp.sum(lv[2] * lv[3])) + lam_init
    scale = DA_HEAD_DIM ** -0.5

    def combine(o):
        B, H, _, L, dv = o.shape
        o = o[:, :, 0] - lam.astype(o.dtype) * o[:, :, 1]
        o = rmsnorm(o, gain, 1e-5) * (1.0 - lam_init)
        return o.transpose(0, 2, 1, 3).reshape(B, L, H * dv)

    q_l = apply_rope(heads_qk(pl[0]), cos, sin)
    k_l = apply_rope(heads_qk(pl[1]), cos, sin)
    v_l = heads_v(pl[2])
    k_c, v_c = heads_qk(pc[1]), heads_v(pc[2])
    o = combine(blocked_attention(q_l, jnp.concatenate([k_c, k_l], axis=3), jnp.concatenate([v_c, v_l], axis=2), scale))
    o_c = combine(sdpa(heads_qk(pc[0]), k_c, v_c, scale)) if need_ctx else None
    return o, o_c

def latent_attention(pl, pc, q_norm, w_uq, kv_norm, w_ukv, rope, need_ctx):
    cos, sin = rope
    scale = (MLA_NOPE + MLA_ROPE) ** -0.5

    def queries(cq, rotate):
        B, L, _ = cq.shape
        q = (rmsnorm(cq, q_norm) @ w_uq).reshape(B, L, MLA_HEADS, MLA_NOPE + MLA_ROPE).transpose(0, 2, 1, 3)
        q_nope, q_rope = q[..., :MLA_NOPE], q[..., MLA_NOPE:]
        if rotate:
            q_rope = apply_rope(q_rope, cos, sin)
        return jnp.concatenate([q_nope, q_rope], axis=-1)[:, :, None]

    def keys_values(ckv, kr, rotate):
        B, L, _ = ckv.shape
        kv = (rmsnorm(ckv, kv_norm) @ w_ukv).reshape(B, L, MLA_HEADS, MLA_NOPE + MLA_V).transpose(0, 2, 1, 3)
        k_rope = kr[:, None]
        if rotate:
            k_rope = apply_rope(k_rope, cos, sin)
        k = jnp.concatenate([kv[..., :MLA_NOPE], jnp.broadcast_to(k_rope, (B, MLA_HEADS, L, MLA_ROPE))], axis=-1)
        return k[:, :, None], kv[..., MLA_NOPE:]

    def merge(o):
        B, H, _, L, dv = o.shape
        return o[:, :, 0].transpose(0, 2, 1, 3).reshape(B, L, H * dv)

    k_l, v_l = keys_values(pl[1], pl[2], True)
    k_c, v_c = keys_values(pc[1], pc[2], False)
    o = merge(blocked_attention(queries(pl[0], True), jnp.concatenate([k_c, k_l], axis=3), jnp.concatenate([v_c, v_l], axis=2), scale))
    o_c = merge(sdpa(queries(pc[0], False), k_c, v_c, scale)) if need_ctx else None
    return o, o_c

def chunk_scan(q, k, v, logf, s0):
    B, H, L, dk = q.shape
    dv = v.shape[-1]
    n = L // HG_CHUNK

    def chunks(a):
        return jnp.moveaxis(a.astype(jnp.float32).reshape(B, H, n, HG_CHUNK, a.shape[-1]), 2, 0)

    lower = jnp.tril(jnp.ones((HG_CHUNK, HG_CHUNK), bool))[:, :, None]

    def step(s, inp):
        qc, kc, vc, gc = inp
        b = jnp.cumsum(gc, axis=2)
        b_last = b[:, :, -1:, :]
        o_inter = jnp.einsum("bhtd,bhde->bhte", qc * jnp.exp(b), s)
        rel = jnp.exp(jnp.where(lower, b[:, :, :, None, :] - b[:, :, None, :, :], -jnp.inf))
        scores = jnp.einsum("bhtd,bhtsd,bhsd->bhts", qc, rel, kc)
        o = o_inter + jnp.einsum("bhts,bhse->bhte", scores, vc)
        s_new = jnp.exp(b_last[:, :, 0, :])[..., None] * s + jnp.einsum("bhsd,bhse->bhde", kc * jnp.exp(b_last - b), vc)
        return s_new, o

    s_final, o = lax.scan(step, s0.astype(jnp.float32), (chunks(q), chunks(k), chunks(v), chunks(logf)))
    return jnp.moveaxis(o, 0, 2).reshape(B, H, L, dv), s_final

def final_state(k, v, logf):
    b = jnp.cumsum(logf.astype(jnp.float32), axis=2)
    return jnp.einsum("bhsd,bhse->bhde", k.astype(jnp.float32) * jnp.exp(b[:, :, -1:] - b), v.astype(jnp.float32))

def hgrn2(pl, pc, lb_fwd, lb_bwd, gain, need_ctx):
    def heads(a):
        B, L, _ = a.shape
        return a.reshape(B, L, HG_HEADS, -1).transpose(0, 2, 1, 3)

    def gates(f_raw, lb):
        z = heads(f_raw).astype(jnp.float32)
        lb = lb.reshape(HG_HEADS, 1, HG_KEY)
        return (1.0 - lb) * jax.nn.sigmoid(-z), jnp.log(lb + (1.0 - lb) * jax.nn.sigmoid(z))

    def flip(a):
        return a[:, :, ::-1]

    def readout(o, g):
        B, H, L, dv = o.shape
        o = rmsnorm(o, gain).transpose(0, 2, 1, 3).reshape(B, L, H * dv)
        return o.astype(g.dtype) * jax.nn.silu(g)

    q_l, i_l, ff_l, fb_l, g_l = pl
    q_c, i_c, ff_c, fb_c, g_c = pc
    scale = HG_KEY ** -0.5
    v_l, v_c = heads(i_l), heads(i_c)
    kf_l, logf_l = gates(ff_l, lb_fwd)
    kb_l, logb_l = gates(fb_l, lb_bwd)
    kf_c, logf_c = gates(ff_c, lb_fwd)
    kb_c, logb_c = gates(fb_c, lb_bwd)
    if need_ctx:
        qc = heads(q_c) * scale
        zeros = jnp.zeros(qc.shape[:2] + (HG_KEY, HG_VAL), jnp.float32)
        oc_f, s_fwd = chunk_scan(qc, kf_c, v_c, logf_c, zeros)
        oc_b, s_bwd = chunk_scan(flip(qc), flip(kb_c), flip(v_c), flip(logb_c), zeros)
        o_c = readout(oc_f + flip(oc_b), g_c)
    else:
        s_fwd = final_state(kf_c, v_c, logf_c)
        s_bwd = final_state(flip(kb_c), flip(v_c), flip(logb_c))
        o_c = None
    ql = heads(q_l) * scale
    o_f, _ = chunk_scan(ql, kf_l, v_l, logf_l, s_fwd)
    o_b, _ = chunk_scan(flip(ql), flip(kb_l), flip(v_l), flip(logb_l), s_bwd)
    return readout(o_f + flip(o_b), g_l), o_c

def swiglu(h, w_gate, w_up, w_down):
    return (jax.nn.silu(h @ w_gate) * (h @ w_up)) @ w_down

def moe_swiglu(h, router, w_gate, w_up, w_down):
    B, L, D = h.shape
    t = h.reshape(B * L, D)
    logits = (t @ router).astype(jnp.float32)
    top_logit, top_idx = lax.top_k(logits, TOP_K)
    top_w = jax.nn.softmax(top_logit, axis=-1)
    gates = jnp.einsum("nk,nke->ne", top_w, jax.nn.one_hot(top_idx, N_EXPERTS, dtype=jnp.float32)).astype(h.dtype)
    out = jnp.zeros_like(t)
    for e in range(N_EXPERTS):
        out = out + gates[:, e:e + 1] * swiglu(t, w_gate[e], w_up[e], w_down[e])
    return out.reshape(B, L, D)

def setup_inputs(seed: int = 0) -> dict:
    key = jax.random.key(seed)
    ks = jax.random.split(key, 26)
    f32 = jnp.float32
    D = D_MODEL

    def normal(i, shape, scale):
        return scale * jax.random.normal(ks[i], shape, f32)

    def gain(i, shape):
        return 1.0 + 0.05 * jax.random.normal(ks[i], shape, f32)

    return {
        "x": normal(0, (BATCH, SEQ, D), 1.0),
        "c": normal(1, (BATCH, D), 1.0),
        "ctx": normal(2, (BATCH, CTX_LEN, D), 1.0),
        "c_ctx": normal(3, (D,), 1.0),
        "w_mod": normal(4, (DEPTH, D, 6 * D), 0.5 * D ** -0.5),
        "b_mod": normal(5, (DEPTH, 6 * D), 0.02),
        "norm_mix": gain(6, (DEPTH, D)),
        "norm_ffn": gain(7, (DEPTH, D)),
        "norm_final": gain(8, (D,)),
        "w_in": normal(9, (DEPTH, D, IN_COLS), D ** -0.5),
        "w_out": normal(10, (DEPTH, D_MIX, D), D_MIX ** -0.5),
        "diff_lambda": normal(11, (DEPTH, 4, DA_HEAD_DIM), 0.1),
        "diff_norm": gain(12, (DEPTH, 2 * DA_HEAD_DIM)),
        "mla_q_norm": gain(13, (DEPTH, MLA_Q_RANK)),
        "mla_w_uq": normal(14, (DEPTH, MLA_Q_RANK, MLA_HEADS * (MLA_NOPE + MLA_ROPE)), MLA_Q_RANK ** -0.5),
        "mla_kv_norm": gain(15, (DEPTH, MLA_KV_RANK)),
        "mla_w_ukv": normal(16, (DEPTH, MLA_KV_RANK, MLA_HEADS * (MLA_NOPE + MLA_V)), MLA_KV_RANK ** -0.5),
        "hgrn_lb_logits": normal(17, (2, DEPTH, HG_WIDTH), 0.5),
        "hgrn_norm": gain(18, (DEPTH, HG_VAL)),
        "ffn_w_gate": normal(19, (N_DENSE, D, D_FF), D ** -0.5),
        "ffn_w_up": normal(20, (N_DENSE, D, D_FF), D ** -0.5),
        "ffn_w_down": normal(21, (N_DENSE, D_FF, D), D_FF ** -0.5),
        "moe_router": normal(22, (N_MOE, D, N_EXPERTS), D ** -0.5),
        "moe_w_gate": normal(23, (N_MOE, N_EXPERTS, D, D_FF_EXPERT), D ** -0.5),
        "moe_w_up": normal(24, (N_MOE, N_EXPERTS, D, D_FF_EXPERT), D ** -0.5),
        "moe_w_down": normal(25, (N_MOE, N_EXPERTS, D_FF_EXPERT, D), D_FF_EXPERT ** -0.5),
    }

def reference(x, c, ctx, c_ctx, w_mod, b_mod, norm_mix, norm_ffn, norm_final, w_in, w_out,
              diff_lambda, diff_norm, mla_q_norm, mla_w_uq, mla_kv_norm, mla_w_ukv,
              hgrn_lb_logits, hgrn_norm, ffn_w_gate, ffn_w_up, ffn_w_down,
              moe_router, moe_w_gate, moe_w_up, moe_w_down):
    L = x.shape[1]
    rope_da = axial_rope_tables(L, DA_HEAD_DIM, x.dtype)
    rope_mla = axial_rope_tables(L, MLA_ROPE, x.dtype)
    lb = jnp.cumsum(jax.nn.softmax(hgrn_lb_logits.astype(jnp.float32), axis=1), axis=1)
    lb = lb - lb[:, :1]
    cond = jax.nn.silu(c)
    cond_ctx = jax.nn.silu(c_ctx)
    xc = ctx
    for l in range(DEPTH):
        need_ctx = l < DEPTH - 1
        mod = [m[:, None, :] for m in jnp.split(cond @ w_mod[l] + b_mod[l], 6, axis=-1)]
        mod_c = jnp.split(cond_ctx @ w_mod[l] + b_mod[l], 6, axis=-1)
        lam_init = 0.8 - 0.6 * math.exp(-0.3 * l)

        h = modulate(rmsnorm(x, norm_mix[l]), mod[0], mod[1])
        hc = modulate(rmsnorm(xc, norm_mix[l]), mod_c[0], mod_c[1])
        pl = split_columns(h @ w_in[l])
        pc = split_columns(hc @ w_in[l])
        oa, oa_c = diff_attention(pl[0:3], pc[0:3], diff_lambda[l], diff_norm[l], lam_init, rope_da, need_ctx)
        ob, ob_c = latent_attention(pl[3:6], pc[3:6], mla_q_norm[l], mla_w_uq[l], mla_kv_norm[l], mla_w_ukv[l], rope_mla, need_ctx)
        og, og_c = hgrn2(pl[6:11], pc[6:11], lb[0, l], lb[1, l], hgrn_norm[l], need_ctx)
        x = x + mod[2] * (jnp.concatenate([oa, ob, og], axis=-1) @ w_out[l])

        h = modulate(rmsnorm(x, norm_ffn[l]), mod[3], mod[4])
        if need_ctx:
            xc = xc + mod_c[2] * (jnp.concatenate([oa_c, ob_c, og_c], axis=-1) @ w_out[l])
            hc = modulate(rmsnorm(xc, norm_ffn[l]), mod_c[3], mod_c[4])
            h = jnp.concatenate([hc, h], axis=1)
        if l % 2 == 0:
            y = swiglu(h, ffn_w_gate[l // 2], ffn_w_up[l // 2], ffn_w_down[l // 2])
        else:
            y = moe_swiglu(h, moe_router[l // 2], moe_w_gate[l // 2], moe_w_up[l // 2], moe_w_down[l // 2])
        if need_ctx:
            n_ctx = xc.shape[1]
            xc = xc + mod_c[5] * y[:, :n_ctx]
            y = y[:, n_ctx:]
        x = x + mod[5] * y
    return rmsnorm(x, norm_final)


_drawn_inputs = setup_inputs


def setup_inputs(seed=0):
    import zlib

    import numpy as np

    out = dict(_drawn_inputs(seed))
    spreads = {}
    factors = {'diff_norm': 3.34, 'mla_q_norm': 8.0, 'mla_kv_norm': 8.0, 'hgrn_norm': 8.0}
    for name, (base, spread) in spreads.items():
        noise = np.random.default_rng([zlib.crc32(name.encode()), seed]).standard_normal(out[name].shape)
        drawn = base * np.exp(spread * noise) if base else spread * noise
        out[name] = jnp.asarray(drawn.astype(out[name].dtype))
    for name, factor in factors.items():
        out[name] = (out[name] * factor).astype(out[name].dtype)
    return out
```

```python
import math
from contextlib import ExitStack

import concourse.bass as bass
import numpy as np
from concourse import mybir

F32 = mybir.dt.float32
F32R = mybir.dt.float32r
ALU = mybir.AluOpType
ACT = mybir.ActivationFunctionType
AX = mybir.AxisListType

P = 128
D = 1024
KD = D // P
DEPTH = 2
SEQ = CTX = 256
TOK = SEQ + CTX
TILES = TOK // P
GRID_W, ROPE_BASE = 64, 10000.0
DA_HEADS, DA_DIM = 4, 64
MLA_HEADS, MLA_NOPE, MLA_ROPE, MLA_V, MLA_Q, MLA_KV = 4, 64, 32, 64, 256, 128
MLA_QK = MLA_NOPE + MLA_ROPE
HG_HEADS, HG_DIM = 4, 64
IN_SPLITS = (512, 512, 512, MLA_Q, MLA_KV, MLA_ROPE, 256, 256, 256, 256, 256)
IN_COLS = sum(IN_SPLITS)
(C_DQ, C_DK, C_DV, C_CQ, C_CKV, C_KR, C_HQ, C_HI, C_FF, C_FB, C_HG) = [sum(IN_SPLITS[:i]) for i in range(11)]
IN_CHUNKS = [(C_DQ, C_DK), (C_DK, C_DV), (C_DV, C_CQ), (C_CQ, C_HQ), (C_HQ, C_FF), (C_FF, C_HG), (C_HG, IN_COLS)]
CTX_KEYS_ONLY = {0: None, 3: (C_CKV, C_HQ), 4: (C_HI, C_FF), 6: None}
FF = 2816
EXPERTS = 8
SLAB = 2048
RING = 3
GU = 256
FF_CHUNKS = FF // GU
LEVELS = [1, 2, 4, 8, 16, 32, 64]
FF_GROUPS = [(0, 6), (6, 11)]


def constants():
    p = np.arange(P)
    cols = {"ident": np.eye(P)}
    same = lambda m: (p[:, None] // (2 * m) == p[None] // (2 * m)) & (p[:, None] // m != p[None] // m)
    cols["masks"] = np.concatenate([same(m) for m in LEVELS], 1)
    pos = np.arange(SEQ)
    for name, rot in (("da", DA_DIM), ("mla", MLA_ROPE)):
        n = rot // 4
        inv = (ROPE_BASE ** (-np.arange(n, dtype=np.float32) / n)).astype(np.float32)
        ang = np.concatenate([(pos // GRID_W)[:, None] * inv, (pos % GRID_W)[:, None] * inv], -1)
        ang = ang.astype(np.float32).reshape(2, P, -1)
        cols[f"cos_{name}"] = np.concatenate(list(np.cos(ang)), 1)
        cols[f"sin_{name}"] = np.concatenate(list(np.sin(ang)), 1)
    pick = np.zeros((P, 2))
    for j in range(2):
        pick[[j, j + 2, 4], j] = 1
    cols["pick"] = pick
    cols["pick_rows"] = np.repeat(pick.T[:, :, None], P, 2).transpose(1, 0, 2).reshape(P, 2 * P)
    cols["slots"] = np.tile(np.arange(P), (P, 1))
    cols["earlier"] = p[:, None] < p[None]
    cols["ones"] = np.ones((P, 1))
    cols["order8"] = np.tile(8.0 - np.arange(EXPERTS), (P, 1))
    at, n = {}, 0
    for k, v in cols.items():
        at[k] = (n, v.shape[1])
        n += v.shape[1]
    return np.concatenate(list(cols.values()), 1).astype(np.float32), at


VEC = {"norm_mix": 0, "norm_ffn": 8, "q_norm": 16, "kv_norm": 18, "lb_logits": 19}
VEC_COLS = 23
ROW = {"diff_norm": (0, 128), "hgrn_norm": (128, 64), "diff_lambda": (192, 256)}
ROW_COLS = 448


class Prologue:

    def __init__(self, signal):
        self.source = signal

    def did(self, key=None):
        return self.source.sem, 1


class Signal:

    def __init__(self, sem, known):
        self.sem, self.known, self.seen, self.count = sem, known, {}, 0

    def did(self, key=None):
        self.count += 1
        self.seen[key] = self.count
        return self.sem, 1

    def at(self, key=None):
        return self.sem, self.known.get(key, 1)

    def last(self):
        return self.sem, self.count

    def each(self):
        return len(self.known) or 1

    def turn(self, key, item):
        return self.sem, self.known.get(key, 1) + self.each() * item


def program(nc, dram, out, known, seen):
    table, at = constants()
    NCONST = table.shape[1]
    signals = {}

    with ExitStack() as ctx:

        def sig(name):
            if name not in signals:
                signals[name] = Signal(ctx.enter_context(nc.semaphore(name)), known.get(name, {}))
            return signals[name]

        cursor = [16544]

        def place(name, shape, dt=F32, offset=None):
            size = int(np.prod(shape[1:])) * 4
            where = cursor[0] if offset is None else offset
            if offset is None:
                cursor[0] += (size + 31) // 32 * 32
            return nc.alloc_sbuf_tensor_at(name, shape, dt, offset=where)

        const = place("const", [P, NCONST])
        vecs = place("vecs", [P, DEPTH, VEC_COLS])
        cond_in = place("cond_in", [P, 2 * KD])
        rows = place("rows", [P, ROW_COLS])
        lam = place("lam", [P, 8])
        lb = place("lb", [P, 4])
        one_less_lb = place("one_less_lb", [P, 4])
        small = place("small", [P, 64])
        stats = place("stats", [P, 64])
        shift_col = place("shift_col", [P, 2, KD, 2])
        scale_col = place("scale_col", [P, 2, KD, 2])
        x = place("x", [P, TILES, D])
        raw = place("raw", [P, RING, SLAB])
        w_hi = place("w_hi", [P, RING, SLAB], F32R)
        w_lo = place("w_lo", [P, RING, SLAB], F32R)
        H = cursor[0]
        hT_hi = place("hT_hi", [P, KD, TOK], F32R)
        hT_lo = place("hT_lo", [P, KD, TOK], F32R)
        PJ = cursor[0]
        pj = place("pj", [P, TILES, IN_COLS])
        F = cursor[0]
        END = 229368
        scratch_bytes = END - F

        def over(name, shape, base, dt=F32):
            size = (int(np.prod(shape[1:])) * 4 + 31) // 32 * 32
            t = nc.alloc_sbuf_tensor_at(name, shape, dt, offset=base[0])
            base[0] += size
            assert base[0] <= END, (name, base[0] - END)
            return t

        b = [PJ]
        cond4 = over("cond4", [P, KD, P], b, F32R)
        cond_act = over("cond_act", [P, 2 * KD], b)
        mod_rows = over("mod_rows", [5, 4, D], b)
        b = [F]
        gate_rows = over("gate_rows", [5, 2, D], b)
        FREE = b[0]
        b = [PJ]
        xn = over("xn", [P, TILES, D], b)
        hf = over("hf", [P, 2, TOK], b)
        b = [FREE]
        gate_all = over("gate_all", [P, 2, D], b)
        upd = over("upd", [P, 2, 512], b)
        act_gate = over("act_gate", [P, 2, GU], b)
        act_tok = over("act_tok", [P, TILES, GU], b)
        b = [H]
        daqT = over("daqT", [P, DA_HEADS, TOK], b)
        dakT = over("dakT", [P, DA_HEADS, TOK], b)
        mqT = over("mqT", [MLA_QK, MLA_HEADS, TOK], b)
        mkT = over("mkT", [MLA_QK, MLA_HEADS, TOK], b)
        assert b[0] <= PJ
        b = [FREE]
        w_uq = over("w_uq", [P, 2, MLA_HEADS * MLA_QK], b)
        w_ukv = over("w_ukv", [P, MLA_HEADS * (MLA_NOPE + MLA_V)], b)
        c_tok = over("c_tok", [P, 2, MLA_Q + MLA_KV], b)
        q_tok = over("q_tok", [P, 2, MLA_HEADS, MLA_QK], b)
        k_tok = over("k_tok", [P, 2, MLA_HEADS, MLA_QK], b)
        rope_tmp = over("rope_tmp", [P, 2, 512], b)
        cT = over("cT", [P, 3, P], b)
        b = [FREE]
        probs = over("probs", [P, 2, 2, TOK], b)
        probsT = over("probsT", [P, 2, 4, P], b)
        b = [H]
        hqT = over("hqT", [P, 2, TOK], b)
        sig_f = over("sig_f", [P, 4, TOK], b)
        hkT = over("hkT", [P, 4, TOK], b)
        cum = over("cum", [P, 4, TOK], b)
        s_far = over("s_far", [P, 2, 2, SEQ], b)
        assert b[0] <= PJ, b[0] - PJ
        b = [H + 4 * TOK * 2]
        s_diag = over("s_diag", [P, 2, TILES, P], b)
        s_off = over("s_off", [P, 2, 2, 2, P], b)
        b = [FREE]
        dec = over("dec", [P, 2, 4, SEQ], b)
        lev_k = over("lev_k", [P, 2, 2, TOK], b)
        lev_q = pj[:, :, C_DV:C_DV + 2 * SEQ].rearrange("p (b d) (h s) -> p b d h s", b=2, h=2)
        assert b[0] <= END
        b = [FREE]
        ro = over("ro", [P, 2, 768], b)
        b = [PJ]
        AK = 2 * max(e - s for s, e in FF_GROUPS)
        aT_hi = over("aT_hi", [P, AK, TOK], b, F32R)
        aT_lo = over("aT_lo", [P, AK, TOK], b, F32R)
        assert b[0] <= F

        b = [PJ]
        h_tok_hi = over("h_tok_hi", [P, 2, D], b, F32R)
        h_tok_lo = over("h_tok_lo", [P, 2, D], b, F32R)
        hg_hi = over("hg_hi", [P, KD, P], b, F32R)
        hg_lo = over("hg_lo", [P, KD, P], b, F32R)
        eT_hi = over("eT_hi", [P, 2 * FF_CHUNKS, P], b, F32R)
        eT_lo = over("eT_lo", [P, 2 * FF_CHUNKS, P], b, F32R)
        pick_tok = over("pick_tok", [P, 2, P], b, F32R)
        assert b[0] <= F
        b = [H]
        moe_sum = over("moe_sum", [P, 2, D], b)
        y_sb = over("y_sb", [P, D], b)
        e_gate = over("e_gate", [P, 2, GU], b)
        e_tok = over("e_tok", [P, 2, GU], b)
        pick_slot = over("pick_slot", [P, 2, P], b)
        final_gain = over("final_gain", [P, D], b)
        squares = over("squares", [P, D], b)
        assert b[0] <= PJ
        b = [FREE + 2 * D * 4]
        router = over("router", [P, KD, EXPERTS], b)
        ones_sq = over("ones_sq", [P, P], b)
        items = over("items", [P, 2 * EXPERTS + 2, 4], b)
        cur = over("cur", [P, 4], b)
        route = over("route", [P, 12, 2, EXPERTS], b)
        route1 = over("route1", [P, 12, 2], b)
        passes = nc.alloc_sbuf_tensor_at("passes", [P, 1], mybir.dt.int32, offset=b[0])

        def c_(name):
            o, w = at[name]
            return const[:, o:o + w]

        ident = c_("ident")
        pick, pick_rows = c_("pick"), c_("pick_rows").rearrange("p (j n) -> p j n", j=2)
        acc = [ctx.enter_context(nc.psum_tensor(f"acc{i}", [P, 512], F32)) for i in range(4)]
        tmp = [ctx.enter_context(nc.psum_tensor(f"tmp{i}", [P, 512], F32)) for i in range(4)]

        slabs, slab_at = [], {}

        last_slab = {}

        def slab(key, nk, w, parts):
            slab_at[key] = len(slabs)
            slabs.append((key, nk, w, parts))

        def rows_of(wt, k0, nk, c0, c1):
            return wt[k0 * P:(k0 + nk) * P, c0:c1].rearrange("(k p) n -> p k n", p=P)

        def two_halves(key, wt, k0, nk, c0, c1):
            w = c1 - c0
            h = nk // 2
            slab(key, nk, w, [(0, h, w, 0, w, rows_of(wt, k0, h, c0, c1)), (h, nk, w, 0, w, rows_of(wt, k0 + h, nk - h, c0, c1))])

        for l in range(DEPTH):
            for n in range(12):
                for kh in range(2):
                    two_halves(("mod", l, n, kh), dram["w_mod"][l], 4 * kh, 4, n * 512, (n + 1) * 512)
            for c, (c0, c1) in enumerate(IN_CHUNKS):
                for kh in range(2):
                    two_halves(("in", l, c, kh), dram["w_in"][l], 4 * kh, 4, c0, c1)
            for n in range(2):
                for kh in range(2):
                    two_halves(("out", l, n, kh), dram["w_out"][l], 4 * kh, 4, n * 512, (n + 1) * 512)
            if l % 2 == 0:
                for g, (j0, j1) in enumerate(FF_GROUPS):
                    for j in range(j0, j1):
                        for kh in range(2):
                            parts = [(0, 4, 512, o, o + GU, rows_of(dram[f"ffn_w_{nm}"][0], 4 * kh, 4, j * GU, (j + 1) * GU))
                                     for nm, o in (("gate", 0), ("up", GU))]
                            slab(("gu", l, j, kh), 4, 512, parts)
                    nk = 2 * (j1 - j0)
                    for n in range(2):
                        for s in range(0, nk, 4):
                            two_halves(("down", l, g, n, s), dram["ffn_w_down"][0], 2 * j0 + s, min(4, nk - s), n * 512, (n + 1) * 512)

        for i, (key, *_) in enumerate(slabs):
            if key[0] != "mod" and (i + 1 == len(slabs) or slabs[i + 1][0][:-1] != key[:-1]):
                last_slab[i] = key[:-1]

        def view(t, i, nk, w):
            return t[:, i % RING, 0:nk * w].rearrange("p (k n) -> p k n", k=nk)

        loaded = [sig(f"slab_loaded{i}") for i in range(RING)]
        hi_split, lo_split, slab_used = sig("hi_split"), sig("lo_split"), sig("slab_used")

        def used(i):
            return sig("acc_ready").at((last_slab[i], TILES - 1)) if i in last_slab else slab_used.at(i)

        class Splitter:

            def __init__(self, eng, part):
                self.eng, self.part, self.n = eng, part, 0

            def up_to(self, last):
                while self.n < min(last + 1, len(slabs)):
                    i = self.n
                    _, nk, w, _ = slabs[i]
                    src = raw[:, i % RING, 0:nk * w]
                    hi, lo = w_hi[:, i % RING, 0:nk * w], w_lo[:, i % RING, 0:nk * w]
                    if i >= RING:
                        self.eng.wait_ge(*used(i - RING))
                    if self.part == "hi":
                        self.eng.wait_ge(*loaded[i % RING].at(i))
                        nc.scalar.activation(hi, src, ACT.Copy).then_inc(*hi_split.did(i))
                    else:
                        self.eng.wait_ge(*hi_split.at(i))
                        nc.vector.tensor_tensor(lo, src, hi.bitcast(F32), ALU.subtract).then_inc(*lo_split.did(i))
                    self.n += 1

        def active(l):
            return list(range(TILES)) if l < DEPTH - 1 else [2, 3]

        def in_cols(l, c, t):
            if t in active(l):
                return IN_CHUNKS[c]
            return CTX_KEYS_ONLY.get(c, IN_CHUNKS[c])

        consts_in, x_in = sig("consts_loaded"), sig("x_loaded")
        vec_in, row_in = sig("vecs_loaded"), sig("rows_loaded")
        bias_in, mlaw_in = sig("bias_loaded"), sig("mla_weights_loaded")
        stored = sig("stored")
        phase = sig("phase_ended")
        ENGINES = 3
        marks = {}

        def phase_end(eng, who, n):
            eng.sem_inc(phase.sem, 1)
            marks[who] = marks.get(who, 0) + 1
            eng.wait_ge(phase.sem, ENGINES * marks[who])

        UP_SLABS, DOWN_SLABS = 2 * FF_CHUNKS, FF_CHUNKS
        E_SLABS = UP_SLABS + DOWN_SLABS
        assert E_SLABS % RING == 0
        base_slot = len(slabs) % RING
        e_slot = lambda q: (base_slot + q) % RING
        HALF = SLAB // 2
        e_loaded = [[sig(f"expert_half{h}_loaded{i}") for h in range(2)] for i in range(RING)]

        def e_loaded_at(q, half, item):
            return e_loaded[e_slot(q)][half].sem, 16 * ((item - 1) * (E_SLABS // RING) + q // RING + 1)

        def e_half(t, q, half):
            return t[:, e_slot(q), half * HALF:(half + 1) * HALF]

        def e_moving(t, q, kk, n0):
            if q < UP_SLABS:
                return t[:, e_slot(q), :].rearrange("p (u k n) -> p u k n", u=2, k=4)[:, :, kk, :]
            return t[:, e_slot(q), kk * D + n0:kk * D + n0 + 512]

        gather_banks = [tmp[2], tmp[3], acc[0], acc[1]]
        scatter_banks = [tmp[2], tmp[3], tmp[1], tmp[2]]

        def experts_loop(eng, body):
            eng.wait_ge(*sig("passes_known").at())
            n = eng.value_load(passes[0:1, 0:1], min_val=1, max_val=2)
            with eng.Fori(0, n) as half:
                with eng.Fori(0, EXPERTS) as e:
                    body(half * EXPERTS + e + 1, e)
            return n * EXPERTS + 1

        def consts_in_at():
            return consts_in.sem, 16

        def level_list():
            return [0] + LEVELS + [128, 256]

        def level_steps():
            return [(p, n, m) for p in range(2) for n, m in enumerate(level_list())]

        def level_banks(l, m):
            return [1] if l == DEPTH - 1 and 0 < m <= P else [0, 1]

        def level_bank(i, b):
            return tmp[(2 * i + b) % 4]

        def level_read(l, i, b):
            return sig("s_read_act" if level_steps()[i][2] >= P else "s_read").at((l, i, b))

        def units(l):
            return [("da", t, h) for t in active(l) for h in range(DA_HEADS)] + \
                   [("mla", t, h) for t in active(l) for h in range(MLA_HEADS)]

        block = ctx.enter_context(nc.Block())

        def expert_loads(sp):
            sp.wait_ge(phase.sem, ENGINES * known.get("phases", {}).get("norm1", 1))
            sp.dma_start(router[:, :, :], dram["moe_router"][0].rearrange("(k p) e -> p k e", p=P)).then_inc(sig("router_loaded").sem, 16)
            sp.wait_ge(phase.sem, ENGINES * known.get("phases", {}).get("route", 1))
            sp.dma_start(final_gain[:, :], dram["norm_final"]).then_inc(sig("final_gain_loaded").sem, 16)

            def body(item, e):
                for q in range(E_SLABS):
                    back, turn = (q - RING, item) if q >= RING else (q - RING + E_SLABS, item - 1)
                    for half, name in enumerate(("gate", "up")):
                        sp.wait_ge(*sig("e_lo").turn((back, half), turn))
                        if q < UP_SLABS:
                            j, kh = divmod(q, 2)
                            src = dram[f"moe_w_{name}"][0][e][kh * 512:(kh + 1) * 512, j * GU:(j + 1) * GU].rearrange("(k p) n -> p k n", p=P)
                            dst = e_half(raw, q, half).rearrange("p (k n) -> p k n", k=4)
                        else:
                            k0 = 2 * (q - UP_SLABS) + half
                            src, dst = dram["moe_w_down"][0][e][k0 * P:(k0 + 1) * P, :], e_half(raw, q, half)
                        sp.dma_start(dst, src).then_inc(e_loaded[e_slot(q)][half].sem, 16)

            experts_loop(sp, body)
            for t in range(2):
                sp.wait_ge(*sig("final_x").at(t))
                sp.dma_start(out[0, t * P:(t + 1) * P, :], x[:, 2 + t, :]).then_inc(stored.sem, 16)
            sp.wait_ge(stored.sem, 32)

        def loads(sp):
            def slab_loads(first, last):
                for i in range(first, last):
                    _, nk, w, parts = slabs[i]
                    if i >= RING:
                        sp.wait_ge(*hi_split.at(i - RING))
                        sp.wait_ge(*lo_split.at(i - RING))
                    dst = view(raw, i, nk, w)
                    for n, (ka, kb, _, ca, cb, src) in enumerate(parts):
                        sp.dma_start(dst[:, ka:kb, ca:cb], src).then_inc(loaded[i % RING].sem, 16)
                    loaded[i % RING].count += 31
                    loaded[i % RING].did(i)

            sp.dma_start(cond_in[:, :], dram["cond"]).then_inc(vec_in.sem, 16)
            sp.dma_start(vecs[:, :, :], dram["vecs"]).then_inc(vec_in.sem, 16)
            sp.dma_start(const[:, :], dram["consts"]).then_inc(consts_in.sem, 16)
            slab_loads(0, RING)
            done = RING
            for l in range(DEPTH):
                if l:
                    done_to = slab_at[("mod", l, 0, 0)] + RING
                    slab_loads(done, done_to)
                    done = done_to
                    sp.wait_ge(phase.sem, ENGINES * known.get("phases", {}).get(("layer", l), 1))
                sp.dma_start(rows[:, :], dram["rows"][:, l, :]).then_inc(row_in.sem, 16)
                bm = dram["b_mod"][l].rearrange("(a q) -> a q", a=1)
                for i, part in enumerate((0, 1, 3, 4)):
                    sp.dma_start(mod_rows[4:5, i, :], bm[:, part * D:(part + 1) * D]).then_inc(bias_in.sem, 16)
                for i, part in enumerate((2, 5)):
                    sp.dma_start(gate_rows[4:5, i, :], bm[:, part * D:(part + 1) * D]).then_inc(bias_in.sem, 16)
                if l == 0:
                    for t in range(TILES):
                        src = dram["ctx"][0] if t < 2 else dram["x"][0]
                        sp.dma_start(x[:, t, :], src[(t % 2) * P:(t % 2 + 1) * P, :]).then_inc(x_in.sem, 16)
                end = slab_at[("out", l, 0, 0)] + RING
                slab_loads(done, end)
                done = end
                sp.wait_ge(phase.sem, ENGINES * known.get("phases", {}).get(("mla", l), 1))
                sp.dma_start(w_uq[:, :, :], dram["mla_w_uq"][l].rearrange("(k p) n -> p k n", p=P)).then_inc(mlaw_in.sem, 16)
                sp.dma_start(w_ukv[:, :], dram["mla_w_ukv"][l]).then_inc(mlaw_in.sem, 16)
                end = slab_at[("mod", l + 1, 0, 0)] if l + 1 < DEPTH else len(slabs)
                if l + 1 < DEPTH:
                    slab_loads(done, end)
                    done = end
                else:
                    slab_loads(done, end)
                    expert_loads(sp)

        @block.sync
        def _(sp):
            loads(sp)

        def experts_pe(pe):
            for r in range(8):
                part, t, half = (hT_hi, hT_lo)[r // 4], 2 + r // 2 % 2, r % 2
                if r >= 4:
                    pe.wait_ge(*sig("h_tok_read").at(r - 4))
                for k in range(4):
                    mm = nc.tensor.transpose(tmp[r % 4][:, k * P:(k + 1) * P], part[:, 4 * half + k, t * P:(t + 1) * P].bitcast(F32), ident)
                mm.then_inc(*sig("h_tok_ps").did(r))
            pe.wait_ge(sig("router_loaded").sem, 16)
            for t in range(2):
                for k in range(KD):
                    for part in (hT_hi, hT_lo):
                        mm = nc.tensor.matmul(acc[0][:, t * EXPERTS:(t + 1) * EXPERTS], part[:, k, (2 + t) * P:(3 + t) * P].bitcast(F32),
                                              router[:, k, :], start=(k == 0 and part is hT_hi), stop=(k == KD - 1 and part is hT_lo))
            mm.then_inc(*sig("logits").did())
            pe.wait_ge(*sig("chosen").at())
            m = route[:, 0]
            nc.tensor.matmul(acc[1][:, 0:EXPERTS], c_("earlier"), m[:, 0, :], start=True, stop=True)
            nc.tensor.matmul(acc[1][:, EXPERTS:2 * EXPERTS], c_("earlier"), m[:, 1, :], start=True, stop=False)
            nc.tensor.matmul(acc[1][:, EXPERTS:2 * EXPERTS], ones_sq[:, :], m[:, 0, :], start=False, stop=True)
            nc.tensor.matmul(acc[1][:, 2 * EXPERTS:3 * EXPERTS], ones_sq[:, :], m[:, 0, :], start=True, stop=False)
            nc.tensor.matmul(acc[1][:, 2 * EXPERTS:3 * EXPERTS], ones_sq[:, :], m[:, 1, :], start=False, stop=True).then_inc(*sig("ranks").did())
            pe.wait_ge(*sig("h_tok_read").at(7))
            pe.wait_ge(*sig("passes_known").at())
            phase_end(pe, "pe", "route")

            def gather(pick_at, signal):
                pe.wait_ge(*pick_at)
                for r in range(4):
                    for c in range(2):
                        k = 2 * r + c
                        for i, part in enumerate((h_tok_hi, h_tok_lo)):
                            for t in range(2):
                                o = (2 * i + c) * P
                                mm = nc.tensor.matmul(gather_banks[r][:, o:o + P], part[:, t, k * P:(k + 1) * P], pick_tok[:, t, :],
                                                      start=(t == 0), stop=(t == 1))
                    mm.then_inc(*signal.did(r))

            def scatter(item, last):
                pe.wait_ge(*(sig("y_last").at() if last else sig("e_y").turn(1, item)))
                pe.wait_ge(*sig("e_slot_pick").turn(0, item - 1))
                pe.wait_ge(*sig("e_add").turn(3, item - 1))
                for r in range(4):
                    t, n = divmod(r, 2)
                    if r == 3:
                        pe.wait_ge(*(sig("add_last").at(0) if last else sig("e_add").turn(0, item)))
                    nc.tensor.matmul(scatter_banks[r][:, :], pick_slot[:, t, :], y_sb[:, n * 512:(n + 1) * 512], start=True, stop=True)\
                        .then_inc(*(sig("scatter_last") if last else sig("e_scatter")).did(r))

            def hidden_transposes(j, item):
                pe.wait_ge(*sig("e_act").turn(j, item))
                if j >= 2:
                    pe.wait_ge(*sig("e_rest").turn(j - 2, item))
                elif j == 1:
                    pe.wait_ge(*sig("e_add").turn(3, item))
                else:
                    pe.wait_ge(*sig("e_slot_pick").turn(0, item))
                for c in range(2):
                    mm = nc.tensor.transpose(tmp[j % 2][:, c * P:(c + 1) * P], e_tok[:, j % 2, c * P:(c + 1) * P], ident)
                mm.then_inc(*sig("e_hT_ps").did(j))

            def products(q, bank, st_hi, st_lo, k0, nk, n0, first, last):
                for kk in range(nk):
                    for st, wt in ((st_hi, w_hi), (st_hi, w_lo), (st_lo, w_hi)):
                        mm = nc.tensor.matmul(bank[:, :], st[:, k0 + kk, :], e_moving(wt, q, kk, n0),
                                              start=(first and kk == 0 and wt is w_hi and st is st_hi), stop=(last and kk == nk - 1 and st is st_lo))
                return mm

            for name in ("e_used", "e_scatter", "e_hT_ps", "e_slot_ps"):
                pe.sem_inc(sig(name).sem, sig(name).each())
            gather(sig("e_pick").turn(0, 0), Prologue(sig("e_gathered")))

            def body(item, e):
                for j in range(FF_CHUNKS):
                    for kh in range(2):
                        q = 2 * j + kh
                        pe.wait_ge(*sig("e_lo").turn((q, 1), item))
                        if q == 0:
                            pe.wait_ge(*sig("e_hg_lo").turn(3, item - 1))
                        if kh == 0 and j >= 2:
                            pe.wait_ge(*sig("e_act").turn(j - 2, item))
                        products(q, acc[j % 2], hg_hi, hg_lo, 4 * kh, 4, 0, kh == 0, kh == 1).then_inc(*sig("e_used").did(q))
                    if j == 0:
                        scatter(item, False)
                        pe.wait_ge(*sig("e_rest").turn(FF_CHUNKS - 1, item - 1))
                        for t in range(2):
                            mm = nc.tensor.transpose(tmp[0][:, t * P:(t + 1) * P], pick_tok[:, t, :].bitcast(F32), ident)
                        mm.then_inc(*sig("e_slot_ps").did(0))
                    else:
                        hidden_transposes(j - 1, item)
                for d in range(DOWN_SLABS):
                    q = UP_SLABS + d
                    pe.wait_ge(*sig("e_lo").turn((q, 1), item))
                    if d == 0:
                        pe.wait_ge(*sig("e_y").turn(1, item))
                    pe.wait_ge(*sig("e_rest").turn(d, item))
                    for n in range(2):
                        mm = products(q, acc[2 + n], eT_hi, eT_lo, 2 * d, 2, n * 512, d == 0, d == DOWN_SLABS - 1)
                    mm.then_inc(*sig("e_used").did(q))
                    if d == 0:
                        hidden_transposes(FF_CHUNKS - 1, item)
                    if d == 3:
                        gather(sig("e_pick").turn(0, item), sig("e_gathered"))

            end = experts_loop(pe, body)
            scatter(end, True)

        @block.tensor
        def _(pe):
            bank_free = {}

            def project(key, slab_keys, k_firsts, stat_hi, stat_lo, tiles, cols_of, free_signal):
                for s, sk in enumerate(slab_keys):
                    i = slab_at[sk]
                    _, nk, w, _ = slabs[i]
                    hi, lo = view(w_hi, i, nk, w), view(w_lo, i, nk, w)
                    pe.wait_ge(*lo_split.at(i))
                    last_s = s == len(slab_keys) - 1
                    mm = None
                    for t in tiles:
                        a, bb = cols_of(t)
                        if s == 0 and t in bank_free:
                            pe.wait_ge(*bank_free[t])
                        for kk in range(nk):
                            k = k_firsts[s] + kk
                            for st, wt in ((stat_hi, hi), (stat_hi, lo), (stat_lo, hi)):
                                mm = nc.tensor.matmul(acc[t][:, 0:bb - a], st[:, k, t * P:(t + 1) * P], wt[:, kk, a:bb],
                                                      start=(s == 0 and kk == 0 and st is stat_hi and wt is hi),
                                                      stop=(last_s and kk == nk - 1 and st is stat_lo))
                        if last_s:
                            mm.then_inc(*sig("acc_ready").did((key, t)))
                            bank_free[t] = free_signal(t)
                    if not last_s:
                        mm.then_inc(*slab_used.did(i))

            def transpose_into(dst, src):
                return nc.tensor.transpose(dst, src, ident[0:src.shape[0], 0:src.shape[0]])

            pe.wait_ge(*consts_in_at())
            for l in range(DEPTH):
                act_t = active(l)
                pe.wait_ge(*sig("cond_ready").at(l))
                for n in range(12):
                    bank = acc[n % 4]
                    if n >= 4:
                        pe.wait_ge(*sig("mod_row").at((l, n - 4)))
                    for kh in range(2):
                        i = slab_at[("mod", l, n, kh)]
                        hi, lo = view(w_hi, i, 4, 512), view(w_lo, i, 4, 512)
                        pe.wait_ge(*lo_split.at(i))
                        for kk in range(4):
                            for wt in (hi, lo):
                                mm = nc.tensor.matmul(bank[:, :], cond4[:, 4 * kh + kk, :], wt[:, kk, :],
                                                      start=(kh == 0 and kk == 0 and wt is hi),
                                                      stop=(kh == 1 and kk == 3 and wt is lo))
                        mm.then_inc(*slab_used.did(i))
                pe.wait_ge(*sig("mod_row").at((l, 11)))
                pe.wait_ge(bias_in.sem, 96 * (l + 1))
                for i in range(4):
                    for k in range(KD):
                        o = (i * KD + k) * 2
                        mm = nc.tensor.matmul(tmp[0][:, o:o + 2], mod_rows[0:5, i, k * P:(k + 1) * P], pick[0:5, :],
                                              start=True, stop=True)
                mm.then_inc(*sig("mod_cols").did(l))
                pe.wait_ge(*sig("cols_read").at(l))
                phase_end(pe, "pe", "mod")

                def norm_transposes(which, tiles):
                    for k in range(KD):
                        if k == 0:
                            pe.wait_ge(*sig("xn_ready").at((l, which)))
                        if k >= 4:
                            pe.wait_ge(*sig("modulated").at((l, which, k - 4)))
                        for t in tiles:
                            mm = transpose_into(tmp[k % 4][:, t * P:(t + 1) * P], xn[:, t, k * P:(k + 1) * P])
                        mm.then_inc(*sig("xT").did((l, which, k)))

                norm_transposes(0, range(TILES))
                pe.wait_ge(*sig("h_lo").at((l, 0, KD - 1)))
                phase_end(pe, "pe", "norm0")
                bank_free.clear()
                for c in range(len(IN_CHUNKS)):
                    tiles = [t for t in range(TILES) if in_cols(l, c, t)]
                    c0 = IN_CHUNKS[c][0]

                    def cols_of(t, c=c, c0=c0):
                        a, bb = in_cols(l, c, t)
                        return a - c0, bb - c0
                    project(("in", l, c), [("in", l, c, kh) for kh in range(2)], [0, 4], hT_hi, hT_lo, tiles, cols_of,
                            lambda t, c=c: sig("in_read_act" if t < 2 else "in_read_dve").at((l, c, t)))
                pe.wait_ge(*sig("in_read_act").at(("all", l)))
                pe.wait_ge(*sig("in_read_dve").at(("all", l)))
                phase_end(pe, "pe", "in")

                for h in range(DA_HEADS):
                    if h == 0:
                        pe.wait_ge(*sig("roped").at((l, "da")))
                    else:
                        pe.wait_ge(*sig("daT_read_act").at((l, h - 1)))
                    for t in act_t:
                        mm = transpose_into(tmp[0][:, t * P:(t + 1) * P], pj[:, t, C_DQ + h * P:C_DQ + (h + 1) * P])
                    mm.then_inc(*sig("daqT_ps").did((l, h)))
                    if h:
                        pe.wait_ge(*sig("daT_read_dve").at((l, h - 1)))
                    for t in range(TILES):
                        mm = transpose_into(tmp[1][:, t * P:(t + 1) * P], pj[:, t, C_DK + h * P:C_DK + (h + 1) * P])
                    mm.then_inc(*sig("dakT_ps").did((l, h)))
                for n, t in enumerate(range(TILES)):
                    q = t in act_t
                    pe.wait_ge(*sig("c_tok").at((l, t)))
                    for i in range(0 if q else 2, 3):
                        mm = transpose_into(tmp[2][:, i * P:(i + 1) * P], c_tok[:, t % 2, i * P:(i + 1) * P])
                    mm.then_inc(*sig("cT_ps").did((l, t)))
                    pe.wait_ge(*sig("cT").at((l, t)))
                    pe.wait_ge(mlaw_in.sem, 32 * (l + 1))
                    if q:
                        if t - 1 in act_t:
                            pe.wait_ge(*sig("q_tok").at((l, t - 1)))
                        for i in range(2):
                            mm = nc.tensor.matmul(acc[0][:, 0:MLA_HEADS * MLA_QK], cT[:, i, :], w_uq[:, i, :],
                                                  start=(i == 0), stop=(i == 1))
                        mm.then_inc(*sig("mq_ps").did((l, t)))
                    if n:
                        pe.wait_ge(*sig("kv_tok").at((l, t - 1)))
                    nc.tensor.matmul(acc[1][:, :], cT[:, 2, :], w_ukv[:, :], start=True, stop=True).then_inc(*sig("mkv_ps").did((l, t)))
                    if q:
                        pe.wait_ge(*sig("mq_roped" if t >= 2 else "q_tok").at((l, t)))
                        if t - 1 in act_t:
                            pe.wait_ge(*sig("mqT_read").at((l, t - 1)))
                        for h in range(MLA_HEADS):
                            mm = transpose_into(acc[2][0:MLA_QK, h * P:(h + 1) * P], q_tok[:, t % 2, h, :])
                        mm.then_inc(*sig("mqT_ps").did((l, t)))
                    pe.wait_ge(*sig("mk_roped").at((l, t)))
                    if t:
                        pe.wait_ge(*sig("mkT_read").at((l, t - 1)))
                    for h in range(MLA_HEADS):
                        mm = transpose_into(acc[3][0:MLA_QK, h * P:(h + 1) * P], k_tok[:, t % 2, h, :])
                    mm.then_inc(*sig("mkT_ps").did((l, t)))
                pe.wait_ge(*sig("mkT_read").at((l, TILES - 1)))
                pe.wait_ge(*sig("daT_read_act").at((l, DA_HEADS - 1)))
                pe.wait_ge(*sig("daT_read_dve").at((l, DA_HEADS - 1)))
                phase_end(pe, "pe", "attn_prep")

                us = units(l)

                def scores(u):
                    kind, t, h = us[u]
                    keys = TOK if t >= 2 else CTX
                    if u >= 2:
                        pe.wait_ge(*sig("exp").at((l, u - 2)))
                    for g in range(2 if kind == "da" else 1):
                        bank = tmp[2 * (u % 2) + g]
                        if kind == "da":
                            mm = nc.tensor.matmul(bank[:, 0:keys], daqT[64 * g:64 * g + 64, h, t * P:(t + 1) * P],
                                                  dakT[64 * g:64 * g + 64, h, 0:keys], start=True, stop=True)
                        else:
                            mm = nc.tensor.matmul(bank[:, 0:keys], mqT[:, h, t * P:(t + 1) * P], mkT[:, h, 0:keys],
                                                  start=True, stop=True)
                    mm.then_inc(*sig("scores").did((l, u)))

                def probs_transposes(u):
                    kind, t, h = us[u]
                    nk = (TOK if t >= 2 else CTX) // P
                    pe.wait_ge(*sig("probs" if kind == "da" else "exp").at((l, u)))
                    if u >= 2:
                        pe.wait_ge(*sig("probsT").at((l, u - 2)))
                    for s in range(nk):
                        mm = transpose_into(acc[u % 2][:, s * P:(s + 1) * P], probs[:, u % 2, 0, s * P:(s + 1) * P])
                    mm.then_inc(*sig("probsT_ps").did((l, u)))

                def values(u):
                    kind, t, h = us[u]
                    nk = (TOK if t >= 2 else CTX) // P
                    pe.wait_ge(*sig("probsT").at((l, u)))
                    if u >= 2:
                        pe.wait_ge(*sig("attended").at((l, u - 2)))
                    for s in range(nk):
                        v = pj[:, s, C_DV + h * P:C_DV + (h + 1) * P] if kind == "da" else pj[:, s, C_CQ + h * MLA_V:C_CQ + (h + 1) * MLA_V]
                        mm = nc.tensor.matmul(acc[2 + u % 2][:, 0:v.shape[1]], probsT[:, u % 2, s, :], v,
                                              start=(s == 0), stop=(s == nk - 1))
                    mm.then_inc(*sig("o_ps").did((l, u)))

                for u in range(len(us) + 2):
                    if u < len(us):
                        scores(u)
                    if u >= 2:
                        values(u - 2)
                    if 1 <= u <= len(us):
                        probs_transposes(u - 1)
                pe.wait_ge(*sig("attended").at((l, len(us) - 1)))
                phase_end(pe, "pe", "attn")

                for i in range(6):
                    if i >= 4:
                        pe.wait_ge(*sig("gate_sig").at((l, i - 4)))
                    for t in (range(TILES) if i < 4 else act_t):
                        col = (C_FF + i * P) if i < 4 else (C_HQ + (i - 4) * P)
                        mm = transpose_into(tmp[i % 4][:, t * P:(t + 1) * P], pj[:, t, col:col + P])
                    mm.then_inc(*sig("gT_ps").did((l, i)))
                for p in range(2):
                    for n, m in enumerate(level_list()):
                        i = p * len(level_list()) + n
                        buf = n % 2
                        pe.wait_ge(*sig("level").at((l, p, n)))
                        if i == 0:
                            pe.wait_ge(*sig("gate_sig").at((l, 5)))
                        for b in level_banks(l, m):
                            bank = level_bank(i, b)
                            before = [i - k for k in range(2, i + 1, 2) if b in level_banks(l, level_steps()[i - k][2])]
                            if before:
                                pe.wait_ge(*level_read(l, before[0], b))
                            if m == 0:
                                r = slice(64 * b, 64 * b + 64)
                                for t in act_t:
                                    mm = nc.tensor.matmul(bank[:, t * P:(t + 1) * P], lev_k[r, buf, 0, t * P:(t + 1) * P],
                                                          hqT[r, p, t * P:(t + 1) * P], start=True, stop=True)
                            elif m <= 64:
                                for tt_ in range(2):
                                    t = 2 * b + tt_
                                    o = bank[:, tt_ * 2 * P:(tt_ + 1) * 2 * P].rearrange("s (h b e m) -> s h b e m", h=2, e=2, m=m)
                                    q0 = (t - act_t[0]) * 64
                                    for d in range(2):
                                        q = lev_q[:, buf, d, :, q0:q0 + 64].rearrange("d h (b m) -> d h b m", m=m)
                                        mm = nc.tensor.matmul(o[:, :, :, 1 - d, :], lev_k[:, buf, d, t * P:(t + 1) * P], q,
                                                              start=True, stop=True)
                            elif m == 128:
                                q0 = (b - act_t[0] // 2) * P
                                for d in range(2):
                                    s0 = (2 * b + d) * P
                                    mm = nc.tensor.matmul(bank[:, d * SEQ:(d + 1) * SEQ], lev_k[:, buf, d, s0:s0 + P],
                                                          lev_q[:, buf, d, :, q0:q0 + P], start=True, stop=True)
                            else:
                                for d in range(2):
                                    mm = nc.tensor.matmul(bank[:, :], lev_k[:, buf, d, b * P:(b + 1) * P],
                                                          lev_q[:, buf, d, :, :], start=(d == 0), stop=(d == 1))
                            mm.then_inc(*sig("s_ps").did((l, i, b)))
                    pe.wait_ge(*sig("s_read_act").at((l, p)))
                    pe.wait_ge(*sig("s_read").at((l, len(level_list()) * p + level_list().index(64), 1)))
                    for t in act_t:
                        for hh in range(2):
                            h = 2 * p + hh
                            sg, a = t // 2, t % 2
                            terms = [(t, s_diag[:, hh, t, :]), (2 * sg + 1 - a, s_off[:, hh, sg, 1 - a, :])]
                            if sg:
                                terms += [(s, s_far[:, hh, s, a * P:(a + 1) * P]) for s in range(2)]
                            for q, (s, st) in enumerate(terms):
                                mm = nc.tensor.matmul(acc[t][:, h * 64:(h + 1) * 64], st, pj[:, s, C_HI + h * 64:C_HI + (h + 1) * 64],
                                                      start=(q == 0), stop=(q == len(terms) - 1))
                    mm.then_inc(*sig("hg_o").did((l, p)))
                pe.wait_ge(*sig("mixed").at((l, 3)))
                phase_end(pe, "pe", "hg")

                for k in range(KD):
                    if k >= 4:
                        pe.wait_ge(*sig("oT_lo").at((l, k - 4)))
                    for t in act_t:
                        mm = transpose_into(tmp[k % 4][:, t * P:(t + 1) * P], pj[:, t, k * P:(k + 1) * P])
                    mm.then_inc(*sig("oT_ps").did((l, k)))
                pe.wait_ge(*sig("oT_lo").at((l, KD - 1)))

                def gates(i):
                    for j in range(2):
                        for n in range(2):
                            if j or n:
                                pe.wait_ge(*sig("gate_all").at((l, i, (2 * j + n) - 1)))
                            nc.tensor.matmul(tmp[2][:, :], pick_rows[0:5, j, :], gate_rows[0:5, i, n * 512:(n + 1) * 512],
                                             start=True, stop=True).then_inc(*sig("gate_ps").did((l, i, 2 * j + n)))

                gates(0)
                bank_free.clear()
                for n in range(2):
                    project(("out", l, n), [("out", l, n, kh) for kh in range(2)], [0, 4], hT_hi, hT_lo, act_t,
                            lambda t: (0, 512), lambda t, n=n: sig("acc_added").at((l, "out", n, t)))
                pe.wait_ge(*sig("acc_added").at((l, "out", 1, 3)))
                phase_end(pe, "pe", "out")
                norm_transposes(1, act_t)
                pe.wait_ge(*sig("h_lo").at((l, 1, KD - 1)))
                gates(1)
                pe.wait_ge(*sig("gate_all").at((l, 1, 3)))
                phase_end(pe, "pe", "norm1")
                if l % 2 == 0:
                    bank_free.clear()

                    def hidden_transposes(g, j):
                        j0 = FF_GROUPS[g][0]
                        pe.wait_ge(*sig("act_tok").at((l, j, TILES - 1)))
                        for c in range(2):
                            bank = tmp[(2 * j + c) % 3]
                            if 2 * j + c >= 3:
                                pe.wait_ge(*sig("aT_lo").at((l, 2 * j + c - 3)))
                            for t in range(TILES):
                                mm = transpose_into(bank[:, t * P:(t + 1) * P], act_tok[:, t, c * P:(c + 1) * P])
                            mm.then_inc(*sig("aT_ps").did((l, 2 * j + c)))

                    for g, (j0, j1) in enumerate(FF_GROUPS):
                        for j in range(j0, j1):
                            project(("gu", l, j), [("gu", l, j, kh) for kh in range(2)], [0, 4], hT_hi, hT_lo, range(TILES),
                                    lambda t: (0, 512), lambda t, j=j: sig("act_tok").at((l, j, t)))
                            hidden_transposes(g, j)
                        pe.wait_ge(*sig("aT_lo").at((l, 2 * j1 - 1)))
                        nk = 2 * (j1 - j0)
                        for n in range(2):
                            ss = list(range(0, nk, 4))
                            project(("down", l, g, n), [("down", l, g, n, s) for s in ss], ss, aT_hi, aT_lo, range(TILES),
                                    lambda t: (0, 512), lambda t, g=g, n=n: sig("acc_added").at((l, "down", g, n, t)))
                    pe.wait_ge(*sig("acc_added").at((l, "down", len(FF_GROUPS) - 1, 1, TILES - 1)))
                    phase_end(pe, "pe", "ffn")
                else:
                    experts_pe(pe)

        @block.gpsimd
        def _(pool):
            def sub(o, a, b):
                return nc.gpsimd.tensor_tensor(o, a, b, ALU.subtract)

            for l in range(DEPTH):
                S0 = active(l)[0] * P
                T = TOK - S0
                pool.wait_ge(phase.sem, ENGINES * known.get("phases", {}).get(("attn", l), 1))
                nc.gpsimd.memset(lev_q[:, 0], 0.0)
                nc.gpsimd.memset(lev_q[:, 1], 0.0)
                nc.gpsimd.memset(lev_k[:, :, :, :], 0.0).then_inc(*sig("lev_clear").did(l))
                pool.wait_ge(*sig("cum").at((l, 3)))
                for i, (p, n, m) in enumerate(level_steps()):
                    if m == 0:
                        continue
                    if i >= 2:
                        pool.wait_ge(*sig("level").at((l, *level_steps()[i - 2][:2])))
                    d = dec[:, i % 2]
                    if m <= 128:
                        cf, cb = [cum[:, g, S0:].rearrange("p (b e m) -> p b e m", e=2, m=m) for g in (p, 2 + p)]
                        nb = T // (2 * m)
                        rf = cf[:, :, 0, m - 1:m].broadcast_to([P, nb, m])
                        rb = cb[:, :, 1, 0:1].broadcast_to([P, nb, m])
                        dv = [d[:, q, 0:T // 2].rearrange("p (b m) -> p b m", m=m) for q in range(4)]
                        sub(dv[0], cf[:, :, 1], rf)
                        sub(dv[1], rf, cf[:, :, 0])
                        sub(dv[2], cb[:, :, 0], rb)
                        ins = sub(dv[3], rb, cb[:, :, 1])
                    else:
                        cf, cb = cum[:, p, :], cum[:, 2 + p, :]
                        nc.gpsimd.tensor_copy(d[:, 0, :], cf[:, CTX:])
                        sub(d[:, 1, :], cf[:, CTX - 1:CTX].broadcast_to([P, CTX]), cf[:, 0:CTX])
                        nc.gpsimd.tensor_copy(d[:, 2, :], cb[:, CTX:])
                        ins = sub(d[:, 3, :], cb[:, 0:1].broadcast_to([P, CTX]), cb[:, 0:CTX])
                    ins.then_inc(*sig("dec").did((l, p, n)))

        def experts_act(act):
            act.wait_ge(*hi_split.at(len(slabs) - 1))
            act.sem_inc(sig("e_hi").sem, sig("e_hi").each())
            for r in range(4):
                act.wait_ge(*sig("h_tok_ps").at(r))
                nc.scalar.activation(h_tok_hi[:, r // 2, (r % 2) * 512:(r % 2 + 1) * 512], tmp[r][:, :], ACT.Copy).then_inc(*sig("h_tok_read").did(r))
            act.wait_ge(*sig("logit_gap").at())
            nc.scalar.activation(route1[:, 5], route1[:, 4], ACT.Exp).then_inc(*sig("gap_exp").did())
            act.wait_ge(*sig("passes_known").at())
            phase_end(act, "act", "route")
            for name in ("e_silu", "e_high", "e_y"):
                act.sem_inc(sig(name).sem, sig(name).each())
            act.wait_ge(*sig("y_cleared").at())
            act.sem_inc(sig("e_slot_pick").sem, 1)

            def gathered(at, signal):
                for r in range(4):
                    act.wait_ge(*at(r))
                    nc.scalar.activation(hg_hi[:, 2 * r:2 * r + 2, :], gather_banks[r][:, 0:2 * P].rearrange("p (c s) -> p c s", c=2), ACT.Copy).then_inc(*signal.did(r))

            gathered(lambda r: sig("e_gathered").turn(r, 0), Prologue(sig("e_hg_hi")))

            def body(item, e):
                n = [0]

                def high(to):
                    while n[0] <= to:
                        q = n[0]
                        back, turn = (q - RING, item) if q >= RING else (q - RING + E_SLABS, item - 1)
                        act.wait_ge(*sig("e_used").turn(back, turn))
                        for half in range(2):
                            act.wait_ge(*e_loaded_at(q, half, item))
                            nc.scalar.activation(e_half(w_hi, q, half), e_half(raw, q, half), ACT.Copy).then_inc(*sig("e_hi").did((q, half)))
                        n[0] += 1

                def hidden_high(j):
                    act.wait_ge(*sig("e_hT_ps").turn(j, item))
                    nc.scalar.activation(eT_hi[:, 2 * j:2 * j + 2, :], tmp[j % 2][:, 0:2 * P].rearrange("p (c s) -> p c s", c=2), ACT.Copy).then_inc(*sig("e_high").did(j))

                high(2)
                act.wait_ge(*sig("e_used").turn(E_SLABS - 1, item - 1))
                act.wait_ge(*sig("e_scatter").turn(3, item - 1))
                for h in range(2):
                    nc.scalar.activation(y_sb[:, h * 512:(h + 1) * 512], acc[2 + h][:, :], ACT.Copy).then_inc(*sig("e_y").did(h))
                for j in range(FF_CHUNKS):
                    high(2 * j + 3)
                    act.wait_ge(*sig("e_used").turn(2 * j + 1, item))
                    act.wait_ge(*(sig("e_act").turn(j - 2, item) if j >= 2 else sig("e_act").turn(j - 2 + FF_CHUNKS, item - 1)))
                    nc.scalar.activation(e_gate[:, j % 2, :], acc[j % 2][:, 0:GU], ACT.Silu).then_inc(*sig("e_silu").did(j))
                    if j:
                        hidden_high(j - 1)
                    else:
                        act.wait_ge(*sig("e_slot_ps").turn(0, item))
                        nc.scalar.activation(pick_slot[:, :, :], tmp[0][:, 0:2 * P].rearrange("p (t n) -> p t n", t=2), ACT.Copy).then_inc(*sig("e_slot_pick").did(0))
                high(UP_SLABS + 3)
                hidden_high(FF_CHUNKS - 1)
                high(UP_SLABS + 6)
                gathered(lambda r: sig("e_gathered").turn(r, item), sig("e_hg_hi"))
                high(E_SLABS - 1)

            end = experts_loop(act, body)
            act.wait_ge(*sig("e_used").turn(E_SLABS - 1, end - 1))
            act.wait_ge(*sig("e_scatter").turn(3, end - 1))
            for h in range(2):
                ins = nc.scalar.activation(y_sb[:, h * 512:(h + 1) * 512], acc[2 + h][:, :], ACT.Copy)
            ins.then_inc(*sig("y_last").did())
            for t in range(2):
                act.wait_ge(*sig("x_last").at(t))
                if t:
                    act.wait_ge(*sig("final_sq").at(0))
                nc.scalar.activation(squares[:, :], x[:, 2 + t, :], ACT.Square, accum_out=small[:, t:t + 1]).then_inc(*sig("final_sq").did(t))
            act.wait_ge(*sig("final_mean").at())
            nc.scalar.activation(small[:, 4:6], small[:, 2:4], ACT.Sqrt).then_inc(*sig("final_root").did())

        @block.scalar
        def _(act):
            split = Splitter(act, "hi")

            def norm(l, which, tiles):
                for t in tiles:
                    nc.scalar.activation(xn[:, t, :], x[:, t, :], ACT.Square, accum_out=small[:, t:t + 1]).then_inc(*sig("sq").did((l, which, t)))
                act.wait_ge(*sig("mean").at((l, which)))
                a, bb = tiles[0], tiles[-1] + 1
                nc.scalar.activation(small[:, 8 + a:8 + bb], small[:, 4 + a:4 + bb], ACT.Sqrt).then_inc(*sig("root").did((l, which)))
                for k in range(KD):
                    act.wait_ge(*sig("modulated").at((l, which, k)))
                    nc.scalar.activation(hT_hi[:, k, a * P:bb * P], hf[:, k % 2, a * P:bb * P], ACT.Copy).then_inc(*sig("h_hi").did((l, which, k)))

            act.wait_ge(vec_in.sem, 32)
            for l in range(DEPTH):
                act_t = active(l)
                if l == 0:
                    nc.scalar.activation(cond_act[:, :], cond_in[:, :], ACT.Silu).then_inc(*sig("cond_act").did(l))
                else:
                    nc.scalar.activation(cond_act[:, :], cond_in[:, :], ACT.Silu).then_inc(*sig("cond_act").did(l))
                act.wait_ge(*sig("cond_clear").at(l))
                act.wait_ge(*sig("cond_act").at(l))
                nc.scalar.activation(cond4[:, :, 0:2], cond_act[:, :].rearrange("p (k j) -> p k j", j=2), ACT.Copy).then_inc(*sig("cond_hi").did(l))
                split.up_to(slab_at[("in", l, 0, 0)] + RING - 1)
                act.wait_ge(row_in.sem, 16 * (l + 1))
                act.wait_ge(*sig("lam_sums").at(l))
                nc.scalar.activation(lam[:, 2:4], lam[:, 0:2], ACT.Exp).then_inc(*sig("lam_exp").did(l))
                if l:
                    act.wait_ge(*sig("lb_diff").at(l))
                    nc.scalar.activation(lb[:, :], small[:, 32:36], ACT.Sigmoid).then_inc(*sig("lb").did(l))
                    act.wait_ge(*sig("lb").at(l))
                act.wait_ge(*sig("lam_exp").at(l))
                phase_end(act, "act", "mod")
                if l == 0:
                    act.wait_ge(x_in.sem, 64)
                norm(l, 0, list(range(TILES)))
                act.wait_ge(*sig("h_lo").at((l, 0, KD - 1)))
                phase_end(act, "act", "norm0")
                b0 = slab_at[("in", l, 0, 0)]
                for c in range(len(IN_CHUNKS)):
                    split.up_to(b0 + 2 * c + 3)
                    for t in (0, 1):
                        if in_cols(l, c, t):
                            a, bb = in_cols(l, c, t)
                            act.wait_ge(*sig("acc_ready").at((("in", l, c), t)))
                            nc.scalar.activation(pj[:, t, a:bb], acc[t][:, 0:bb - a], ACT.Copy).then_inc(*sig("in_read_act").did((l, c, t)))
                            sig("in_read_act").seen[("all", l)] = sig("in_read_act").count
                split.up_to(slab_at[("out", l, 0, 0)] + RING - 1)
                act.wait_ge(*sig("in_read_act").at(("all", l)))
                phase_end(act, "act", "in")

                a0 = act_t[0] * P
                for h in range(DA_HEADS):
                    act.wait_ge(*sig("daqT_ps").at((l, h)))
                    nc.scalar.activation(daqT[:, h, a0:], tmp[0][:, a0:], ACT.Copy).then_inc(*sig("daT_read_act").did((l, h)))
                for t in range(TILES):
                    q = t in act_t
                    if t >= 2:
                        act.wait_ge(*sig("cT_ps").at((l, t - 2)))
                    if q:
                        nc.scalar.activation(c_tok[:, t % 2, 0:MLA_Q], pj[:, t, C_CQ:C_CKV], ACT.Square, accum_out=stats[:, t:t + 1]).then_inc(*sig("c_sq").did((l, t, 0)))
                    nc.scalar.activation(c_tok[:, t % 2, MLA_Q:], pj[:, t, C_CKV:C_KR], ACT.Square, accum_out=stats[:, 4 + t:5 + t]).then_inc(*sig("c_sq").did((l, t, 1)))
                    act.wait_ge(*sig("c_mean").at((l, t)))
                    nc.scalar.activation(stats[:, 16 + 2 * t:18 + 2 * t], stats[:, 8 + 2 * t:10 + 2 * t], ACT.Sqrt).then_inc(*sig("c_root").did((l, t)))
                    act.wait_ge(*sig("cT_ps").at((l, t)))
                    for i in range(0 if q else 2, 3):
                        g = vecs[:, l, VEC["q_norm"] + i:VEC["q_norm"] + i + 1]
                        ins = nc.scalar.activation(cT[:, i, :], tmp[2][:, i * P:(i + 1) * P], ACT.Copy, scale=g)
                        ins.then_inc(*sig("cT").did((l, t)))
                    if q:
                        act.wait_ge(*sig("mq_ps").at((l, t)))
                        nc.scalar.activation(q_tok[:, t % 2, :, :], acc[0][:, 0:MLA_HEADS * MLA_QK].rearrange("p (h d) -> p h d", h=MLA_HEADS), ACT.Copy).then_inc(*sig("q_tok").did((l, t)))
                        act.wait_ge(*sig("mqT_ps").at((l, t)))
                        nc.scalar.activation(mqT[:, :, t * P:(t + 1) * P], acc[2][0:MLA_QK, :].rearrange("p (h d) -> p h d", h=MLA_HEADS), ACT.Copy).then_inc(*sig("mqT_read").did((l, t)))
                act.wait_ge(*sig("mqT_read").last())
                phase_end(act, "act", "attn_prep")

                us = units(l)
                for u in range(len(us) + 1):
                    if u < len(us):
                        kind, t, h = us[u]
                        keys = TOK if t >= 2 else CTX
                        sc = (DA_DIM if kind == "da" else MLA_QK) ** -0.5
                        act.wait_ge(*sig("neg_max").at((l, u)))
                        if u >= 2:
                            act.wait_ge(*sig("probsT_ps").at((l, u - 2)))
                        ng = 2 if kind == "da" else 1
                        for g in range(ng):
                            o = 8 * (u % 2) + g
                            ins = nc.scalar.activation(probs[:, u % 2, g, 0:keys], tmp[2 * (u % 2) + g][:, 0:keys], ACT.Exp,
                                                       bias=stats[:, 32 + o:33 + o], scale=sc, accum_out=stats[:, 34 + o:35 + o])
                            if g == ng - 1:
                                ins.then_inc(*sig("exp").did((l, u)))
                    if u:
                        kind, t, h = us[u - 1]
                        nk = (TOK if t >= 2 else CTX) // P
                        act.wait_ge(*sig("probsT_ps").at((l, u - 1)))
                        if u >= 3:
                            act.wait_ge(*sig("o_ps").at((l, u - 3)))
                        nc.scalar.activation(probsT[:, (u - 1) % 2, 0:nk, :], acc[(u - 1) % 2][:, 0:nk * P].rearrange("p (s q) -> p s q", s=nk), ACT.Copy).then_inc(*sig("probsT").did((l, u - 1)))
                act.wait_ge(*sig("probsT").at((l, len(us) - 1)))
                phase_end(act, "act", "attn")

                for i in range(6):
                    act.wait_ge(*sig("gT_ps").at((l, i)))
                    if i < 4:
                        nc.scalar.activation(sig_f[:, i, :], tmp[i][:, :], ACT.Sigmoid).then_inc(*sig("sig_plus").did((l, i)))
                        nc.scalar.activation(hkT[:, i, :], tmp[i][:, :], ACT.Sigmoid, scale=-1.0).then_inc(*sig("gate_sig").did((l, i)))
                    else:
                        nc.scalar.activation(hqT[:, i - 4, a0:], tmp[i % 4][:, a0:], ACT.Copy, scale=HG_DIM ** -0.5).then_inc(*sig("gate_sig").did((l, i)))
                for i in range(4):
                    act.wait_ge(*sig("sig_plus").at((l, i)))
                    nc.scalar.activation(sig_f[:, i, :], sig_f[:, i, :], ACT.Ln, bias=lb[:, i:i + 1], scale=one_less_lb[:, i:i + 1]).then_inc(*sig("logf").did((l, i)))
                steps = [(p, n, m) for p in range(2) for n, m in enumerate(level_list())]
                for i in range(len(steps) + 1):
                    if i < len(steps) and steps[i][2]:
                        p, n, m = steps[i]
                        act.wait_ge(*sig("dec").at((l, p, n)))
                        w = SEQ if (m == 256 or l < DEPTH - 1) else SEQ // 2
                        nc.scalar.activation(dec[:, i % 2, :, 0:w], dec[:, i % 2, :, 0:w], ACT.Exp).then_inc(*sig("dec_exp").did((l, p, n)))
                    if i and steps[i - 1][2] >= 128:
                        p, n, m = steps[i - 1]
                        for b in level_banks(l, m):
                            act.wait_ge(*sig("s_ps").at((l, i - 1, b)))
                            if p and m == 128:
                                act.wait_ge(*sig("hg_o").at((l, 0)))
                            src = level_bank(i - 1, b)
                            if m == 128:
                                ins = nc.scalar.activation(s_off[:, :, b, :, :], src[:, :].rearrange("p (d h q) -> p h d q", d=2, q=P), ACT.Copy)
                            else:
                                ins = nc.scalar.activation(s_far[:, :, b, :], src[:, :].rearrange("p (h q) -> p h q", h=2), ACT.Copy)
                            ins.then_inc(*sig("s_read_act").did((l, i - 1, b)))
                            sig("s_read_act").seen[(l, p)] = sig("s_read_act").count
                for n, t in enumerate(act_t):
                    if n == 0:
                        act.wait_ge(*sig("hg_o").at((l, 1)))
                    else:
                        act.wait_ge(*sig("mixed").at((l, act_t[n - 1])))
                    nc.scalar.activation(ro[:, 0, 0:512], pj[:, t, 0:512], ACT.Square)
                    nc.scalar.activation(ro[:, 0, 512:768], acc[t][:, 0:256], ACT.Square).then_inc(*sig("ro_sq").did((l, t)))
                    nc.scalar.activation(ro[:, 1, 0:256], pj[:, t, C_HG:C_HG + 256], ACT.Silu).then_inc(*sig("ro_silu").did((l, t)))
                    act.wait_ge(*sig("ro_mean").at((l, t)))
                    nc.scalar.activation(stats[:, 16:24], stats[:, 8:16], ACT.Sqrt).then_inc(*sig("ro_root").did((l, t)))
                act.wait_ge(*sig("mixed").at((l, 3)))
                phase_end(act, "act", "hg")
                for k in range(KD):
                    act.wait_ge(*sig("oT_ps").at((l, k)))
                    nc.scalar.activation(hT_hi[:, k, a0:], tmp[k % 4][:, a0:], ACT.Copy).then_inc(*sig("oT_hi").did((l, k)))

                def gates(i):
                    for q in range(4):
                        act.wait_ge(*sig("gate_ps").at((l, i, q)))
                        nc.scalar.activation(gate_all[:, q // 2, (q % 2) * 512:(q % 2 + 1) * 512], tmp[2][:, :], ACT.Copy).then_inc(*sig("gate_all").did((l, i, q)))

                gates(0)
                split.up_to(slab_at[("out", l, 1, 1)] + RING)
                act.wait_ge(*sig("gate_all").at((l, 0, 3)))
                phase_end(act, "act", "out")
                norm(l, 1, act_t)
                gates(1)
                act.wait_ge(*sig("gate_all").at((l, 1, 3)))
                phase_end(act, "act", "norm1")
                if l % 2 == 0:
                    for g, (j0, j1) in enumerate(FF_GROUPS):
                        for j in range(j0, j1):
                            split.up_to(slab_at[("gu", l, j, 1)] + 2)
                            for t in range(TILES):
                                n = j * TILES + t
                                act.wait_ge(*sig("acc_ready").at((("gu", l, j), t)))
                                if n >= 2:
                                    pj_, pt = divmod(n - 2, TILES)
                                    act.wait_ge(*sig("act_tok").at((l, pj_, pt)))
                                nc.scalar.activation(act_gate[:, n % 2, :], acc[t][:, 0:GU], ACT.Silu).then_inc(*sig("silu").did((l, j, t)))
                            for c in range(2):
                                act.wait_ge(*sig("aT_ps").at((l, 2 * j + c)))
                                if c == 0 and j == FF_GROUPS[g][0] and g:
                                    act.wait_ge(*sig("acc_ready").at((("down", l, g - 1, 1), TILES - 1)))
                                nc.scalar.activation(aT_hi[:, 2 * (j - j0) + c, :], tmp[(2 * j + c) % 3][:, :], ACT.Copy).then_inc(*sig("aT_hi").did((l, 2 * j + c)))
                        nk = 2 * (j1 - j0)
                        for n in range(2):
                            split.up_to(slab_at[("down", l, g, n, (nk - 1) // 4 * 4)] + 2)
                    act.wait_ge(*sig("aT_hi").at((l, 2 * FF_CHUNKS - 1)))
                    phase_end(act, "act", "ffn")
                else:
                    experts_act(act)

        def experts_dve(dve, linked):
            tt, ts, stt = nc.vector.tensor_tensor, nc.vector.tensor_scalar, nc.vector.scalar_tensor_tensor
            marks["norm1"] = marks["dve"]
            dve.wait_ge(*lo_split.at(len(slabs) - 1))
            dve.sem_inc(sig("e_lo").sem, sig("e_lo").each())
            nc.vector.memset(ones_sq[:, :], 1.0)
            for r in range(4, 8):
                dve.wait_ge(*sig("h_tok_ps").at(r))
                if r == 4:
                    dve.wait_ge(*sig("h_tok_read").at(3))
                nc.vector.tensor_copy(h_tok_lo[:, r // 2 - 2, (r % 2) * 512:(r % 2 + 1) * 512], tmp[r % 4][:, :]).then_inc(*sig("h_tok_read").did(r))
            dve.wait_ge(*sig("logits").at())
            E = EXPERTS
            R = lambda i: route[:, i]
            wide = lambda i: route1[:, i].unsqueeze(2).broadcast_to([P, 2, E])
            order = c_("order8").unsqueeze(1).broadcast_to([P, 2, E])
            linked(nc.vector.tensor_copy(R(1), acc[0][:, 0:2 * E].rearrange("p (t e) -> p t e", t=2)))
            for i, (src, hot) in enumerate(((1, 2), (3, 4))):
                linked(nc.vector.tensor_reduce(route1[:, i], R(src), AX.X, ALU.max))
                linked(tt(R(5), R(src), wide(i), ALU.is_equal))
                linked(tt(R(5), R(5), order, ALU.mult))
                linked(nc.vector.tensor_reduce(route1[:, 2], R(5), AX.X, ALU.max))
                linked(tt(R(hot), R(5), wide(2), ALU.is_equal))
                if i == 0:
                    linked(stt(R(3), R(2), -3.0e38, R(1), ALU.mult, ALU.add))
            linked(tt(R(0), R(2), R(4), ALU.add))
            tt(route1[:, 4], route1[:, 1], route1[:, 0], ALU.subtract).then_inc(*sig("logit_gap").did())
            nc.vector.memset(items[:, :, 0:2], -1.0)
            nc.vector.memset(items[:, :, 2:4], 0.0).then_inc(*sig("chosen").did())
            dve.wait_ge(*sig("gap_exp").at())
            linked(ts(route1[:, 6], route1[:, 5], 1.0, None, ALU.add))
            linked(nc.vector.reciprocal(route1[:, 7], route1[:, 6]))
            linked(tt(route1[:, 8], route1[:, 7], route1[:, 5], ALU.mult))
            linked(tt(R(6), R(2), wide(7), ALU.mult))
            linked(tt(R(7), R(4), wide(8), ALU.mult))
            linked(tt(R(8), R(6), R(7), ALU.add))
            dve.wait_ge(*sig("ranks").at())
            linked(stt(R(9), acc[1][:, 0:2 * E].rearrange("p (t e) -> p t e", t=2), 1.0, R(0), ALU.add, ALU.mult))
            linked(nc.vector.tensor_reduce(route1[:, 9, 0:1], acc[1][:, 2 * E:3 * E], AX.X, ALU.max))
            for half in range(2):
                dst = items[:, 1 + half * E:1 + (half + 1) * E, :]
                ts(dst[:, :, 0:2].rearrange("p e t -> p t e"), R(9), -1.0 - P * half, None, ALU.add)
                linked(nc.vector.tensor_copy(dst[:, :, 2:4].rearrange("p e t -> p t e"), R(8)))
            ts(passes[:, :], route1[:, 9, 0:1], float(P), 1.0, ALU.is_gt, ALU.add).then_inc(*sig("passes_known").did())
            dve.wait_ge(*sig("passes_known").last())
            dve.wait_ge(*sig("h_tok_read").at(7))
            phase_end(dve, "dve", "route")
            marks["route"] = marks["dve"]
            for name in ("e_act", "e_rest", "e_add"):
                dve.sem_inc(sig(name).sem, sig(name).each())
            linked(nc.vector.memset(moe_sum[:, :, :], 0.0))
            linked(nc.vector.memset(pick_slot[:, :, :], 0.0))
            nc.vector.memset(acc[2][:, :], 0.0)
            nc.vector.memset(acc[3][:, :], 0.0).then_inc(*sig("y_cleared").did())

            def select(cols, signal):
                for t in range(2):
                    ins = ts(pick_tok[:, t, :], c_("slots"), cols[:, t:t + 1], None, ALU.is_equal)
                ins.then_inc(*signal.did(0))

            def gathered(at, signal):
                for r in range(4):
                    dve.wait_ge(*at(r))
                    nc.vector.tensor_copy(hg_lo[:, 2 * r:2 * r + 2, :], gather_banks[r][:, 2 * P:].rearrange("p (c s) -> p c s", c=2)).then_inc(*signal.did(r))

            def add(r, at, signal):
                t, n = divmod(r, 2)
                dve.wait_ge(*at)
                dst = moe_sum[:, t, n * 512:(n + 1) * 512]
                stt(dst, scatter_banks[r][:, :], cur[:, 2 + t:3 + t], dst, ALU.mult, ALU.add).then_inc(*signal.did(r))

            select(items[:, 1, 0:2], Prologue(sig("e_pick")))
            gathered(lambda r: sig("e_hg_hi").turn(r, 0), Prologue(sig("e_hg_lo")))

            def body(item, e):
                n = [0]

                def low(to):
                    while n[0] <= to:
                        q = n[0]
                        for half in range(2):
                            dve.wait_ge(*sig("e_hi").turn((q, half), item))
                            tt(e_half(w_lo, q, half), e_half(raw, q, half), e_half(w_hi, q, half).bitcast(F32), ALU.subtract).then_inc(*sig("e_lo").did((q, half)))
                        n[0] += 1

                def hidden_rest(j):
                    dve.wait_ge(*sig("e_high").turn(j, item))
                    tt(eT_lo[:, 2 * j:2 * j + 2, :], tmp[j % 2][:, 0:2 * P].rearrange("p (c s) -> p c s", c=2),
                       eT_hi[:, 2 * j:2 * j + 2, :].bitcast(F32), ALU.subtract).then_inc(*sig("e_rest").did(j))

                nc.vector.tensor_copy(cur[:, 2:4], items[:, item - 1, 2:4]).then_inc(*sig("e_cur").did(0))
                nc.vector.tensor_copy(cur[:, 0:2], items[:, item + 1, 0:2]).then_inc(*sig("e_cur").did(1))
                low(3)
                dve.wait_ge(sig("e_cur").sem, 2 * item)
                for r in range(4):
                    add(r, sig("e_scatter").turn(r, item), sig("e_add"))
                for j in range(FF_CHUNKS):
                    low(2 * j + 3)
                    dve.wait_ge(*sig("e_silu").turn(j, item))
                    dve.wait_ge(*(sig("e_hT_ps").turn(j - 2, item) if j >= 2 else sig("e_hT_ps").turn(j - 2 + FF_CHUNKS, item - 1)))
                    tt(e_tok[:, j % 2, :], e_gate[:, j % 2, :], acc[j % 2][:, GU:2 * GU], ALU.mult).then_inc(*sig("e_act").did(j))
                    if j:
                        hidden_rest(j - 1)
                dve.wait_ge(*sig("e_slot_ps").turn(0, item))
                select(cur[:, 0:2], sig("e_pick"))
                low(UP_SLABS + 3)
                hidden_rest(FF_CHUNKS - 1)
                low(UP_SLABS + 6)
                gathered(lambda r: sig("e_hg_hi").turn(r, item), sig("e_hg_lo"))
                low(E_SLABS - 1)

            end = experts_loop(dve, body)
            dve.wait_ge(*sig("e_add").turn(3, end - 1))
            nc.vector.tensor_copy(cur[:, 2:4], items[:, end - 1, 2:4]).then_inc(*sig("cur_last").did())
            dve.wait_ge(*sig("cur_last").at())
            for r in range(4):
                add(r, sig("scatter_last").at(r), sig("add_last"))
            dve.wait_ge(*sig("add_last").last())
            for t in range(2):
                linked(tt(moe_sum[:, t, :], moe_sum[:, t, :], gate_all[:, 0, :], ALU.mult))
                tt(x[:, 2 + t, :], x[:, 2 + t, :], moe_sum[:, t, :], ALU.add).then_inc(*sig("x_last").did(t))
            dve.wait_ge(*sig("final_sq").at(1))
            ts(small[:, 2:4], small[:, 0:2], 1.0 / D, 1e-6, ALU.mult, ALU.add).then_inc(*sig("final_mean").did())
            dve.wait_ge(*sig("final_root").at())
            linked(nc.vector.reciprocal(small[:, 6:8], small[:, 4:6]))
            dve.wait_ge(sig("final_gain_loaded").sem, 16)
            for t in range(2):
                stt(x[:, 2 + t, :], x[:, 2 + t, :], small[:, 6 + t:7 + t], final_gain[:, :], ALU.mult, ALU.mult).then_inc(*sig("final_x").did(t))

        @block.vector
        def _(dve):
            split = Splitter(dve, "lo")
            link = sig("dve_link")

            def linked(ins):
                ins.then_inc(*link.did())
                dve.wait_ge(*link.last())

            tt, ts, stt = nc.vector.tensor_tensor, nc.vector.tensor_scalar, nc.vector.scalar_tensor_tensor

            def norm(l, which, tiles):
                a, bb = tiles[0], tiles[-1] + 1
                dve.wait_ge(*sig("sq").at((l, which, tiles[-1])))
                ts(small[:, 4 + a:4 + bb], small[:, a:bb], 1.0 / D, 1e-6, ALU.mult, ALU.add).then_inc(*sig("mean").did((l, which)))
                dve.wait_ge(*sig("root").at((l, which)))
                linked(nc.vector.reciprocal(small[:, 12 + a:12 + bb], small[:, 8 + a:8 + bb]))
                for t in tiles:
                    ins = ts(xn[:, t, :], x[:, t, :], small[:, 12 + t:13 + t], None, ALU.mult)
                ins.then_inc(*sig("xn_ready").did((l, which)))
                for k in range(KD):
                    dve.wait_ge(*sig("xT").at((l, which, k)))
                    if k >= 2:
                        dve.wait_ge(*sig("h_lo").at((l, which, k - 2)))
                    for sg in sorted({t // 2 for t in tiles}, reverse=True):
                        j = 1 - sg
                        ins = ts(hf[:, k % 2, sg * SEQ:(sg + 1) * SEQ], tmp[k % 4][:, sg * SEQ:(sg + 1) * SEQ],
                                 scale_col[:, which, k, j:j + 1], shift_col[:, which, k, j:j + 1], ALU.mult, ALU.add)
                    ins.then_inc(*sig("modulated").did((l, which, k)))
                    if k:
                        rest(l, which, k - 1, a * P, bb * P)
                rest(l, which, KD - 1, a * P, bb * P)
                dve.wait_ge(*sig("h_lo").last())

            def rest(l, which, k, a, bb):
                dve.wait_ge(*sig("h_hi").at((l, which, k)))
                tt(hT_lo[:, k, a:bb], hf[:, k % 2, a:bb], hT_hi[:, k, a:bb].bitcast(F32), ALU.subtract).then_inc(*sig("h_lo").did((l, which, k)))

            dve.wait_ge(vec_in.sem, 32)
            dve.wait_ge(*consts_in_at())
            for l in range(DEPTH):
                act_t = active(l)
                lam_init = 0.8 - 0.6 * math.exp(-0.3 * l)
                nc.vector.memset(cond4[:, :, :].bitcast(F32), 0.0).then_inc(*sig("cond_clear").did(l))
                dve.wait_ge(*sig("cond_hi").at(l))
                dve.wait_ge(*sig("cond_clear").last())
                tt(cond4[:, :, 2:4], cond_act[:, :].rearrange("p (k j) -> p k j", j=2), cond4[:, :, 0:2].bitcast(F32),
                   ALU.subtract).then_inc(*sig("cond_ready").did(l))
                b0 = slab_at[("mod", l, 0, 0)]
                for n in range(12):
                    split.up_to(b0 + 2 * n + 2)
                    part, half = divmod(n, 2)
                    dst = {0: mod_rows[0:4, 0], 1: mod_rows[0:4, 1], 2: gate_rows[0:4, 0], 3: mod_rows[0:4, 2], 4: mod_rows[0:4, 3], 5: gate_rows[0:4, 1]}[part]
                    dve.wait_ge(*slab_used.at(b0 + 2 * n + 1))
                    nc.vector.tensor_copy(dst[:, half * 512:(half + 1) * 512], acc[n % 4][0:4, :]).then_inc(*sig("mod_row").did((l, n)))
                dve.wait_ge(*sig("mod_cols").at(l))
                cols = tmp[0][:, 0:8 * KD].rearrange("p (w s k j) -> p w s k j", w=2, s=2, j=2)
                nc.vector.tensor_copy(shift_col[:, :, :, :], cols[:, :, 0])
                for w, nm in enumerate(("norm_mix", "norm_ffn")):
                    g = vecs[:, l, VEC[nm]:VEC[nm] + KD].unsqueeze(2).broadcast_to([P, KD, 2])
                    ins = stt(scale_col[:, w, :, :], cols[:, w, 1], 1.0, g, ALU.add, ALU.mult)
                ins.then_inc(*sig("cols_read").did(l))
                dve.wait_ge(row_in.sem, 16 * (l + 1))
                lo_, lw = ROW["diff_lambda"]
                lv = rows[:, lo_:lo_ + lw].rearrange("p (a b d) -> p a b d", a=2, b=2)
                linked(tt(upd[:, 0, 0:128].rearrange("p (a d) -> p a d", a=2), lv[:, :, 0], lv[:, :, 1], ALU.mult))
                nc.vector.tensor_reduce(lam[:, 0:2], upd[:, 0, 0:128].rearrange("p (a d) -> p a d", a=2), AX.X, ALU.add).then_inc(*sig("lam_sums").did(l))
                if l:
                    lc = VEC["lb_logits"]
                    tt(small[:, 32:36], vecs[:, 1, lc:lc + 4], vecs[:, 0, lc:lc + 4], ALU.subtract).then_inc(*sig("lb_diff").did(l))
                    dve.wait_ge(*sig("lb").at(l))
                else:
                    linked(nc.vector.memset(lb[:, :], 0.0))
                linked(ts(one_less_lb[:, :], lb[:, :], -1.0, 1.0, ALU.mult, ALU.add))
                dve.wait_ge(*sig("lam_exp").at(l))
                linked(stt(lam[:, 4:5], lam[:, 3:4], -lam_init, lam[:, 2:3], ALU.add, ALU.subtract))
                o_, w_ = ROW["diff_norm"]
                linked(ts(rows[:, o_:o_ + w_], rows[:, o_:o_ + w_], 1.0 - lam_init, None, ALU.mult))
                split.up_to(slab_at[("in", l, 0, 0)] + RING - 1)
                dve.wait_ge(*sig("cols_read").last())
                phase_end(dve, "dve", "mod")
                if l == 0:
                    dve.wait_ge(x_in.sem, 64)
                norm(l, 0, list(range(TILES)))
                phase_end(dve, "dve", "norm0")
                b0 = slab_at[("in", l, 0, 0)]
                for c in range(len(IN_CHUNKS)):
                    split.up_to(b0 + 2 * c + 3)
                    for t in (2, 3):
                        a, bb = in_cols(l, c, t)
                        dve.wait_ge(*sig("acc_ready").at((("in", l, c), t)))
                        nc.vector.tensor_copy(pj[:, t, a:bb], acc[t][:, 0:bb - a]).then_inc(*sig("in_read_dve").did((l, c, t)))
                        sig("in_read_dve").seen[("all", l)] = sig("in_read_dve").count
                split.up_to(slab_at[("out", l, 0, 0)] + RING - 1)
                dve.wait_ge(*sig("in_read_dve").last())
                phase_end(dve, "dve", "in")
                marks[("mla", l)] = marks["dve"]

                def rope(src, nh, half, table, t):
                    n = nh * half
                    cs, sn = [c_(f"{k}_{table}").rearrange("p (t f) -> p t f", t=2)[:, t - 2].unsqueeze(1).broadcast_to([P, nh, half]) for k in ("cos", "sin")]
                    x1, x2 = src[:, :, 0], src[:, :, 1]
                    t1, t2 = [rope_tmp[:, i, 0:n].rearrange("p (h f) -> p h f", h=nh) for i in range(2)]
                    tt(t1, x1, sn, ALU.mult)
                    linked(tt(t2, x2, sn, ALU.mult))
                    linked(tt(x1, x1, cs, ALU.mult))
                    linked(tt(x2, x2, cs, ALU.mult))
                    linked(tt(x1, x1, t2, ALU.subtract))
                    return tt(x2, x2, t1, ALU.add)

                for t in (2, 3):
                    src = pj[:, t, C_DQ:C_DV].rearrange("p (h e f) -> p h e f", e=2, f=DA_DIM // 2)
                    ins = rope(src, 16, DA_DIM // 2, "da", t)
                    if t == 2:
                        linked(ins)
                ins.then_inc(*sig("roped").did((l, "da")))
                dve.wait_ge(*sig("roped").last())
                for h in range(DA_HEADS):
                    dve.wait_ge(*sig("dakT_ps").at((l, h)))
                    nc.vector.tensor_copy(dakT[:, h, :], tmp[1][:, :]).then_inc(*sig("daT_read_dve").did((l, h)))
                for t in range(TILES):
                    q = t in act_t
                    dve.wait_ge(*sig("c_sq").at((l, t, 1)))
                    if q:
                        ts(stats[:, 8 + 2 * t:9 + 2 * t], stats[:, t:t + 1], 1.0 / MLA_Q, 1e-6, ALU.mult, ALU.add)
                    else:
                        nc.vector.memset(stats[:, 8 + 2 * t:9 + 2 * t], 1.0)
                    ts(stats[:, 9 + 2 * t:10 + 2 * t], stats[:, 4 + t:5 + t], 1.0 / MLA_KV, 1e-6, ALU.mult, ALU.add).then_inc(*sig("c_mean").did((l, t)))
                    dve.wait_ge(*sig("c_root").at((l, t)))
                    linked(nc.vector.reciprocal(stats[:, 24 + 2 * t:26 + 2 * t], stats[:, 16 + 2 * t:18 + 2 * t]))
                    if q:
                        ts(c_tok[:, t % 2, 0:MLA_Q], pj[:, t, C_CQ:C_CKV], stats[:, 24 + 2 * t:25 + 2 * t], None, ALU.mult)
                    ts(c_tok[:, t % 2, MLA_Q:], pj[:, t, C_CKV:C_KR], stats[:, 25 + 2 * t:26 + 2 * t], None, ALU.mult).then_inc(*sig("c_tok").did((l, t)))
                    if q:
                        dve.wait_ge(*sig("q_tok").at((l, t)))
                        if t >= 2:
                            src = q_tok[:, t % 2, :, MLA_NOPE:].rearrange("p h (e f) -> p h e f", e=2)
                            rope(src, MLA_HEADS, MLA_ROPE // 2, "mla", t).then_inc(*sig("mq_roped").did((l, t)))
                            dve.wait_ge(*sig("mq_roped").last())
                    if t >= 2:
                        linked(rope(pj[:, t, C_KR:C_HQ].rearrange("p (h e f) -> p h e f", h=1, e=2), 1, MLA_ROPE // 2, "mla", t))
                    dve.wait_ge(*sig("mkv_ps").at((l, t)))
                    if t >= 2:
                        dve.wait_ge(*sig("mkT_ps").at((l, t - 2)))
                    kv = acc[1][:, :].rearrange("p (h d) -> p h d", h=MLA_HEADS)
                    nc.vector.tensor_copy(k_tok[:, t % 2, :, 0:MLA_NOPE], kv[:, :, 0:MLA_NOPE])
                    nc.vector.tensor_copy(pj[:, t, C_CQ:C_CQ + 256].rearrange("p (h d) -> p h d", h=MLA_HEADS), kv[:, :, MLA_NOPE:]).then_inc(*sig("kv_tok").did((l, t)))
                    kr = pj[:, t, C_KR:C_HQ].unsqueeze(1).broadcast_to([P, MLA_HEADS, MLA_ROPE])
                    nc.vector.tensor_copy(k_tok[:, t % 2, :, MLA_NOPE:], kr).then_inc(*sig("mk_roped").did((l, t)))
                    dve.wait_ge(*sig("mkT_ps").at((l, t)))
                    nc.vector.tensor_copy(mkT[:, :, t * P:(t + 1) * P], acc[3][0:MLA_QK, :].rearrange("p (h d) -> p h d", h=MLA_HEADS)).then_inc(*sig("mkT_read").did((l, t)))
                dve.wait_ge(*sig("mkT_read").last())
                phase_end(dve, "dve", "attn_prep")

                us = units(l)

                def finish(u):
                    kind, t, h = us[u]
                    dve.wait_ge(*sig("o_ps").at((l, u)))
                    o = acc[2 + u % 2]
                    s = 48 + 8 * (u % 2)
                    if kind == "mla":
                        ts(pj[:, t, 512 + h * 64:512 + (h + 1) * 64], o[:, 0:64], stats[:, s + 4:s + 5], None, ALU.mult).then_inc(*sig("attended").did((l, u)))
                        return
                    nc.vector.tensor_copy(pj[:, t, h * P:(h + 1) * P], o[:, 0:P]).then_inc(*sig("attended").did((l, u)))

                def maximum(u):
                    kind, t, h = us[u]
                    keys = TOK if t >= 2 else CTX
                    sc = (DA_DIM if kind == "da" else MLA_QK) ** -0.5
                    ng = 2 if kind == "da" else 1
                    o = 8 * (u % 2)
                    dve.wait_ge(*sig("scores").at((l, u)))
                    for g in range(ng):
                        ins = nc.vector.tensor_reduce(small[:, 16 + o + g:17 + o + g], tmp[2 * (u % 2) + g][:, 0:keys], AX.X, ALU.max)
                    linked(ins)
                    ts(stats[:, 32 + o:32 + o + ng], small[:, 16 + o:16 + o + ng], -sc, None, ALU.mult).then_inc(*sig("neg_max").did((l, u)))

                def weights(u):
                    kind, t, h = us[u]
                    keys = TOK if t >= 2 else CTX
                    ng = 2 if kind == "da" else 1
                    o = 8 * (u % 2)
                    s = 48 + o
                    dve.wait_ge(*sig("exp").at((l, u)))
                    if u >= 2:
                        dve.wait_ge(*sig("attended").at((l, u - 2)))
                    linked(nc.vector.reciprocal(stats[:, s + 4:s + 4 + ng] if kind == "mla" else stats[:, s:s + 2], stats[:, 34 + o:34 + o + ng]))
                    if kind == "da":
                        linked(tt(stats[:, s + 2:s + 3], stats[:, s + 1:s + 2], lam[:, 4:5], ALU.mult))
                        linked(ts(probs[:, u % 2, 1, 0:keys], probs[:, u % 2, 1, 0:keys], stats[:, s + 2:s + 3], None, ALU.mult))
                        stt(probs[:, u % 2, 0, 0:keys], probs[:, u % 2, 0, 0:keys], stats[:, s:s + 1], probs[:, u % 2, 1, 0:keys], ALU.mult, ALU.add).then_inc(*sig("probs").did((l, u)))

                for u in range(len(us) + 2):
                    if 1 <= u <= len(us):
                        weights(u - 1)
                    if u < len(us):
                        maximum(u)
                    if u >= 2:
                        finish(u - 2)
                dve.wait_ge(*sig("attended").last())
                phase_end(dve, "dve", "attn")
                marks[("attn", l)] = marks["dve"]

                for i in range(4):
                    dve.wait_ge(*sig("gate_sig").at((l, i)))
                    ts(hkT[:, i, :], hkT[:, i, :], one_less_lb[:, i:i + 1], None, ALU.mult).then_inc(*sig("hk").did((l, i)))
                ones = c_("ones").broadcast_to([P, SEQ])
                for i in range(4):
                    dve.wait_ge(*sig("logf").at((l, i)))
                    for sg in range(2):
                        a, bb = sg * SEQ, (sg + 1) * SEQ
                        o, g = cum[:, i, a:bb], sig_f[:, i, a:bb]
                        if i >= 2:
                            o, g = o[:, ::-1], g[:, ::-1]
                        ins = nc.vector.tensor_tensor_scan(o, ones, g, 0.0, ALU.mult, ALU.add)
                    ins.then_inc(*sig("cum").did((l, i)))
                dve.wait_ge(*sig("cum").last())
                dve.wait_ge(*sig("hk").last())
                dve.wait_ge(*sig("gate_sig").at((l, 5)))
                S0 = act_t[0] * P
                T = TOK - S0
                steps = level_steps()
                heads = [slice(0, 64), slice(64, P)]

                def blocks(ap, m):
                    return ap.rearrange("p (b e m) -> p b e m", e=2, m=m)

                def scaled(i):
                    p, n, m = steps[i]
                    f, bk = p, 2 + p
                    buf = n % 2
                    if i >= 2:
                        dve.wait_ge(*sig("s_ps").at((l, i - 2, 1)))
                    done = sig("level").did((l, p, n))
                    if m == 0:
                        tt(lev_k[:, buf, 0, S0:], hkT[:, f, S0:], hkT[:, bk, S0:], ALU.add).then_inc(*done)
                        return
                    d = dec[:, i % 2]
                    dve.wait_ge(*sig("dec_exp").at((l, p, n)))
                    if m <= 128:
                        q_, kf_, kb_ = blocks(hqT[:, p, S0:], m), blocks(hkT[:, f, S0:], m), blocks(hkT[:, bk, S0:], m)
                        dv = [d[:, q, 0:T // 2].rearrange("p (b m) -> p b m", m=m) for q in range(4)]
                        for r, h in zip(heads, range(2)):
                            for e in range(2):
                                tt(lev_q[r, buf, e, h, 0:T // 2].rearrange("p (b m) -> p b m", m=m), q_[r, :, 1 - e], dv[2 * e][r], ALU.mult)
                        lk = [blocks(lev_k[:, buf, q, S0:], m) for q in range(2)]
                        tt(lk[0][:, :, 0], kf_[:, :, 0], dv[1], ALU.mult)
                        tt(lk[1][:, :, 1], kb_[:, :, 1], dv[3], ALU.mult).then_inc(*done)
                    else:
                        for r, h in zip(heads, range(2)):
                            for e in range(2):
                                tt(lev_q[r, buf, e, h, :], hqT[r, p, CTX:], d[r, 2 * e, :], ALU.mult)
                        tt(lev_k[:, buf, 0, 0:CTX], hkT[:, f, 0:CTX], d[:, 1, :], ALU.mult)
                        tt(lev_k[:, buf, 1, 0:CTX], hkT[:, bk, 0:CTX], d[:, 3, :], ALU.mult).then_inc(*done)

                def placed(i):
                    p, n, m = steps[i]
                    if m > 64:
                        return
                    for b in level_banks(l, m):
                        dve.wait_ge(*sig("s_ps").at((l, i, b)))
                        if p and n == 0:
                            dve.wait_ge(*sig("hg_o").at((l, 0)))
                        if m == 0:
                            src = level_bank(i, b)[:, S0:].rearrange("p (t q) -> p t q", q=P)
                            ins = nc.vector.tensor_copy(s_diag[:, b, act_t[0]:, :], src)
                        else:
                            src = level_bank(i, b)[:, :].rearrange("p (t h q) -> p h t q", t=2, h=2)
                            dst = s_diag[:, :, 2 * b:2 * b + 2, :]
                            dve.wait_ge(*sig("s_read").at((l, i - 1, 1)))
                            mk = c_("masks").rearrange("p (v q) -> p v q", q=P)[:, LEVELS.index(m)].bitcast(mybir.dt.int32)
                            ins = nc.vector.copy_predicated(dst, mk.unsqueeze(1).unsqueeze(1).broadcast_to([P, 2, 2, P]), src)
                        ins.then_inc(*sig("s_read").did((l, i, b)))

                dve.wait_ge(*sig("lev_clear").at(l))
                for i in range(len(steps) + 1):
                    if i < len(steps):
                        scaled(i)
                    if i:
                        placed(i - 1)
                gains = [rows[:, o_:o_ + w_] for o_, w_ in (ROW["diff_norm"], ROW["hgrn_norm"])]
                for t in act_t:
                    da_o, hg_o = pj[:, t, 0:512].rearrange("p (h d) -> p h d", h=DA_HEADS), ro[:, 0, 512:768].rearrange("p (h d) -> p h d", h=HG_HEADS)
                    dve.wait_ge(*sig("ro_sq").at((l, t)))
                    nc.vector.tensor_reduce(stats[:, 0:4], ro[:, 0, 0:512].rearrange("p (h d) -> p h d", h=DA_HEADS), AX.X, ALU.add)
                    linked(nc.vector.tensor_reduce(stats[:, 4:8], hg_o, AX.X, ALU.add))
                    ts(stats[:, 8:12], stats[:, 0:4], 1.0 / P, 1e-5, ALU.mult, ALU.add)
                    ts(stats[:, 12:16], stats[:, 4:8], 1.0 / HG_DIM, 1e-6, ALU.mult, ALU.add).then_inc(*sig("ro_mean").did((l, t)))
                    dve.wait_ge(*sig("ro_root").at((l, t)))
                    linked(nc.vector.reciprocal(stats[:, 24:32], stats[:, 16:24]))
                    tt(hg_o, acc[t][:, 0:256].rearrange("p (h d) -> p h d", h=HG_HEADS), stats[:, 28:32].unsqueeze(2).broadcast_to([P, HG_HEADS, HG_DIM]), ALU.mult)
                    linked(tt(da_o, da_o, stats[:, 24:28].unsqueeze(2).broadcast_to([P, DA_HEADS, P]), ALU.mult))
                    tt(da_o, da_o, gains[0].unsqueeze(1).broadcast_to([P, DA_HEADS, P]), ALU.mult)
                    linked(tt(hg_o, hg_o, gains[1].unsqueeze(1).broadcast_to([P, HG_HEADS, HG_DIM]), ALU.mult))
                    dve.wait_ge(*sig("ro_silu").at((l, t)))
                    tt(pj[:, t, 768:1024], ro[:, 0, 512:768], ro[:, 1, 0:256], ALU.mult).then_inc(*sig("mixed").did((l, t)))
                dve.wait_ge(*sig("mixed").last())
                phase_end(dve, "dve", "hg")

                for k in range(KD):
                    dve.wait_ge(*sig("oT_hi").at((l, k)))
                    tt(hT_lo[:, k, S0:], tmp[k % 4][:, S0:], hT_hi[:, k, S0:].bitcast(F32), ALU.subtract).then_inc(*sig("oT_lo").did((l, k)))

                def add_gated(key, t, n):
                    j = 1 - t // 2
                    dve.wait_ge(*sig("acc_ready").at((key, t)))
                    linked(tt(upd[:, 0, :], acc[t][:, :], gate_all[:, j, n * 512:(n + 1) * 512], ALU.mult))
                    return tt(x[:, t, n * 512:(n + 1) * 512], x[:, t, n * 512:(n + 1) * 512], upd[:, 0, :], ALU.add)

                dve.wait_ge(*sig("gate_all").at((l, 0, 3)))
                for n in range(2):
                    split.up_to(slab_at[("out", l, n, 1)] + 2)
                    for t in act_t:
                        add_gated(("out", l, n), t, n).then_inc(*sig("acc_added").did((l, "out", n, t)))
                        dve.wait_ge(*sig("acc_added").last())
                phase_end(dve, "dve", "out")
                norm(l, 1, act_t)
                phase_end(dve, "dve", "norm1")
                if l % 2 == 0:
                    for g, (j0, j1) in enumerate(FF_GROUPS):
                        for j in range(j0, j1):
                            split.up_to(slab_at[("gu", l, j, 1)] + 2)
                            for t in range(TILES):
                                n = j * TILES + t
                                dve.wait_ge(*sig("silu").at((l, j, t)))
                                if j:
                                    dve.wait_ge(*sig("aT_ps").at((l, 2 * j - 1)))
                                tt(act_tok[:, t, :], act_gate[:, n % 2, :], acc[t][:, GU:2 * GU], ALU.mult).then_inc(*sig("act_tok").did((l, j, t)))
                            for c in range(2):
                                dve.wait_ge(*sig("aT_hi").at((l, 2 * j + c)))
                                kc = 2 * (j - j0) + c
                                tt(aT_lo[:, kc, :], tmp[(2 * j + c) % 3][:, :], aT_hi[:, kc, :].bitcast(F32), ALU.subtract).then_inc(*sig("aT_lo").did((l, 2 * j + c)))
                        nk = 2 * (j1 - j0)
                        for n in range(2):
                            split.up_to(slab_at[("down", l, g, n, (nk - 1) // 4 * 4)] + 2)
                            for t in range(TILES):
                                add_gated(("down", l, g, n), t, n).then_inc(*sig("acc_added").did((l, "down", g, n, t)))
                                dve.wait_ge(*sig("acc_added").last())
                    phase_end(dve, "dve", "ffn")
                    marks[("layer", l + 1)] = marks["dve"]
                else:
                    experts_dve(dve, linked)

        seen.update({k: s.seen for k, s in signals.items()})
        seen["phases"] = {k: v for k, v in marks.items() if k not in ("pe", "act", "dve")}


def layout(inputs):
    f = lambda k: np.ascontiguousarray(np.asarray(inputs[k]))
    cols = lambda v: v.reshape(-1, P).T
    arrays = {k: f(k) for k in ("x", "ctx", "w_mod", "b_mod", "w_in", "w_out", "mla_w_uq", "mla_w_ukv", "ffn_w_gate",
                                "ffn_w_up", "ffn_w_down", "moe_router", "moe_w_gate", "moe_w_up", "moe_w_down")}
    arrays["consts"] = constants()[0]
    arrays["cond"] = np.stack([cols(f("c")[0]), cols(f("c_ctx"))], 2).reshape(P, -1)
    vecs = np.zeros((P, DEPTH, VEC_COLS), np.float32)
    rows = np.zeros((P, DEPTH, ROW_COLS), np.float32)
    for l in range(DEPTH):
        for name, v in (("norm_mix", f("norm_mix")[l]), ("norm_ffn", f("norm_ffn")[l]), ("q_norm", f("mla_q_norm")[l]),
                        ("kv_norm", f("mla_kv_norm")[l]), ("lb_logits", f("hgrn_lb_logits")[:, l])):
            c = cols(v)
            vecs[:, l, VEC[name]:VEC[name] + c.shape[1]] = c
        for name, v in (("diff_norm", f("diff_norm")[l]), ("hgrn_norm", f("hgrn_norm")[l]), ("diff_lambda", f("diff_lambda")[l])):
            o, w = ROW[name]
            rows[:, l, o:o + w] = v.reshape(-1)
    arrays["vecs"], arrays["rows"] = vecs, rows
    arrays["norm_final"] = np.tile(f("norm_final"), (P, 1))
    return {k: np.ascontiguousarray(v) for k, v in arrays.items()}


def kernel(**inputs):
    import concourse.bacc as bacc
    from concourse.bass_utils import run_bass_kernel_spmd

    arrays = layout(inputs)

    def build(known):
        nc = bacc.Bacc("TRN2", target_bir_lowering=False, num_devices=1)
        dram = {k: nc.dram_tensor(k, v.shape, mybir.dt.from_np(v.dtype), kind="ExternalInput").ap() for k, v in arrays.items()}
        out = nc.dram_tensor("out", (1, SEQ, D), F32, kind="ExternalOutput").ap()
        seen = {}
        program(nc, dram, out, known, seen)
        return nc, seen

    nc, seen = build(build({})[1])
    return run_bass_kernel_spmd(nc, [arrays], core_ids=[0]).results[0]["out"]
```

```python
import math
from contextlib import ExitStack

import concourse.bass as bass
import numpy as np
from concourse import mybir

F32 = mybir.dt.float32
F32R = mybir.dt.float32r
ALU = mybir.AluOpType
ACT = mybir.ActivationFunctionType
AX = mybir.AxisListType

P = 128
D = 1024
KD = D // P
DEPTH = 2
SEQ = CTX = 256
TOK = SEQ + CTX
TILES = TOK // P
GRID_W, ROPE_BASE = 64, 10000.0
DA_HEADS, DA_DIM = 4, 64
MLA_HEADS, MLA_NOPE, MLA_ROPE, MLA_V, MLA_Q, MLA_KV = 4, 64, 32, 64, 256, 128
MLA_QK = MLA_NOPE + MLA_ROPE
HG_HEADS, HG_DIM = 4, 64
IN_SPLITS = (512, 512, 512, MLA_Q, MLA_KV, MLA_ROPE, 256, 256, 256, 256, 256)
IN_COLS = sum(IN_SPLITS)
(C_DQ, C_DK, C_DV, C_CQ, C_CKV, C_KR, C_HQ, C_HI, C_FF, C_FB, C_HG) = [sum(IN_SPLITS[:i]) for i in range(11)]
IN_CHUNKS = [(C_DQ, C_DK), (C_DK, C_DV), (C_DV, C_CQ), (C_CQ, C_HQ), (C_HQ, C_FF), (C_FF, C_HG), (C_HG, IN_COLS)]
CTX_KEYS_ONLY = {0: None, 3: (C_CKV, C_HQ), 4: (C_HI, C_FF), 6: None}
FF = 2816
EXPERTS = 8
SLAB = 2048
RING = 3
HF = 4
DECAYS = 3
MOD_CHUNKS, MOD_FIRST = 6 * D // 512, 2 * D // 512
GU = 256
FF_CHUNKS = FF // GU
LEVELS = [1, 2, 4, 8, 16, 32, 64]
FF_GROUPS = [(0, 6), (6, 11)]


def constants():
    p = np.arange(P)
    cols = {"ident": np.eye(P)}
    same = lambda m: (p[:, None] // (2 * m) == p[None] // (2 * m)) & (p[:, None] // m != p[None] // m)
    cols["masks"] = np.concatenate([same(m) for m in LEVELS], 1)
    pos = np.arange(SEQ)
    for name, rot in (("da", DA_DIM), ("mla", MLA_ROPE)):
        n = rot // 4
        inv = (ROPE_BASE ** (-np.arange(n, dtype=np.float32) / n)).astype(np.float32)
        ang = np.concatenate([(pos // GRID_W)[:, None] * inv, (pos % GRID_W)[:, None] * inv], -1)
        ang = ang.astype(np.float32).reshape(2, P, -1)
        cols[f"cos_{name}"] = np.concatenate(list(np.cos(ang)), 1)
        cols[f"sin_{name}"] = np.concatenate(list(np.sin(ang)), 1)
    pick = np.zeros((P, 2))
    for j in range(2):
        pick[[j, j + 2], j] = 1
    cols["pick"] = pick
    cols["slots"] = np.tile(np.arange(P), (P, 1))
    cols["earlier"] = p[:, None] < p[None]
    cols["ones"] = np.ones((P, 1))
    cols["order8"] = np.tile(8.0 - np.arange(EXPERTS), (P, 1))
    at, n = {}, 0
    for k, v in cols.items():
        at[k] = (n, v.shape[1])
        n += v.shape[1]
    return np.concatenate(list(cols.values()), 1).astype(np.float32), at


VEC = {"norm_mix": 0, "norm_ffn": 8, "q_norm": 16, "kv_norm": 18, "lb_logits": 19, "b_mod": 23}
VEC_COLS = 71
ROW = {"diff_norm": (0, 128), "hgrn_norm": (128, 64), "diff_lambda": (192, 256)}
ROW_COLS, ROW_GAINS = 448, 192


class Prologue:

    def __init__(self, signal):
        self.source = signal

    def did(self, key=None):
        return self.source.sem, 1


class Signal:

    def __init__(self, sem, known):
        self.sem, self.known, self.seen, self.count = sem, known, {}, 0

    def did(self, key=None):
        self.count += 1
        self.seen[key] = self.count
        return self.sem, 1

    def at(self, key=None):
        return self.sem, self.known.get(key, 1)

    def last(self):
        return self.sem, self.count

    def each(self):
        return len(self.known) or 1

    def turn(self, key, item):
        return self.sem, self.known.get(key, 1) + self.each() * item


def program(nc, dram, out, known, seen):
    table, at = constants()
    NCONST = table.shape[1]
    signals = {}

    with ExitStack() as ctx:

        def sig(name):
            if name not in signals:
                signals[name] = Signal(ctx.enter_context(nc.semaphore(name)), known.get(name, {}))
            return signals[name]

        cursor = [16544]

        def place(name, shape, dt=F32, offset=None):
            size = int(np.prod(shape[1:])) * 4
            where = cursor[0] if offset is None else offset
            if offset is None:
                cursor[0] += (size + 31) // 32 * 32
            return nc.alloc_sbuf_tensor_at(name, shape, dt, offset=where)

        const = place("const", [P, NCONST])
        vecs = place("vecs", [P, DEPTH, VEC_COLS])
        cond_in = place("cond_in", [P, 2 * KD])
        cond_act = place("cond_act", [P, KD, 2])
        cond4 = place("cond4", [P, KD, 4], F32R)
        rows = place("rows", [P, DEPTH, ROW_GAINS])
        lam = place("lam", [P, DEPTH, 8])
        lb = place("lb", [P, DEPTH, 4])
        one_less_lb = place("one_less_lb", [P, DEPTH, 4])
        small = place("small", [P, 64])
        stats = place("stats", [P, 64])
        mod_cols = place("mod_cols", [P, DEPTH, 6, KD, 2])
        scale_col = place("scale_col", [P, KD, 2])
        x = place("x", [P, TILES, D])
        raw = place("raw", [P, RING, SLAB])
        w_hi = place("w_hi", [P, RING, SLAB], F32R)
        w_lo = place("w_lo", [P, RING, SLAB], F32R)
        H = cursor[0]
        hT_hi = place("hT_hi", [P, KD, TOK], F32R)
        hT_lo = place("hT_lo", [P, KD, TOK], F32R)
        PJ = cursor[0]
        pj = place("pj", [P, TILES, IN_COLS])
        F = cursor[0]
        END = 229368

        def over(name, shape, base, dt=F32):
            size = (int(np.prod(shape[1:])) * 4 + 31) // 32 * 32
            t = nc.alloc_sbuf_tensor_at(name, shape, dt, offset=base[0])
            base[0] += size
            assert base[0] <= END, (name, base[0] - END)
            return t

        b = [F]
        mod_row = over("mod_row", [4, 512], b)
        FREE = b[0]
        b = [H]
        lam_in = over("lam_in", [P, DEPTH, ROW_COLS - ROW_GAINS], b)
        b = [PJ]
        xn = over("xn", [P, TILES, D], b)
        hf = over("hf", [P, HF, TOK], b)
        b = [FREE]
        gate_all = over("gate_all", [P, 2, D], b)
        upd = over("upd", [P, 2, 512], b)
        act_gate = over("act_gate", [P, 2, GU], b)
        act_tok = over("act_tok", [P, TILES, GU], b)
        b = [H]
        daqT = over("daqT", [P, DA_HEADS, TOK], b)
        dakT = over("dakT", [P, DA_HEADS, TOK], b)
        mqT = over("mqT", [MLA_QK, MLA_HEADS, TOK], b)
        mkT = over("mkT", [MLA_QK, MLA_HEADS, TOK], b)
        assert b[0] <= PJ
        b = [FREE]
        w_uq = over("w_uq", [P, 2, MLA_HEADS * MLA_QK], b)
        w_ukv = over("w_ukv", [P, MLA_HEADS * (MLA_NOPE + MLA_V)], b)
        c_tok = over("c_tok", [P, TILES, MLA_Q + MLA_KV], b)
        q_tok = over("q_tok", [P, 2, MLA_HEADS, MLA_QK], b)
        k_tok = over("k_tok", [P, 2, MLA_HEADS, MLA_QK], b)
        rope_tmp = over("rope_tmp", [P, 2, 512], b)
        cT = over("cT", [P, 2, 3, P], b)
        b = [FREE]
        probs = over("probs", [P, 2, 2, TOK], b)
        probsT = over("probsT", [P, 2, 4, P], b)
        b = [H]
        hqT = over("hqT", [P, 2, TOK], b)
        sig_f = over("sig_f", [P, 4, TOK], b)
        hkT = over("hkT", [P, 4, TOK], b)
        cum = over("cum", [P, 4, TOK], b)
        s_far = over("s_far", [P, 2, 2, SEQ], b)
        assert b[0] <= PJ, b[0] - PJ
        b = [H + 4 * TOK * 2]
        s_diag = over("s_diag", [P, 2, TILES, P], b)
        s_off = over("s_off", [P, 2, 2, 2, P], b)
        b = [FREE]
        dec = over("dec", [P, DECAYS, 4, SEQ], b)
        lev_k = over("lev_k", [P, 2, 2, TOK], b)
        lev_q = pj[:, :, C_DV:C_DV + 2 * SEQ].rearrange("p (b d) (h s) -> p b d h s", b=2, h=2)
        squared = over("squared", [P, 2, 512], b)
        b = [PJ]
        AK = 2 * max(e - s for s, e in FF_GROUPS)
        aT_hi = over("aT_hi", [P, AK, TOK], b, F32R)
        aT_lo = over("aT_lo", [P, AK, TOK], b, F32R)
        assert b[0] <= F

        b = [PJ]
        h_tok_hi = over("h_tok_hi", [P, 2, D], b, F32R)
        h_tok_lo = over("h_tok_lo", [P, 2, D], b, F32R)
        hg_hi = over("hg_hi", [P, KD, P], b, F32R)
        hg_lo = over("hg_lo", [P, KD, P], b, F32R)
        eT_hi = over("eT_hi", [P, 2 * FF_CHUNKS, P], b, F32R)
        eT_lo = over("eT_lo", [P, 2 * FF_CHUNKS, P], b, F32R)
        pick_tok = over("pick_tok", [P, 2, P], b, F32R)
        assert b[0] <= F
        b = [H]
        moe_sum = over("moe_sum", [P, 2, D], b)
        y_sb = over("y_sb", [P, D], b)
        e_gate = over("e_gate", [P, 2, GU], b)
        e_tok = over("e_tok", [P, 2, GU], b)
        pick_slot = over("pick_slot", [P, 2, P], b)
        final_gain = over("final_gain", [P, D], b)
        squares = over("squares", [P, D], b)
        assert b[0] <= PJ
        b = [FREE + 2 * D * 4]
        router = over("router", [P, KD, EXPERTS], b)
        ones_sq = over("ones_sq", [P, P], b)
        items = over("items", [P, 2 * EXPERTS + 2, 4], b)
        cur = over("cur", [P, 4], b)
        route = over("route", [P, 12, 2, EXPERTS], b)
        route1 = over("route1", [P, 12, 2], b)
        passes = nc.alloc_sbuf_tensor_at("passes", [P, 1], mybir.dt.int32, offset=b[0])

        def c_(name):
            o, w = at[name]
            return const[:, o:o + w]

        ident = c_("ident")
        acc = [ctx.enter_context(nc.psum_tensor(f"acc{i}", [P, 512], F32)) for i in range(4)]
        tmp = [ctx.enter_context(nc.psum_tensor(f"tmp{i}", [P, 512], F32)) for i in range(4)]

        slabs, slab_at = [], {}

        last_slab = {}

        def slab(key, nk, w, parts):
            slab_at[key] = len(slabs)
            slabs.append((key, nk, w, parts))

        def rows_of(wt, k0, nk, c0, c1):
            return wt[k0 * P:(k0 + nk) * P, c0:c1].rearrange("(k p) n -> p k n", p=P)

        def two_halves(key, wt, k0, nk, c0, c1):
            w = c1 - c0
            h = nk // 2
            slab(key, nk, w, [(0, h, w, 0, w, rows_of(wt, k0, h, c0, c1)), (h, nk, w, 0, w, rows_of(wt, k0 + h, nk - h, c0, c1))])

        def mod_slabs(l, first, last):
            for n in range(first, last):
                for kh in range(2):
                    two_halves(("mod", l, n, kh), dram["w_mod"][l], 4 * kh, 4, n * 512, (n + 1) * 512)

        for l in range(DEPTH):
            if l == 0:
                mod_slabs(0, 0, MOD_FIRST)
            for c, (c0, c1) in enumerate(IN_CHUNKS):
                for kh in range(2):
                    two_halves(("in", l, c, kh), dram["w_in"][l], 4 * kh, 4, c0, c1)
            if l == 0:
                mod_slabs(0, MOD_FIRST, MOD_CHUNKS)
                mod_slabs(1, 0, MOD_CHUNKS)
            for n in range(2):
                for kh in range(2):
                    two_halves(("out", l, n, kh), dram["w_out"][l], 4 * kh, 4, n * 512, (n + 1) * 512)
            if l % 2 == 0:
                for g, (j0, j1) in enumerate(FF_GROUPS):
                    for j in range(j0, j1):
                        for kh in range(2):
                            parts = [(0, 4, 512, o, o + GU, rows_of(dram[f"ffn_w_{nm}"][0], 4 * kh, 4, j * GU, (j + 1) * GU))
                                     for nm, o in (("gate", 0), ("up", GU))]
                            slab(("gu", l, j, kh), 4, 512, parts)
                    nk = 2 * (j1 - j0)
                    for n in range(2):
                        for s in range(0, nk, 4):
                            two_halves(("down", l, g, n, s), dram["ffn_w_down"][0], 2 * j0 + s, min(4, nk - s), n * 512, (n + 1) * 512)

        for i, (key, *_) in enumerate(slabs):
            if key[0] != "mod" and (i + 1 == len(slabs) or slabs[i + 1][0][:-1] != key[:-1]):
                last_slab[i] = key[:-1]

        def view(t, i, nk, w):
            return t[:, i % RING, 0:nk * w].rearrange("p (k n) -> p k n", k=nk)

        loaded = [sig(f"slab_loaded{i}") for i in range(RING)]
        hi_split, lo_split, slab_used = sig("hi_split"), sig("lo_split"), sig("slab_used")

        def used(i):
            return sig("acc_ready").at((last_slab[i], TILES - 1)) if i in last_slab else slab_used.at(i)

        def mod_split(l, n):
            return l == 0 and n >= MOD_FIRST

        class Splitter:

            def __init__(self, eng, part):
                self.eng, self.part, self.n = eng, part, 0

            def up_to(self, last):
                while self.n < min(last + 1, len(slabs)):
                    i = self.n
                    key, nk, w, _ = slabs[i]
                    if key[0] == "mod" and not mod_split(*key[1:3]):
                        self.n += 1
                        continue
                    src = raw[:, i % RING, 0:nk * w]
                    hi, lo = w_hi[:, i % RING, 0:nk * w], w_lo[:, i % RING, 0:nk * w]
                    if i >= RING:
                        self.eng.wait_ge(*used(i - RING))
                    if self.part == "hi":
                        self.eng.wait_ge(*loaded[i % RING].at(i))
                        nc.scalar.activation(hi, src, ACT.Copy).then_inc(*hi_split.did(i))
                    else:
                        self.eng.wait_ge(*hi_split.at(i))
                        nc.vector.tensor_tensor(lo, src, hi.bitcast(F32), ALU.subtract).then_inc(*lo_split.did(i))
                    self.n += 1

        def active(l):
            return list(range(TILES)) if l < DEPTH - 1 else [2, 3]

        def in_cols(l, c, t):
            if t in active(l):
                return IN_CHUNKS[c]
            return CTX_KEYS_ONLY.get(c, IN_CHUNKS[c])

        consts_in, x_in = sig("consts_loaded"), sig("x_loaded")
        vec_in, row_in = sig("vecs_loaded"), sig("rows_loaded")
        mlaw_in = sig("mla_weights_loaded")
        stored = sig("stored")
        phase = sig("phase_ended")
        ENGINES = 3
        marks = {}

        def phase_end(eng, who, n):
            eng.sem_inc(phase.sem, 1)
            marks[who] = marks.get(who, 0) + 1
            eng.wait_ge(phase.sem, ENGINES * marks[who])

        UP_SLABS, DOWN_SLABS = 2 * FF_CHUNKS, FF_CHUNKS
        E_SLABS = UP_SLABS + DOWN_SLABS
        assert E_SLABS % RING == 0
        base_slot = len(slabs) % RING
        e_slot = lambda q: (base_slot + q) % RING
        HALF = SLAB // 2
        e_loaded = [[sig(f"expert_half{h}_loaded{i}") for h in range(2)] for i in range(RING)]

        def e_loaded_at(q, half, item):
            return e_loaded[e_slot(q)][half].sem, 16 * ((item - 1) * (E_SLABS // RING) + q // RING + 1)

        def e_half(t, q, half):
            return t[:, e_slot(q), half * HALF:(half + 1) * HALF]

        def e_moving(t, q, kk, n0):
            if q < UP_SLABS:
                return t[:, e_slot(q), :].rearrange("p (u k n) -> p u k n", u=2, k=4)[:, :, kk, :]
            return t[:, e_slot(q), kk * D + n0:kk * D + n0 + 512]

        gather_banks = [tmp[2], tmp[3], acc[0], acc[1]]
        scatter_banks = [tmp[2], tmp[3], tmp[1], tmp[2]]

        def experts_loop(eng, body):
            eng.wait_ge(*sig("passes_known").at())
            n = eng.value_load(passes[0:1, 0:1], min_val=1, max_val=2)
            with eng.Fori(0, n) as half:
                with eng.Fori(0, EXPERTS) as e:
                    body(half * EXPERTS + e + 1, e)
            return n * EXPERTS + 1

        def mod_before(l, n):
            return (l, n - 1) if n else (l - 1, MOD_CHUNKS - 1) if l else None

        BESIDE_UNIT = TILES * DA_HEADS
        AHEAD_OF_LEVELS = 4
        assert 2 * (MOD_CHUNKS - MOD_FIRST) == TILES * MLA_HEADS and 2 * MOD_CHUNKS == AHEAD_OF_LEVELS + 2 * 10

        def modulated(l, which, k):
            return sig("modulated_by_act" if k % 2 else "modulated_by_dve").at((l, which, k))

        def consts_in_at():
            return consts_in.sem, 16

        def level_list():
            return [0] + LEVELS + [128, 256]

        def hg_out(t):
            return acc[t // 2][:, t % 2 * 256:(t % 2 + 1) * 256]

        SQUARES_AT, ROOTS_AT, GAINS_AT = 2, 5, 6

        def level_steps():
            return [(p, n, m) for p in range(2) for n, m in enumerate(level_list())]

        def level_banks(l, m):
            return [1] if l == DEPTH - 1 and 0 < m <= P else [0, 1]

        def level_bank(i, b):
            return tmp[(2 * i + b) % 4]

        def level_read(l, i, b):
            return sig("s_read_act" if level_steps()[i][2] >= P else "s_read").at((l, i, b))

        def units(l):
            return [("da", t, h) for t in active(l) for h in range(DA_HEADS)] + \
                   [("mla", t, h) for t in active(l) for h in range(MLA_HEADS)]

        block = ctx.enter_context(nc.Block())

        def expert_loads(sp):
            sp.wait_ge(phase.sem, ENGINES * known.get("phases", {}).get("norm1", 1))
            sp.dma_start(router[:, :, :], dram["moe_router"][0].rearrange("(k p) e -> p k e", p=P)).then_inc(sig("router_loaded").sem, 16)
            sp.wait_ge(phase.sem, ENGINES * known.get("phases", {}).get("route", 1))
            sp.dma_start(final_gain[:, :], dram["norm_final"]).then_inc(sig("final_gain_loaded").sem, 16)

            def body(item, e):
                for q in range(E_SLABS):
                    back, turn = (q - RING, item) if q >= RING else (q - RING + E_SLABS, item - 1)
                    for half, name in enumerate(("gate", "up")):
                        sp.wait_ge(*sig("e_lo").turn((back, half), turn))
                        if q < UP_SLABS:
                            j, kh = divmod(q, 2)
                            src = dram[f"moe_w_{name}"][0][e][kh * 512:(kh + 1) * 512, j * GU:(j + 1) * GU].rearrange("(k p) n -> p k n", p=P)
                            dst = e_half(raw, q, half).rearrange("p (k n) -> p k n", k=4)
                        else:
                            k0 = 2 * (q - UP_SLABS) + half
                            src, dst = dram["moe_w_down"][0][e][k0 * P:(k0 + 1) * P, :], e_half(raw, q, half)
                        sp.dma_start(dst, src).then_inc(e_loaded[e_slot(q)][half].sem, 16)

            experts_loop(sp, body)
            for t in range(2):
                sp.wait_ge(*sig("final_x").at(t))
                sp.dma_start(out[0, t * P:(t + 1) * P, :], x[:, 2 + t, :]).then_inc(stored.sem, 16)
            sp.wait_ge(stored.sem, 32)

        def loads(sp):
            def slab_loads(first, last):
                for i in range(first, last):
                    _, nk, w, parts = slabs[i]
                    before = slabs[i - RING][0] if i >= RING else None
                    if before and before[0] == "mod" and not mod_split(*before[1:3]):
                        sp.wait_ge(*slab_used.at(i - RING))
                    elif i >= RING:
                        sp.wait_ge(*hi_split.at(i - RING))
                        sp.wait_ge(*lo_split.at(i - RING))
                    dst = view(raw, i, nk, w)
                    for n, (ka, kb, _, ca, cb, src) in enumerate(parts):
                        sp.dma_start(dst[:, ka:kb, ca:cb], src).then_inc(loaded[i % RING].sem, 16)
                    loaded[i % RING].count += 31
                    loaded[i % RING].did(i)

            sp.dma_start(cond_in[:, :], dram["cond"]).then_inc(vec_in.sem, 16)
            sp.dma_start(vecs[:, :, :], dram["vecs"]).then_inc(vec_in.sem, 16)
            sp.dma_start(const[:, :], dram["consts"]).then_inc(consts_in.sem, 16)
            slab_loads(0, RING)
            sp.dma_start(rows[:, :, :], dram["rows"][:, :, 0:ROW_GAINS]).then_inc(row_in.sem, 16)
            sp.dma_start(lam_in[:, :, :], dram["rows"][:, :, ROW_GAINS:]).then_inc(row_in.sem, 16)
            for t in range(TILES):
                src = dram["ctx"][0] if t < 2 else dram["x"][0]
                sp.dma_start(x[:, t, :], src[(t % 2) * P:(t % 2 + 1) * P, :]).then_inc(x_in.sem, 16)
            done = RING
            for l in range(DEPTH):
                if l:
                    end = slab_at[("in", l, 0, 0)] + RING
                    slab_loads(done, end)
                    done = end
                    sp.wait_ge(phase.sem, ENGINES * known.get("phases", {}).get(("layer", l), 1))
                sp.dma_start(w_uq[:, :, :], dram["mla_w_uq"][l].rearrange("(k p) n -> p k n", p=P)).then_inc(mlaw_in.sem, 16)
                sp.dma_start(w_ukv[:, :], dram["mla_w_ukv"][l]).then_inc(mlaw_in.sem, 16)
                end = slab_at[("in", l + 1, 0, 0)] if l + 1 < DEPTH else len(slabs)
                slab_loads(done, end)
                done = end
            expert_loads(sp)

        @block.sync
        def _(sp):
            loads(sp)

        def experts_pe(pe):
            for r in range(8):
                part, t, half = (hT_hi, hT_lo)[r // 4], 2 + r // 2 % 2, r % 2
                if r >= 4:
                    pe.wait_ge(*sig("h_tok_read").at(r - 4))
                for k in range(4):
                    mm = nc.tensor.transpose(tmp[r % 4][:, k * P:(k + 1) * P], part[:, 4 * half + k, t * P:(t + 1) * P].bitcast(F32), ident)
                mm.then_inc(*sig("h_tok_ps").did(r))
            pe.wait_ge(sig("router_loaded").sem, 16)
            for t in range(2):
                for k in range(KD):
                    for part in (hT_hi, hT_lo):
                        mm = nc.tensor.matmul(acc[0][:, t * EXPERTS:(t + 1) * EXPERTS], part[:, k, (2 + t) * P:(3 + t) * P].bitcast(F32),
                                              router[:, k, :], start=(k == 0 and part is hT_hi), stop=(k == KD - 1 and part is hT_lo))
            mm.then_inc(*sig("logits").did())
            pe.wait_ge(*sig("chosen").at())
            m = route[:, 0]
            nc.tensor.matmul(acc[1][:, 0:EXPERTS], c_("earlier"), m[:, 0, :], start=True, stop=True)
            nc.tensor.matmul(acc[1][:, EXPERTS:2 * EXPERTS], c_("earlier"), m[:, 1, :], start=True, stop=False)
            nc.tensor.matmul(acc[1][:, EXPERTS:2 * EXPERTS], ones_sq[:, :], m[:, 0, :], start=False, stop=True)
            nc.tensor.matmul(acc[1][:, 2 * EXPERTS:3 * EXPERTS], ones_sq[:, :], m[:, 0, :], start=True, stop=False)
            nc.tensor.matmul(acc[1][:, 2 * EXPERTS:3 * EXPERTS], ones_sq[:, :], m[:, 1, :], start=False, stop=True).then_inc(*sig("ranks").did())
            pe.wait_ge(*sig("h_tok_read").at(7))
            pe.wait_ge(*sig("passes_known").at())
            phase_end(pe, "pe", "route")

            def gather(pick_at, signal):
                pe.wait_ge(*pick_at)
                for r in range(4):
                    for c in range(2):
                        k = 2 * r + c
                        for i, part in enumerate((h_tok_hi, h_tok_lo)):
                            for t in range(2):
                                o = (2 * i + c) * P
                                mm = nc.tensor.matmul(gather_banks[r][:, o:o + P], part[:, t, k * P:(k + 1) * P], pick_tok[:, t, :],
                                                      start=(t == 0), stop=(t == 1))
                    mm.then_inc(*signal.did(r))

            def scatter(item, last):
                pe.wait_ge(*(sig("y_last").at() if last else sig("e_y").turn(1, item)))
                pe.wait_ge(*sig("e_slot_pick").turn(0, item - 1))
                pe.wait_ge(*sig("e_add").turn(3, item - 1))
                for r in range(4):
                    t, n = divmod(r, 2)
                    if r == 3:
                        pe.wait_ge(*(sig("add_last").at(0) if last else sig("e_add").turn(0, item)))
                    nc.tensor.matmul(scatter_banks[r][:, :], pick_slot[:, t, :], y_sb[:, n * 512:(n + 1) * 512], start=True, stop=True)\
                        .then_inc(*(sig("scatter_last") if last else sig("e_scatter")).did(r))

            def hidden_transposes(j, item):
                pe.wait_ge(*sig("e_act").turn(j, item))
                if j >= 2:
                    pe.wait_ge(*sig("e_rest").turn(j - 2, item))
                elif j == 1:
                    pe.wait_ge(*sig("e_add").turn(3, item))
                else:
                    pe.wait_ge(*sig("e_slot_pick").turn(0, item))
                for c in range(2):
                    mm = nc.tensor.transpose(tmp[j % 2][:, c * P:(c + 1) * P], e_tok[:, j % 2, c * P:(c + 1) * P], ident)
                mm.then_inc(*sig("e_hT_ps").did(j))

            def products(q, bank, st_hi, st_lo, k0, nk, n0, first, last):
                for kk in range(nk):
                    for st, wt in ((st_hi, w_hi), (st_hi, w_lo), (st_lo, w_hi)):
                        mm = nc.tensor.matmul(bank[:, :], st[:, k0 + kk, :], e_moving(wt, q, kk, n0),
                                              start=(first and kk == 0 and wt is w_hi and st is st_hi), stop=(last and kk == nk - 1 and st is st_lo))
                return mm

            for name in ("e_used", "e_scatter", "e_hT_ps", "e_slot_ps"):
                pe.sem_inc(sig(name).sem, sig(name).each())
            gather(sig("e_pick").turn(0, 0), Prologue(sig("e_gathered")))

            def body(item, e):
                for j in range(FF_CHUNKS):
                    for kh in range(2):
                        q = 2 * j + kh
                        pe.wait_ge(*sig("e_lo").turn((q, 1), item))
                        if q == 0:
                            pe.wait_ge(*sig("e_hg_lo").turn(3, item - 1))
                        if kh == 0 and j >= 2:
                            pe.wait_ge(*sig("e_act").turn(j - 2, item))
                        products(q, acc[j % 2], hg_hi, hg_lo, 4 * kh, 4, 0, kh == 0, kh == 1).then_inc(*sig("e_used").did(q))
                    if j == 0:
                        scatter(item, False)
                        pe.wait_ge(*sig("e_rest").turn(FF_CHUNKS - 1, item - 1))
                        for t in range(2):
                            mm = nc.tensor.transpose(tmp[0][:, t * P:(t + 1) * P], pick_tok[:, t, :].bitcast(F32), ident)
                        mm.then_inc(*sig("e_slot_ps").did(0))
                    else:
                        hidden_transposes(j - 1, item)
                for d in range(DOWN_SLABS):
                    q = UP_SLABS + d
                    pe.wait_ge(*sig("e_lo").turn((q, 1), item))
                    if d == 0:
                        pe.wait_ge(*sig("e_y").turn(1, item))
                    pe.wait_ge(*sig("e_rest").turn(d, item))
                    for n in range(2):
                        mm = products(q, acc[2 + n], eT_hi, eT_lo, 2 * d, 2, n * 512, d == 0, d == DOWN_SLABS - 1)
                    mm.then_inc(*sig("e_used").did(q))
                    if d == 0:
                        hidden_transposes(FF_CHUNKS - 1, item)
                    if d == 3:
                        gather(sig("e_pick").turn(0, item), sig("e_gathered"))

            end = experts_loop(pe, body)
            scatter(end, True)

        @block.tensor
        def _(pe):
            bank_free = {}

            def project(key, slab_keys, k_firsts, stat_hi, stat_lo, tiles, cols_of, free_signal, after_slab=lambda s: None):
                for s, sk in enumerate(slab_keys):
                    i = slab_at[sk]
                    _, nk, w, _ = slabs[i]
                    hi, lo = view(w_hi, i, nk, w), view(w_lo, i, nk, w)
                    pe.wait_ge(*lo_split.at(i))
                    last_s = s == len(slab_keys) - 1
                    mm = None
                    for t in tiles:
                        a, bb = cols_of(t)
                        if s == 0 and t in bank_free:
                            pe.wait_ge(*bank_free[t])
                        for kk in range(nk):
                            k = k_firsts[s] + kk
                            for st, wt in ((stat_hi, hi), (stat_hi, lo), (stat_lo, hi)):
                                mm = nc.tensor.matmul(acc[t][:, 0:bb - a], st[:, k, t * P:(t + 1) * P], wt[:, kk, a:bb],
                                                      start=(s == 0 and kk == 0 and st is stat_hi and wt is hi),
                                                      stop=(last_s and kk == nk - 1 and st is stat_lo))
                        if last_s:
                            mm.then_inc(*sig("acc_ready").did((key, t)))
                            bank_free[t] = free_signal(t)
                    if not last_s:
                        mm.then_inc(*slab_used.did(i))
                        after_slab(s)

            def transpose_into(dst, src):
                return nc.tensor.transpose(dst, src, ident[0:src.shape[0], 0:src.shape[0]])

            pe.wait_ge(*consts_in_at())

            def mod_product(l, n, kh, bank):
                i = slab_at[("mod", l, n, kh)]
                if kh == 0 and mod_before(l, n):
                    pe.wait_ge(*sig("mod_row").at(mod_before(l, n)))
                if mod_split(l, n):
                    pe.wait_ge(*lo_split.at(i))
                    for kk in range(4):
                        for part in (w_hi, w_lo):
                            mm = nc.tensor.matmul(bank[0:4, :], cond4[:, 4 * kh + kk, :], view(part, i, 4, 512)[:, kk, :],
                                                  start=(kh == 0 and kk == 0 and part is w_hi), stop=(kh == 1 and kk == 3 and part is w_lo))
                else:
                    pe.wait_ge(*loaded[i % RING].at(i))
                    for kk in range(4):
                        mm = nc.tensor.matmul(bank[0:2, :], cond_act[:, 4 * kh + kk, :], view(raw, i, 4, 512)[:, kk, :],
                                              start=(kh == 0 and kk == 0), stop=(kh == 1 and kk == 3))
                mm.then_inc(*slab_used.did(i))

            def mod_columns(l, n, bank):
                pe.wait_ge(*sig("mod_row").at((l, n)))
                if mod_before(l, n):
                    pe.wait_ge(*sig("mod_cols").at(mod_before(l, n)))
                m = 4 if mod_split(l, n) else 2
                for k in range(4):
                    mm = nc.tensor.matmul(bank[:, 2 * k:2 * k + 2], mod_row[0:m, k * P:(k + 1) * P], c_("pick")[0:m, :], start=True, stop=True)
                mm.then_inc(*sig("mod_cols_ps").did((l, n)))

            for l in range(DEPTH):
                act_t = active(l)
                if l == 0:
                    pe.wait_ge(*sig("cond_act").at())
                    for n in range(MOD_FIRST):
                        mod_product(0, n, 0, tmp[0])
                        if n:
                            mod_columns(0, n - 1, tmp[1])
                        mod_product(0, n, 1, tmp[0])
                    mod_columns(0, MOD_FIRST - 1, tmp[1])
                    pe.wait_ge(*sig("mod_cols").at((0, MOD_FIRST - 1)))
                    phase_end(pe, "pe", "mod")

                def norm_transposes(which, tiles):
                    for k in range(KD):
                        if k == 0:
                            pe.wait_ge(*sig("xn_ready").at((l, which)))
                        if k >= 4:
                            pe.wait_ge(*modulated(l, which, k - 4))
                        for t in tiles:
                            mm = transpose_into(tmp[k % 4][:, t * P:(t + 1) * P], xn[:, t, k * P:(k + 1) * P])
                        mm.then_inc(*sig("xT").did((l, which, k)))

                norm_transposes(0, range(TILES))
                pe.wait_ge(*sig("h_lo").at((l, 0, KD - 1)))
                phase_end(pe, "pe", "norm0")
                bank_free.clear()
                for c in range(len(IN_CHUNKS)):
                    tiles = [t for t in range(TILES) if in_cols(l, c, t)]
                    c0 = IN_CHUNKS[c][0]

                    def cols_of(t, c=c, c0=c0):
                        a, bb = in_cols(l, c, t)
                        return a - c0, bb - c0
                    project(("in", l, c), [("in", l, c, kh) for kh in range(2)], [0, 4], hT_hi, hT_lo, tiles, cols_of,
                            lambda t, c=c: sig("in_read_act" if t < 2 else "in_read_dve").at((l, c, t)))
                pe.wait_ge(*sig("in_read_act").at(("all", l)))
                pe.wait_ge(*sig("in_read_dve").at(("all", l)))
                phase_end(pe, "pe", "in")

                def da_transposes(h):
                    if h:
                        pe.wait_ge(*sig("daT_read_act").at((l, h - 1)))
                    for t in act_t:
                        mm = transpose_into(tmp[0][:, t * P:(t + 1) * P], pj[:, t, C_DQ + h * P:C_DQ + (h + 1) * P])
                    mm.then_inc(*sig("daqT_ps").did((l, h)))
                    if h:
                        pe.wait_ge(*sig("daT_read_dve").at((l, h - 1)))
                    for t in range(TILES):
                        mm = transpose_into(tmp[1][:, t * P:(t + 1) * P], pj[:, t, C_DK + h * P:C_DK + (h + 1) * P])
                    mm.then_inc(*sig("dakT_ps").did((l, h)))

                def compressed_transposes(t):
                    if t:
                        pe.wait_ge(*sig("cT").at((l, t - 1)))
                    for i in range(0 if t in act_t else 2, 3):
                        mm = transpose_into(tmp[2][:, i * P:(i + 1) * P], c_tok[:, t, i * P:(i + 1) * P])
                    mm.then_inc(*sig("cT_ps").did((l, t)))

                def expand(t):
                    pe.wait_ge(*sig("cT").at((l, t)))
                    if t in act_t:
                        if t - 1 in act_t:
                            pe.wait_ge(*sig("q_tok").at((l, t - 1)))
                        for i in range(2):
                            mm = nc.tensor.matmul(acc[0][:, 0:MLA_HEADS * MLA_QK], cT[:, t % 2, i, :], w_uq[:, i, :],
                                                  start=(i == 0), stop=(i == 1))
                        mm.then_inc(*sig("mq_ps").did((l, t)))
                    if t:
                        pe.wait_ge(*sig("kv_tok").at((l, t - 1)))
                        pe.wait_ge(*sig("mk_roped").at((l, t - 1)))
                    nc.tensor.matmul(acc[1][:, :], cT[:, t % 2, 2, :], w_ukv[:, :], start=True, stop=True).then_inc(*sig("mkv_ps").did((l, t)))

                def mla_transposes(t):
                    if t in act_t:
                        pe.wait_ge(*sig("mq_roped" if t >= 2 else "q_tok").at((l, t)))
                        if t - 1 in act_t:
                            pe.wait_ge(*sig("mqT_read").at((l, t - 1)))
                        for h in range(MLA_HEADS):
                            mm = transpose_into(acc[2][0:MLA_QK, h * P:(h + 1) * P], q_tok[:, t % 2, h, :])
                        mm.then_inc(*sig("mqT_ps").did((l, t)))
                    pe.wait_ge(*sig("mk_roped").at((l, t)))
                    if t:
                        pe.wait_ge(*sig("mkT_read").at((l, t - 1)))
                    for h in range(MLA_HEADS):
                        mm = transpose_into(acc[3][0:MLA_QK, h * P:(h + 1) * P], k_tok[:, t % 2, h, :])
                    mm.then_inc(*sig("mkT_ps").did((l, t)))

                pe.wait_ge(mlaw_in.sem, 32 * (l + 1))
                for s in range(TILES + 2):
                    if s < TILES:
                        compressed_transposes(s)
                        da_transposes(s)
                    if 1 <= s <= TILES:
                        expand(s - 1)
                    if s >= 2:
                        mla_transposes(s - 2)
                pe.wait_ge(*sig("mkT_read").at((l, TILES - 1)))
                pe.wait_ge(*sig("daT_read_act").at((l, DA_HEADS - 1)))
                pe.wait_ge(*sig("daT_read_dve").at((l, DA_HEADS - 1)))
                phase_end(pe, "pe", "attn_prep")

                us = units(l)

                def scores(u):
                    kind, t, h = us[u]
                    keys = TOK if t >= 2 else CTX
                    if u >= 2:
                        pe.wait_ge(*sig("exp").at((l, u - 2)))
                    for g in range(2 if kind == "da" else 1):
                        bank = tmp[2 * (u % 2) + g]
                        if kind == "da":
                            mm = nc.tensor.matmul(bank[:, 0:keys], daqT[64 * g:64 * g + 64, h, t * P:(t + 1) * P],
                                                  dakT[64 * g:64 * g + 64, h, 0:keys], start=True, stop=True)
                        else:
                            mm = nc.tensor.matmul(bank[:, 0:keys], mqT[:, h, t * P:(t + 1) * P], mkT[:, h, 0:keys],
                                                  start=True, stop=True)
                    mm.then_inc(*sig("scores").did((l, u)))

                def probs_transposes(u):
                    kind, t, h = us[u]
                    nk = (TOK if t >= 2 else CTX) // P
                    pe.wait_ge(*sig("probs" if kind == "da" else "exp").at((l, u)))
                    if u >= 2:
                        pe.wait_ge(*sig("probsT").at((l, u - 2)))
                    for s in range(nk):
                        mm = transpose_into(acc[u % 2][:, s * P:(s + 1) * P], probs[:, u % 2, 0, s * P:(s + 1) * P])
                    mm.then_inc(*sig("probsT_ps").did((l, u)))

                def values(u):
                    kind, t, h = us[u]
                    nk = (TOK if t >= 2 else CTX) // P
                    pe.wait_ge(*sig("probsT").at((l, u)))
                    if u >= 2:
                        pe.wait_ge(*sig("attended").at((l, u - 2)))
                    for s in range(nk):
                        v = pj[:, s, C_DV + h * P:C_DV + (h + 1) * P] if kind == "da" else pj[:, s, C_CQ + h * MLA_V:C_CQ + (h + 1) * MLA_V]
                        mm = nc.tensor.matmul(acc[2 + u % 2][:, 0:v.shape[1]], probsT[:, u % 2, s, :], v,
                                              start=(s == 0), stop=(s == nk - 1))
                    mm.then_inc(*sig("o_ps").did((l, u)))

                for u in range(len(us) + 2):
                    if u < len(us):
                        scores(u)
                    if u >= 2:
                        values(u - 2)
                    if 1 <= u <= len(us):
                        probs_transposes(u - 1)
                    if l == 0 and BESIDE_UNIT <= u < len(us):
                        n, kh = divmod(u - BESIDE_UNIT + 2 * MOD_FIRST, 2)
                        if kh and n > MOD_FIRST:
                            mod_columns(0, n - 1, tmp[3])
                        mod_product(0, n, kh, tmp[1])
                if l == 0:
                    mod_columns(0, MOD_CHUNKS - 1, tmp[3])
                pe.wait_ge(*sig("attended").at((l, len(us) - 1)))
                phase_end(pe, "pe", "attn")

                for i in range(6):
                    if i >= 4:
                        pe.wait_ge(*sig("gate_sig").at((l, i - 4)))
                    for t in (range(TILES) if i < 4 else act_t):
                        col = (C_FF + i * P) if i < 4 else (C_HQ + (i - 4) * P)
                        mm = transpose_into(tmp[i % 4][:, t * P:(t + 1) * P], pj[:, t, col:col + P])
                    mm.then_inc(*sig("gT_ps").did((l, i)))
                if l == 0:
                    for k in range(AHEAD_OF_LEVELS):
                        if k % 2 and k > 1:
                            mod_columns(1, k // 2 - 1, acc[3])
                        mod_product(1, k // 2, k % 2, acc[2])
                for p in range(2):
                    for n, m in enumerate(level_list()):
                        i = p * len(level_list()) + n
                        buf = n % 2
                        pe.wait_ge(*sig("level").at((l, p, n)))
                        if i == 0:
                            pe.wait_ge(*sig("gate_sig").at((l, 5)))
                        for b in level_banks(l, m):
                            bank = level_bank(i, b)
                            before = [i - k for k in range(2, i + 1, 2) if b in level_banks(l, level_steps()[i - k][2])]
                            if before:
                                pe.wait_ge(*level_read(l, before[0], b))
                            if m == 0:
                                r = slice(64 * b, 64 * b + 64)
                                for t in act_t:
                                    mm = nc.tensor.matmul(bank[:, t * P:(t + 1) * P], lev_k[r, buf, 0, t * P:(t + 1) * P],
                                                          hqT[r, p, t * P:(t + 1) * P], start=True, stop=True)
                            elif m <= 64:
                                for tt_ in range(2):
                                    t = 2 * b + tt_
                                    o = bank[:, tt_ * 2 * P:(tt_ + 1) * 2 * P].rearrange("s (h b e m) -> s h b e m", h=2, e=2, m=m)
                                    q0 = (t - act_t[0]) * 64
                                    for d in range(2):
                                        q = lev_q[:, buf, d, :, q0:q0 + 64].rearrange("d h (b m) -> d h b m", m=m)
                                        mm = nc.tensor.matmul(o[:, :, :, 1 - d, :], lev_k[:, buf, d, t * P:(t + 1) * P], q,
                                                              start=True, stop=True)
                            elif m == 128:
                                q0 = (b - act_t[0] // 2) * P
                                for d in range(2):
                                    s0 = (2 * b + d) * P
                                    mm = nc.tensor.matmul(bank[:, d * SEQ:(d + 1) * SEQ], lev_k[:, buf, d, s0:s0 + P],
                                                          lev_q[:, buf, d, :, q0:q0 + P], start=True, stop=True)
                            else:
                                for d in range(2):
                                    mm = nc.tensor.matmul(bank[:, :], lev_k[:, buf, d, b * P:(b + 1) * P],
                                                          lev_q[:, buf, d, :, :], start=(d == 0), stop=(d == 1))
                            mm.then_inc(*sig("s_ps").did((l, i, b)))
                        if l == 0:
                            c, kh = divmod(AHEAD_OF_LEVELS + i, 2)
                            if kh:
                                mod_columns(1, c - 1, acc[3])
                            mod_product(1, c, kh, acc[2])
                    pe.wait_ge(*sig("s_read_act").at((l, p)))
                    pe.wait_ge(*sig("s_read").at((l, len(level_list()) * p + level_list().index(64), 1)))
                    for t in act_t:
                        for hh in range(2):
                            h = 2 * p + hh
                            sg, a = t // 2, t % 2
                            terms = [(t, s_diag[:, hh, t, :]), (2 * sg + 1 - a, s_off[:, hh, sg, 1 - a, :])]
                            if sg:
                                terms += [(s, s_far[:, hh, s, a * P:(a + 1) * P]) for s in range(2)]
                            for q, (s, st) in enumerate(terms):
                                mm = nc.tensor.matmul(hg_out(t)[:, h * 64:(h + 1) * 64], st, pj[:, s, C_HI + h * 64:C_HI + (h + 1) * 64],
                                                      start=(q == 0), stop=(q == len(terms) - 1))
                    mm.then_inc(*sig("hg_o").did((l, p)))
                if l == 0:
                    mod_columns(1, MOD_CHUNKS - 1, acc[3])
                phase_end(pe, "pe", "hg")

                def gates(i):
                    for q in range(4):
                        j, n = divmod(q, 2)
                        if q >= 2:
                            pe.wait_ge(*sig("gate_all").at((l, i, q - 2)))
                        for k in range(4):
                            g = mod_cols[:, l, 3 * i + 2, 4 * n + k, j:j + 1].broadcast_to([P, P])
                            mm = nc.tensor.matmul((tmp if i else acc)[2 + q % 2][:, k * P:(k + 1) * P], g, ident, start=True, stop=True)
                        mm.then_inc(*sig("gate_ps").did((l, i, q)))

                for k in range(KD):
                    if k == 768 // P:
                        gates(0)
                        pe.wait_ge(*sig("mixed").at((l, 3)))
                    if k >= 4:
                        pe.wait_ge(*sig("oT_lo").at((l, k - 4)))
                    for t in act_t:
                        mm = transpose_into(tmp[k % 4][:, t * P:(t + 1) * P], pj[:, t, k * P:(k + 1) * P])
                    mm.then_inc(*sig("oT_ps").did((l, k)))
                pe.wait_ge(*sig("oT_lo").at((l, KD - 1)))
                pe.wait_ge(*sig("gate_all").at((l, 0, 3)))

                bank_free.clear()
                for n in range(2):
                    project(("out", l, n), [("out", l, n, kh) for kh in range(2)], [0, 4], hT_hi, hT_lo, act_t,
                            lambda t: (0, 512), lambda t, n=n: sig("acc_added").at((l, "out", n, t)))
                pe.wait_ge(*sig("acc_added").at((l, "out", 1, 3)))
                gates(1)
                pe.wait_ge(*sig("gate_all").at((l, 1, 3)))
                phase_end(pe, "pe", "out")
                norm_transposes(1, act_t)
                pe.wait_ge(*sig("h_lo").at((l, 1, KD - 1)))
                phase_end(pe, "pe", "norm1")
                if l % 2 == 0:
                    bank_free.clear()

                    def hidden_transposes(g, j):
                        j0 = FF_GROUPS[g][0]
                        pe.wait_ge(*sig("act_tok").at((l, j, TILES - 1)))
                        for c in range(2):
                            bank = tmp[(2 * j + c) % 3]
                            if 2 * j + c >= 3:
                                pe.wait_ge(*sig("aT_lo").at((l, 2 * j + c - 3)))
                            for t in range(TILES):
                                mm = transpose_into(bank[:, t * P:(t + 1) * P], act_tok[:, t, c * P:(c + 1) * P])
                            mm.then_inc(*sig("aT_ps").did((l, 2 * j + c)))

                    for g, (j0, j1) in enumerate(FF_GROUPS):
                        for j in range(j0, j1):
                            project(("gu", l, j), [("gu", l, j, kh) for kh in range(2)], [0, 4], hT_hi, hT_lo, range(TILES),
                                    lambda t: (0, 512), lambda t, j=j: sig("act_tok").at((l, j, t)),
                                    lambda s, j=j, g=g: hidden_transposes(g, j - 1) if j > FF_GROUPS[g][0] else None)

                        def last_hidden(s, n, g=g, last=j1 - 1, before_last=(2 * (j1 - j0) - 1) // 4 - 1):
                            if n == 0 and s == 0:
                                hidden_transposes(g, last)
                            if n == 0 and s == before_last:
                                pe.wait_ge(*sig("aT_lo").at((l, 2 * last + 1)))

                        pe.wait_ge(*sig("aT_lo").at((l, 2 * j1 - 3)))
                        nk = 2 * (j1 - j0)
                        for n in range(2):
                            ss = list(range(0, nk, 4))
                            project(("down", l, g, n), [("down", l, g, n, s) for s in ss], ss, aT_hi, aT_lo, range(TILES),
                                    lambda t: (0, 512), lambda t, g=g, n=n: sig("acc_added").at((l, "down", g, n, t)),
                                    lambda s, n=n: last_hidden(s, n))
                    pe.wait_ge(*sig("acc_added").at((l, "down", len(FF_GROUPS) - 1, 1, TILES - 1)))
                    phase_end(pe, "pe", "ffn")
                else:
                    experts_pe(pe)

        @block.gpsimd
        def _(pool):
            def sub(o, a, b):
                return nc.gpsimd.tensor_tensor(o, a, b, ALU.subtract)

            for l in range(DEPTH):
                S0 = active(l)[0] * P
                T = TOK - S0
                pool.wait_ge(phase.sem, ENGINES * known.get("phases", {}).get(("attn", l), 1))
                nc.gpsimd.memset(lev_q[:, 0], 0.0)
                nc.gpsimd.memset(lev_q[:, 1], 0.0)
                nc.gpsimd.memset(lev_k[:, :, :, :], 0.0).then_inc(*sig("lev_clear").did(l))
                pool.wait_ge(*sig("cum").at((l, 3)))
                for i, (p, n, m) in enumerate(level_steps()):
                    if m == 0:
                        continue
                    if i >= DECAYS:
                        pool.wait_ge(*sig("level").at((l, *level_steps()[i - DECAYS][:2])))
                    d = dec[:, i % DECAYS]
                    if m <= 128:
                        cf, cb = [cum[:, g, S0:].rearrange("p (b e m) -> p b e m", e=2, m=m) for g in (p, 2 + p)]
                        nb = T // (2 * m)
                        rf = cf[:, :, 0, m - 1:m].broadcast_to([P, nb, m])
                        rb = cb[:, :, 1, 0:1].broadcast_to([P, nb, m])
                        dv = [d[:, q, 0:T // 2].rearrange("p (b m) -> p b m", m=m) for q in range(4)]
                        sub(dv[0], cf[:, :, 1], rf)
                        sub(dv[1], rf, cf[:, :, 0])
                        sub(dv[2], cb[:, :, 0], rb)
                        ins = sub(dv[3], rb, cb[:, :, 1])
                    else:
                        cf, cb = cum[:, p, :], cum[:, 2 + p, :]
                        nc.gpsimd.tensor_copy(d[:, 0, :], cf[:, CTX:])
                        sub(d[:, 1, :], cf[:, CTX - 1:CTX].broadcast_to([P, CTX]), cf[:, 0:CTX])
                        nc.gpsimd.tensor_copy(d[:, 2, :], cb[:, CTX:])
                        ins = sub(d[:, 3, :], cb[:, 0:1].broadcast_to([P, CTX]), cb[:, 0:CTX])
                    ins.then_inc(*sig("dec").did((l, p, n)))

        def experts_act(act):
            act.wait_ge(*hi_split.at(len(slabs) - 1))
            act.sem_inc(sig("e_hi").sem, sig("e_hi").each())
            for r in range(4):
                act.wait_ge(*sig("h_tok_ps").at(r))
                nc.scalar.activation(h_tok_hi[:, r // 2, (r % 2) * 512:(r % 2 + 1) * 512], tmp[r][:, :], ACT.Copy).then_inc(*sig("h_tok_read").did(r))
            act.wait_ge(*sig("logit_gap").at())
            nc.scalar.activation(route1[:, 5], route1[:, 4], ACT.Exp).then_inc(*sig("gap_exp").did())
            act.wait_ge(*sig("passes_known").at())
            phase_end(act, "act", "route")
            for name in ("e_silu", "e_high", "e_y"):
                act.sem_inc(sig(name).sem, sig(name).each())
            act.wait_ge(*sig("y_cleared").at())
            act.sem_inc(sig("e_slot_pick").sem, 1)

            def gathered(at, signal):
                for r in range(4):
                    act.wait_ge(*at(r))
                    nc.scalar.activation(hg_hi[:, 2 * r:2 * r + 2, :], gather_banks[r][:, 0:2 * P].rearrange("p (c s) -> p c s", c=2), ACT.Copy).then_inc(*signal.did(r))

            gathered(lambda r: sig("e_gathered").turn(r, 0), Prologue(sig("e_hg_hi")))

            def body(item, e):
                n = [0]

                def high(to):
                    while n[0] <= to:
                        q = n[0]
                        back, turn = (q - RING, item) if q >= RING else (q - RING + E_SLABS, item - 1)
                        act.wait_ge(*sig("e_used").turn(back, turn))
                        for half in range(2):
                            act.wait_ge(*e_loaded_at(q, half, item))
                            nc.scalar.activation(e_half(w_hi, q, half), e_half(raw, q, half), ACT.Copy).then_inc(*sig("e_hi").did((q, half)))
                        n[0] += 1

                def hidden_high(j):
                    act.wait_ge(*sig("e_hT_ps").turn(j, item))
                    nc.scalar.activation(eT_hi[:, 2 * j:2 * j + 2, :], tmp[j % 2][:, 0:2 * P].rearrange("p (c s) -> p c s", c=2), ACT.Copy).then_inc(*sig("e_high").did(j))

                high(2)
                act.wait_ge(*sig("e_used").turn(E_SLABS - 1, item - 1))
                act.wait_ge(*sig("e_scatter").turn(3, item - 1))
                for h in range(2):
                    nc.scalar.activation(y_sb[:, h * 512:(h + 1) * 512], acc[2 + h][:, :], ACT.Copy).then_inc(*sig("e_y").did(h))
                for j in range(FF_CHUNKS):
                    high(2 * j + 3)
                    act.wait_ge(*sig("e_used").turn(2 * j + 1, item))
                    act.wait_ge(*(sig("e_act").turn(j - 2, item) if j >= 2 else sig("e_act").turn(j - 2 + FF_CHUNKS, item - 1)))
                    nc.scalar.activation(e_gate[:, j % 2, :], acc[j % 2][:, 0:GU], ACT.Silu).then_inc(*sig("e_silu").did(j))
                    if j:
                        hidden_high(j - 1)
                    else:
                        act.wait_ge(*sig("e_slot_ps").turn(0, item))
                        nc.scalar.activation(pick_slot[:, :, :], tmp[0][:, 0:2 * P].rearrange("p (t n) -> p t n", t=2), ACT.Copy).then_inc(*sig("e_slot_pick").did(0))
                high(UP_SLABS + 3)
                hidden_high(FF_CHUNKS - 1)
                high(UP_SLABS + 6)
                gathered(lambda r: sig("e_gathered").turn(r, item), sig("e_hg_hi"))
                high(E_SLABS - 1)

            end = experts_loop(act, body)
            act.wait_ge(*sig("e_used").turn(E_SLABS - 1, end - 1))
            act.wait_ge(*sig("e_scatter").turn(3, end - 1))
            for h in range(2):
                ins = nc.scalar.activation(y_sb[:, h * 512:(h + 1) * 512], acc[2 + h][:, :], ACT.Copy)
            ins.then_inc(*sig("y_last").did())
            for t in range(2):
                act.wait_ge(*sig("x_last").at(t))
                if t:
                    act.wait_ge(*sig("final_sq").at(0))
                nc.scalar.activation(squares[:, :], x[:, 2 + t, :], ACT.Square, accum_out=small[:, t:t + 1]).then_inc(*sig("final_sq").did(t))
            act.wait_ge(*sig("final_mean").at())
            nc.scalar.activation(small[:, 4:6], small[:, 2:4], ACT.Sqrt).then_inc(*sig("final_root").did())

        @block.scalar
        def _(act):
            split = Splitter(act, "hi")

            def squares_of_x(l, which, t):
                if t != (active(l)[0] if which else 0):
                    act.wait_ge(*sig("sq").at((l, which, t - 1)))
                nc.scalar.activation(act_tok[:, :, :].rearrange("p t n -> p (t n)"), x[:, t, :], ACT.Square, accum_out=small[:, t:t + 1]).then_inc(*sig("sq").did((l, which, t)))

            def norm_roots(l, which, tiles):
                act.wait_ge(*sig("mean").at((l, which)))
                a, bb = tiles[0], tiles[-1] + 1
                nc.scalar.activation(small[:, 8 + a:8 + bb], small[:, 4 + a:4 + bb], ACT.Sqrt).then_inc(*sig("root").did((l, which)))

            def norm_high(l, which, tiles):
                a, bb = tiles[0], tiles[-1] + 1
                for k in range(KD + 1):
                    if k % 2:
                        act.wait_ge(*sig("xT").at((l, which, k)))
                        if k >= HF:
                            act.wait_ge(*sig("h_lo").at((l, which, k - HF)))
                        for sg in sorted({t // 2 for t in tiles}, reverse=True):
                            j = 1 - sg
                            ins = nc.scalar.activation(hf[:, k % HF, sg * SEQ:(sg + 1) * SEQ], tmp[k % 4][:, sg * SEQ:(sg + 1) * SEQ], ACT.Identity,
                                                       scale=scale_col[:, k, j:j + 1], bias=mod_cols[:, l, 3 * which, k, j:j + 1])
                        ins.then_inc(*sig("modulated_by_act").did((l, which, k)))
                    if k:
                        act.wait_ge(*modulated(l, which, k - 1))
                        nc.scalar.activation(hT_hi[:, k - 1, a * P:bb * P], hf[:, (k - 1) % HF, a * P:bb * P], ACT.Copy).then_inc(*sig("h_hi").did((l, which, k - 1)))

            def mod_row_copy(l, n, bank):
                act.wait_ge(*slab_used.at(slab_at[("mod", l, n, 1)]))
                if mod_before(l, n):
                    act.wait_ge(*sig("mod_cols_ps").at(mod_before(l, n)))
                m = 4 if mod_split(l, n) else 2
                nc.scalar.activation(mod_row[0:m, :], bank[0:m, :], ACT.Copy).then_inc(*sig("mod_row").did((l, n)))

            act.wait_ge(vec_in.sem, 32)
            for l in range(DEPTH):
                act_t = active(l)
                if l == 0:
                    nc.scalar.activation(cond_act[:, :, :], cond_in[:, :].rearrange("p (k j) -> p k j", j=2), ACT.Silu).then_inc(*sig("cond_act").did())
                    act.wait_ge(*sig("cond_act").at())
                    nc.scalar.activation(cond4[:, :, 0:2], cond_act[:, :, :], ACT.Copy).then_inc(*sig("cond_hi").did())
                    mod_row_copy(0, 0, tmp[0])
                    act.wait_ge(x_in.sem, 64)
                    for t in range(TILES):
                        squares_of_x(0, 0, t)
                    mod_row_copy(0, 1, tmp[0])
                    norm_roots(0, 0, range(TILES))
                    for n in range(2, MOD_FIRST):
                        mod_row_copy(0, n, tmp[0])
                    split.up_to(slab_at[("in", 0, 0, 0)] + RING - 1)
                    act.wait_ge(*sig("lam_sums").at())
                    nc.scalar.activation(lam[:, :, 2:4], lam[:, :, 0:2], ACT.Exp).then_inc(*sig("lam_exp").did())
                    act.wait_ge(*sig("lb_diff").at())
                    nc.scalar.activation(lb[:, 1, :], small[:, 32:36], ACT.Sigmoid).then_inc(*sig("lb").did())
                    act.wait_ge(*sig("lb").at())
                    phase_end(act, "act", "mod")
                norm_high(l, 0, range(TILES))
                act.wait_ge(*sig("h_lo").at((l, 0, KD - 1)))
                phase_end(act, "act", "norm0")
                b0 = slab_at[("in", l, 0, 0)]
                for c in range(len(IN_CHUNKS)):
                    split.up_to(b0 + 2 * c + 3)
                    for t in (0, 1):
                        if in_cols(l, c, t):
                            a, bb = in_cols(l, c, t)
                            act.wait_ge(*sig("acc_ready").at((("in", l, c), t)))
                            nc.scalar.activation(pj[:, t, a:bb], acc[t][:, 0:bb - a], ACT.Copy).then_inc(*sig("in_read_act").did((l, c, t)))
                            sig("in_read_act").seen[("all", l)] = sig("in_read_act").count
                    if c == 4:
                        for t in range(TILES):
                            act.wait_ge(*sig("in_read_act" if t < 2 else "in_read_dve").at((l, 3, t)))
                            if t in act_t:
                                nc.scalar.activation(c_tok[:, t, 0:MLA_Q], pj[:, t, C_CQ:C_CKV], ACT.Square, accum_out=stats[:, t:t + 1])
                            ins = nc.scalar.activation(c_tok[:, t, MLA_Q:], pj[:, t, C_CKV:C_KR], ACT.Square, accum_out=stats[:, 4 + t:5 + t])
                        ins.then_inc(*sig("c_sq").did(l))
                    if c == 5:
                        act.wait_ge(*sig("c_mean").at(l))
                        nc.scalar.activation(stats[:, 16 + act_t[0]:24], stats[:, 8 + act_t[0]:16], ACT.Sqrt).then_inc(*sig("c_root").did(l))
                split.up_to(slab_at[("out", l, 0, 0) if l else ("mod", 0, MOD_FIRST, 0)] + RING - 1)
                act.wait_ge(*sig("in_read_act").at(("all", l)))
                phase_end(act, "act", "in")

                a0 = act_t[0] * P
                for s in range(TILES + 2):
                    if s < TILES:
                        act.wait_ge(*sig("cT_ps").at((l, s)))
                        if s >= 2:
                            act.wait_ge(*sig("mkv_ps").at((l, s - 2)))
                        for i in range(0 if s in act_t else 2, 3):
                            g = vecs[:, l, VEC["q_norm"] + i:VEC["q_norm"] + i + 1]
                            ins = nc.scalar.activation(cT[:, s % 2, i, :], tmp[2][:, i * P:(i + 1) * P], ACT.Copy, scale=g)
                        ins.then_inc(*sig("cT").did((l, s)))
                        act.wait_ge(*sig("daqT_ps").at((l, s)))
                        nc.scalar.activation(daqT[:, s, a0:], tmp[0][:, a0:], ACT.Copy).then_inc(*sig("daT_read_act").did((l, s)))
                    if s - 1 in act_t:
                        t = s - 1
                        act.wait_ge(*sig("mq_ps").at((l, t)))
                        if t - 2 in act_t:
                            act.wait_ge(*sig("mqT_ps").at((l, t - 2)))
                        nc.scalar.activation(q_tok[:, t % 2, :, :], acc[0][:, 0:MLA_HEADS * MLA_QK].rearrange("p (h d) -> p h d", h=MLA_HEADS), ACT.Copy).then_inc(*sig("q_tok").did((l, t)))
                    if s - 2 in act_t:
                        t = s - 2
                        act.wait_ge(*sig("mqT_ps").at((l, t)))
                        nc.scalar.activation(mqT[:, :, t * P:(t + 1) * P], acc[2][0:MLA_QK, :].rearrange("p (h d) -> p h d", h=MLA_HEADS), ACT.Copy).then_inc(*sig("mqT_read").did((l, t)))
                act.wait_ge(*sig("mqT_read").last())
                phase_end(act, "act", "attn_prep")

                us = units(l)
                for u in range(len(us) + 1):
                    if l == 0 and u >= BESIDE_UNIT:
                        n, kh = divmod(u - BESIDE_UNIT + 2 * MOD_FIRST, 2)
                        if kh == 0 and n > MOD_FIRST:
                            mod_row_copy(0, n - 1, tmp[1])
                    if u < len(us):
                        kind, t, h = us[u]
                        keys = TOK if t >= 2 else CTX
                        sc = (DA_DIM if kind == "da" else MLA_QK) ** -0.5
                        act.wait_ge(*sig("neg_max").at((l, u)))
                        if u >= 2:
                            act.wait_ge(*sig("probsT_ps").at((l, u - 2)))
                        ng = 2 if kind == "da" else 1
                        for g in range(ng):
                            o = 8 * (u % 2) + g
                            ins = nc.scalar.activation(probs[:, u % 2, g, 0:keys], tmp[2 * (u % 2) + g][:, 0:keys], ACT.Exp,
                                                       bias=stats[:, 32 + o:33 + o], scale=sc, accum_out=stats[:, 34 + o:35 + o])
                            if g == ng - 1:
                                ins.then_inc(*sig("exp").did((l, u)))
                    if u:
                        kind, t, h = us[u - 1]
                        nk = (TOK if t >= 2 else CTX) // P
                        act.wait_ge(*sig("probsT_ps").at((l, u - 1)))
                        if u >= 3:
                            act.wait_ge(*sig("o_ps").at((l, u - 3)))
                        nc.scalar.activation(probsT[:, (u - 1) % 2, 0:nk, :], acc[(u - 1) % 2][:, 0:nk * P].rearrange("p (s q) -> p s q", s=nk), ACT.Copy).then_inc(*sig("probsT").did((l, u - 1)))
                    if l == 0 and u >= BESIDE_UNIT:
                        split.up_to(slab_at[("mod", 0, MOD_FIRST, 0)] + u - BESIDE_UNIT + 2)
                act.wait_ge(*sig("probsT").at((l, len(us) - 1)))
                phase_end(act, "act", "attn")

                for i in range(6):
                    act.wait_ge(*sig("gT_ps").at((l, i)))
                    if i < 4:
                        nc.scalar.activation(sig_f[:, i, :], tmp[i][:, :], ACT.Sigmoid).then_inc(*sig("sig_plus").did((l, i)))
                        nc.scalar.activation(hkT[:, i, :], tmp[i][:, :], ACT.Sigmoid, scale=-1.0).then_inc(*sig("gate_sig").did((l, i)))
                    else:
                        nc.scalar.activation(hqT[:, i - 4, a0:], tmp[i % 4][:, a0:], ACT.Copy, scale=HG_DIM ** -0.5).then_inc(*sig("gate_sig").did((l, i)))
                for i in range(4):
                    act.wait_ge(*sig("sig_plus").at((l, i)))
                    nc.scalar.activation(sig_f[:, i, :], sig_f[:, i, :], ACT.Ln, bias=lb[:, l, i:i + 1], scale=one_less_lb[:, l, i:i + 1]).then_inc(*sig("logf").did((l, i)))
                steps = level_steps()
                if l == 0:
                    mod_row_copy(1, 0, acc[2])
                for i in range(len(steps) + 1):
                    if i < len(steps) and steps[i][2]:
                        p, n, m = steps[i]
                        act.wait_ge(*sig("dec").at((l, p, n)))
                        w = SEQ if (m == 256 or l < DEPTH - 1) else SEQ // 2
                        nc.scalar.activation(dec[:, i % DECAYS, :, 0:w], dec[:, i % DECAYS, :, 0:w], ACT.Exp).then_inc(*sig("dec_exp").did((l, p, n)))
                    if i and steps[i - 1][2] >= 128:
                        p, n, m = steps[i - 1]
                        for b in level_banks(l, m):
                            act.wait_ge(*sig("s_ps").at((l, i - 1, b)))
                            if p and m == 128:
                                act.wait_ge(*sig("hg_o").at((l, 0)))
                            src = level_bank(i - 1, b)
                            if m == 128:
                                ins = nc.scalar.activation(s_off[:, :, b, :, :], src[:, :].rearrange("p (d h q) -> p h d q", d=2, q=P), ACT.Copy)
                            else:
                                ins = nc.scalar.activation(s_far[:, :, b, :], src[:, :].rearrange("p (h q) -> p h q", h=2), ACT.Copy)
                            ins.then_inc(*sig("s_read_act").did((l, i - 1, b)))
                            sig("s_read_act").seen[(l, p)] = sig("s_read_act").count
                    if l == 0:
                        c, kh = divmod(AHEAD_OF_LEVELS + i, 2)
                        if kh == 0:
                            mod_row_copy(1, c - 1, acc[2])
                    if 0 <= i - SQUARES_AT < len(act_t) // 2:
                        tp = act_t[0] // 2 + i - SQUARES_AT
                        if i > SQUARES_AT:
                            act.wait_ge(*sig("da_sum").at((l, tp - 1)))
                        nc.scalar.activation(squared[:, :, :], pj[:, 2 * tp:2 * tp + 2, 0:512], ACT.Square).then_inc(*sig("da_sq").did((l, tp)))
                    if i == ROOTS_AT:
                        act.wait_ge(*sig("da_mean").at(l))
                        nc.scalar.activation(stats[:, 32:48], stats[:, 16:32], ACT.Sqrt).then_inc(*sig("da_root").did(l))
                        g = pj[:, act_t[0]:, C_HG:C_HG + 256]
                        nc.scalar.activation(g, g, ACT.Silu).then_inc(*sig("hg_silu").did(l))
                if l == 0:
                    split.up_to(slab_at[("out", l, 0, 0)] + RING - 1)
                phase_end(act, "act", "hg")
                act.wait_ge(*sig("hg_o").at((l, 1)))
                for tp in range(act_t[0] // 2, 2):
                    nc.scalar.activation(squared[:, tp, :], acc[tp][:, :], ACT.Square).then_inc(*sig("hg_sq").did((l, tp)))
                def gates(i):
                    for q in range(4):
                        act.wait_ge(*sig("gate_ps").at((l, i, q)))
                        nc.scalar.activation(gate_all[:, q // 2, (q % 2) * 512:(q % 2 + 1) * 512], (tmp if i else acc)[2 + q % 2][:, :], ACT.Copy).then_inc(*sig("gate_all").did((l, i, q)))

                for k in range(KD):
                    if k == 768 // P:
                        gates(0)
                    if k == 2:
                        act.wait_ge(*sig("hg_mean").at(l))
                        nc.scalar.activation(small[:, 32:48], small[:, 16:32], ACT.Sqrt).then_inc(*sig("hg_root").did(l))
                    act.wait_ge(*sig("oT_ps").at((l, k)))
                    nc.scalar.activation(hT_hi[:, k, a0:], tmp[k % 4][:, a0:], ACT.Copy).then_inc(*sig("oT_hi").did((l, k)))

                split.up_to(slab_at[("out", l, 1, 1)] + RING)
                for t in act_t:
                    act.wait_ge(*sig("acc_added").at((l, "out", 1, t)))
                    squares_of_x(l, 1, t)
                norm_roots(l, 1, act_t)
                gates(1)
                act.wait_ge(*sig("gate_all").at((l, 1, 3)))
                phase_end(act, "act", "out")
                norm_high(l, 1, act_t)
                phase_end(act, "act", "norm1")
                if l % 2 == 0:
                    for g, (j0, j1) in enumerate(FF_GROUPS):
                        for j in range(j0, j1):
                            split.up_to(slab_at[("gu", l, j, 1)] + 2)
                            for t in range(TILES):
                                n = j * TILES + t
                                act.wait_ge(*sig("acc_ready").at((("gu", l, j), t)))
                                if n >= 2:
                                    pj_, pt = divmod(n - 2, TILES)
                                    act.wait_ge(*sig("act_tok").at((l, pj_, pt)))
                                nc.scalar.activation(act_gate[:, n % 2, :], acc[t][:, 0:GU], ACT.Silu).then_inc(*sig("silu").did((l, j, t)))
                            for c in range(2):
                                act.wait_ge(*sig("aT_ps").at((l, 2 * j + c)))
                                if c == 0 and j == FF_GROUPS[g][0] and g:
                                    act.wait_ge(*sig("acc_ready").at((("down", l, g - 1, 1), TILES - 1)))
                                nc.scalar.activation(aT_hi[:, 2 * (j - j0) + c, :], tmp[(2 * j + c) % 3][:, :], ACT.Copy).then_inc(*sig("aT_hi").did((l, 2 * j + c)))
                        nk = 2 * (j1 - j0)
                        for n in range(2):
                            split.up_to(slab_at[("down", l, g, n, (nk - 1) // 4 * 4)] + 2)
                    act.wait_ge(*sig("aT_hi").at((l, 2 * FF_CHUNKS - 1)))
                    for t in range(TILES):
                        act.wait_ge(*sig("acc_added").at((l, "down", len(FF_GROUPS) - 1, 1, t)))
                        squares_of_x(l + 1, 0, t)
                    norm_roots(l + 1, 0, range(TILES))
                    phase_end(act, "act", "ffn")
                else:
                    experts_act(act)

        def experts_dve(dve, linked):
            tt, ts, stt = nc.vector.tensor_tensor, nc.vector.tensor_scalar, nc.vector.scalar_tensor_tensor
            marks["norm1"] = marks["dve"]
            dve.wait_ge(*lo_split.at(len(slabs) - 1))
            dve.sem_inc(sig("e_lo").sem, sig("e_lo").each())
            nc.vector.memset(ones_sq[:, :], 1.0)
            for r in range(4, 8):
                dve.wait_ge(*sig("h_tok_ps").at(r))
                if r == 4:
                    dve.wait_ge(*sig("h_tok_read").at(3))
                nc.vector.tensor_copy(h_tok_lo[:, r // 2 - 2, (r % 2) * 512:(r % 2 + 1) * 512], tmp[r % 4][:, :]).then_inc(*sig("h_tok_read").did(r))
            dve.wait_ge(*sig("logits").at())
            E = EXPERTS
            R = lambda i: route[:, i]
            wide = lambda i: route1[:, i].unsqueeze(2).broadcast_to([P, 2, E])
            order = c_("order8").unsqueeze(1).broadcast_to([P, 2, E])
            linked(nc.vector.tensor_copy(R(1), acc[0][:, 0:2 * E].rearrange("p (t e) -> p t e", t=2)))
            for i, (src, hot) in enumerate(((1, 2), (3, 4))):
                linked(nc.vector.tensor_reduce(route1[:, i], R(src), AX.X, ALU.max))
                linked(tt(R(5), R(src), wide(i), ALU.is_equal))
                linked(tt(R(5), R(5), order, ALU.mult))
                linked(nc.vector.tensor_reduce(route1[:, 2], R(5), AX.X, ALU.max))
                linked(tt(R(hot), R(5), wide(2), ALU.is_equal))
                if i == 0:
                    linked(stt(R(3), R(2), -3.0e38, R(1), ALU.mult, ALU.add))
            linked(tt(R(0), R(2), R(4), ALU.add))
            tt(route1[:, 4], route1[:, 1], route1[:, 0], ALU.subtract).then_inc(*sig("logit_gap").did())
            nc.vector.memset(items[:, :, 0:2], -1.0)
            nc.vector.memset(items[:, :, 2:4], 0.0).then_inc(*sig("chosen").did())
            dve.wait_ge(*sig("gap_exp").at())
            linked(ts(route1[:, 6], route1[:, 5], 1.0, None, ALU.add))
            linked(nc.vector.reciprocal(route1[:, 7], route1[:, 6]))
            linked(tt(route1[:, 8], route1[:, 7], route1[:, 5], ALU.mult))
            linked(tt(R(6), R(2), wide(7), ALU.mult))
            linked(tt(R(7), R(4), wide(8), ALU.mult))
            linked(tt(R(8), R(6), R(7), ALU.add))
            dve.wait_ge(*sig("ranks").at())
            linked(stt(R(9), acc[1][:, 0:2 * E].rearrange("p (t e) -> p t e", t=2), 1.0, R(0), ALU.add, ALU.mult))
            linked(nc.vector.tensor_reduce(route1[:, 9, 0:1], acc[1][:, 2 * E:3 * E], AX.X, ALU.max))
            for half in range(2):
                dst = items[:, 1 + half * E:1 + (half + 1) * E, :]
                ts(dst[:, :, 0:2].rearrange("p e t -> p t e"), R(9), -1.0 - P * half, None, ALU.add)
                linked(nc.vector.tensor_copy(dst[:, :, 2:4].rearrange("p e t -> p t e"), R(8)))
            ts(passes[:, :], route1[:, 9, 0:1], float(P), 1.0, ALU.is_gt, ALU.add).then_inc(*sig("passes_known").did())
            dve.wait_ge(*sig("passes_known").last())
            dve.wait_ge(*sig("h_tok_read").at(7))
            phase_end(dve, "dve", "route")
            marks["route"] = marks["dve"]
            for name in ("e_act", "e_rest", "e_add"):
                dve.sem_inc(sig(name).sem, sig(name).each())
            linked(nc.vector.memset(moe_sum[:, :, :], 0.0))
            linked(nc.vector.memset(pick_slot[:, :, :], 0.0))
            nc.vector.memset(acc[2][:, :], 0.0)
            nc.vector.memset(acc[3][:, :], 0.0).then_inc(*sig("y_cleared").did())

            def select(cols, signal):
                for t in range(2):
                    ins = ts(pick_tok[:, t, :], c_("slots"), cols[:, t:t + 1], None, ALU.is_equal)
                ins.then_inc(*signal.did(0))

            def gathered(at, signal):
                for r in range(4):
                    dve.wait_ge(*at(r))
                    nc.vector.tensor_copy(hg_lo[:, 2 * r:2 * r + 2, :], gather_banks[r][:, 2 * P:].rearrange("p (c s) -> p c s", c=2)).then_inc(*signal.did(r))

            def add(r, at, signal):
                t, n = divmod(r, 2)
                dve.wait_ge(*at)
                dst = moe_sum[:, t, n * 512:(n + 1) * 512]
                stt(dst, scatter_banks[r][:, :], cur[:, 2 + t:3 + t], dst, ALU.mult, ALU.add).then_inc(*signal.did(r))

            select(items[:, 1, 0:2], Prologue(sig("e_pick")))
            gathered(lambda r: sig("e_hg_hi").turn(r, 0), Prologue(sig("e_hg_lo")))

            def body(item, e):
                n = [0]

                def low(to):
                    while n[0] <= to:
                        q = n[0]
                        for half in range(2):
                            dve.wait_ge(*sig("e_hi").turn((q, half), item))
                            tt(e_half(w_lo, q, half), e_half(raw, q, half), e_half(w_hi, q, half).bitcast(F32), ALU.subtract).then_inc(*sig("e_lo").did((q, half)))
                        n[0] += 1

                def hidden_rest(j):
                    dve.wait_ge(*sig("e_high").turn(j, item))
                    tt(eT_lo[:, 2 * j:2 * j + 2, :], tmp[j % 2][:, 0:2 * P].rearrange("p (c s) -> p c s", c=2),
                       eT_hi[:, 2 * j:2 * j + 2, :].bitcast(F32), ALU.subtract).then_inc(*sig("e_rest").did(j))

                nc.vector.tensor_copy(cur[:, 2:4], items[:, item - 1, 2:4]).then_inc(*sig("e_cur").did(0))
                nc.vector.tensor_copy(cur[:, 0:2], items[:, item + 1, 0:2]).then_inc(*sig("e_cur").did(1))
                low(3)
                dve.wait_ge(sig("e_cur").sem, 2 * item)
                for r in range(4):
                    add(r, sig("e_scatter").turn(r, item), sig("e_add"))
                for j in range(FF_CHUNKS):
                    low(2 * j + 3)
                    dve.wait_ge(*sig("e_silu").turn(j, item))
                    dve.wait_ge(*(sig("e_hT_ps").turn(j - 2, item) if j >= 2 else sig("e_hT_ps").turn(j - 2 + FF_CHUNKS, item - 1)))
                    tt(e_tok[:, j % 2, :], e_gate[:, j % 2, :], acc[j % 2][:, GU:2 * GU], ALU.mult).then_inc(*sig("e_act").did(j))
                    if j:
                        hidden_rest(j - 1)
                dve.wait_ge(*sig("e_slot_ps").turn(0, item))
                select(cur[:, 0:2], sig("e_pick"))
                low(UP_SLABS + 3)
                hidden_rest(FF_CHUNKS - 1)
                low(UP_SLABS + 6)
                gathered(lambda r: sig("e_hg_hi").turn(r, item), sig("e_hg_lo"))
                low(E_SLABS - 1)

            end = experts_loop(dve, body)
            dve.wait_ge(*sig("e_add").turn(3, end - 1))
            nc.vector.tensor_copy(cur[:, 2:4], items[:, end - 1, 2:4]).then_inc(*sig("cur_last").did())
            dve.wait_ge(*sig("cur_last").at())
            for r in range(4):
                add(r, sig("scatter_last").at(r), sig("add_last"))
            dve.wait_ge(*sig("add_last").last())
            for t in range(2):
                linked(tt(moe_sum[:, t, :], moe_sum[:, t, :], gate_all[:, 0, :], ALU.mult))
                tt(x[:, 2 + t, :], x[:, 2 + t, :], moe_sum[:, t, :], ALU.add).then_inc(*sig("x_last").did(t))
            dve.wait_ge(*sig("final_sq").at(1))
            ts(small[:, 2:4], small[:, 0:2], 1.0 / D, 1e-6, ALU.mult, ALU.add).then_inc(*sig("final_mean").did())
            dve.wait_ge(*sig("final_root").at())
            linked(nc.vector.reciprocal(small[:, 6:8], small[:, 4:6]))
            dve.wait_ge(sig("final_gain_loaded").sem, 16)
            for t in range(2):
                stt(x[:, 2 + t, :], x[:, 2 + t, :], small[:, 6 + t:7 + t], final_gain[:, :], ALU.mult, ALU.mult).then_inc(*sig("final_x").did(t))

        @block.vector
        def _(dve):
            split = Splitter(dve, "lo")
            link = sig("dve_link")

            def linked(ins):
                ins.then_inc(*link.did())
                dve.wait_ge(*link.last())

            tt, ts, stt = nc.vector.tensor_tensor, nc.vector.tensor_scalar, nc.vector.scalar_tensor_tensor

            def normalised(l, which, tiles):
                a, bb = tiles[0], tiles[-1] + 1
                dve.wait_ge(*sig("sq").at((l, which, tiles[-1])))
                ts(small[:, 4 + a:4 + bb], small[:, a:bb], 1.0 / D, 1e-6, ALU.mult, ALU.add).then_inc(*sig("mean").did((l, which)))
                dve.wait_ge(*sig("root").at((l, which)))
                linked(nc.vector.reciprocal(small[:, 12 + a:12 + bb], small[:, 8 + a:8 + bb]))
                for t in tiles:
                    ins = ts(xn[:, t, :], x[:, t, :], small[:, 12 + t:13 + t], None, ALU.mult)
                ins.then_inc(*sig("xn_ready").did((l, which)))
                dve.wait_ge(*sig("xn_ready").last())

            def scaled_gain(l, which):
                gain = vecs[:, l, VEC["norm_ffn" if which else "norm_mix"]:][:, 0:KD].unsqueeze(2).broadcast_to([P, KD, 2])
                linked(stt(scale_col[:, :, :], mod_cols[:, l, 3 * which + 1], 1.0, gain, ALU.add, ALU.mult))

            def norm_rest(l, which, tiles):
                a, bb = tiles[0], tiles[-1] + 1
                for k in range(KD + 2):
                    if k < KD and k % 2 == 0:
                        dve.wait_ge(*sig("xT").at((l, which, k)))
                        if k >= HF:
                            dve.wait_ge(*sig("h_lo").at((l, which, k - HF)))
                        for sg in sorted({t // 2 for t in tiles}, reverse=True):
                            j = 1 - sg
                            ins = ts(hf[:, k % HF, sg * SEQ:(sg + 1) * SEQ], tmp[k % 4][:, sg * SEQ:(sg + 1) * SEQ],
                                     scale_col[:, k, j:j + 1], mod_cols[:, l, 3 * which, k, j:j + 1], ALU.mult, ALU.add)
                        ins.then_inc(*sig("modulated_by_dve").did((l, which, k)))
                    if k >= 2:
                        rest(l, which, k - 2, a * P, bb * P)
                dve.wait_ge(*sig("h_lo").last())

            def rest(l, which, k, a, bb):
                dve.wait_ge(*sig("h_hi").at((l, which, k)))
                tt(hT_lo[:, k, a:bb], hf[:, k % HF, a:bb], hT_hi[:, k, a:bb].bitcast(F32), ALU.subtract).then_inc(*sig("h_lo").did((l, which, k)))

            def lam_init(l):
                return 0.8 - 0.6 * math.exp(-0.3 * l)

            def scalars():
                dve.wait_ge(row_in.sem, 32)
                o_, w_ = ROW["diff_norm"]
                for l in range(DEPTH):
                    lv = lam_in[:, l, :].rearrange("p (a b d) -> p a b d", a=2, b=2)
                    prod = upd[:, l, 0:128].rearrange("p (a d) -> p a d", a=2)
                    linked(tt(prod, lv[:, :, 0], lv[:, :, 1], ALU.mult))
                    ins = nc.vector.tensor_reduce(lam[:, l, 0:2], prod, AX.X, ALU.add)
                    if l == DEPTH - 1:
                        ins.then_inc(*sig("lam_sums").did())
                    linked(ts(rows[:, l, o_:o_ + w_], rows[:, l, o_:o_ + w_], 1.0 - lam_init(l), None, ALU.mult))
                linked(nc.vector.memset(lb[:, 0, :], 0.0))
                lc = VEC["lb_logits"]
                tt(small[:, 32:36], vecs[:, 1, lc:lc + 4], vecs[:, 0, lc:lc + 4], ALU.subtract).then_inc(*sig("lb_diff").did())

            def mod_cols_add(l, n, bank):
                part, half = divmod(n, 2)
                dve.wait_ge(*sig("mod_cols_ps").at((l, n)))
                b = vecs[:, l, VEC["b_mod"] + 4 * n:VEC["b_mod"] + 4 * n + 4].unsqueeze(2).broadcast_to([P, 4, 2])
                tt(mod_cols[:, l, part, 4 * half:4 * half + 4, :], bank[:, 0:8].rearrange("p (k j) -> p k j", j=2), b, ALU.add)\
                    .then_inc(*sig("mod_cols").did((l, n)))

            dve.wait_ge(vec_in.sem, 32)
            dve.wait_ge(*consts_in_at())
            for l in range(DEPTH):
                act_t = active(l)
                if l == 0:
                    dve.wait_ge(*sig("cond_hi").at())
                    linked(tt(cond4[:, :, 2:4], cond_act[:, :, :], cond4[:, :, 0:2].bitcast(F32), ALU.subtract))
                    scalars()
                    mod_cols_add(0, 0, tmp[1])
                    dve.wait_ge(x_in.sem, 64)
                    normalised(0, 0, range(TILES))
                    for n in range(1, MOD_FIRST):
                        mod_cols_add(0, n, tmp[1])
                    split.up_to(slab_at[("in", 0, 0, 0)] + RING - 1)
                    dve.wait_ge(*sig("lam_exp").at())
                    for k in range(DEPTH):
                        linked(stt(lam[:, k, 4:5], lam[:, k, 3:4], -lam_init(k), lam[:, k, 2:3], ALU.add, ALU.subtract))
                    dve.wait_ge(*sig("lb").at())
                    linked(ts(one_less_lb[:, :, :], lb[:, :, :], -1.0, 1.0, ALU.mult, ALU.add))
                    dve.wait_ge(*sig("mod_cols").last())
                    scaled_gain(0, 0)
                    phase_end(dve, "dve", "mod")
                norm_rest(l, 0, range(TILES))
                phase_end(dve, "dve", "norm0")
                def rope(src, nh, half, table, t):
                    n = nh * half
                    cs, sn = [c_(f"{k}_{table}").rearrange("p (t f) -> p t f", t=2)[:, t - 2].unsqueeze(1).broadcast_to([P, nh, half]) for k in ("cos", "sin")]
                    x1, x2 = src[:, :, 0], src[:, :, 1]
                    t1, t2 = [rope_tmp[:, i, 0:n].rearrange("p (h f) -> p h f", h=nh) for i in range(2)]
                    tt(t1, x1, sn, ALU.mult)
                    linked(tt(t2, x2, sn, ALU.mult))
                    linked(tt(x1, x1, cs, ALU.mult))
                    linked(tt(x2, x2, cs, ALU.mult))
                    linked(tt(x1, x1, t2, ALU.subtract))
                    return tt(x2, x2, t1, ALU.add)

                b0 = slab_at[("in", l, 0, 0)]
                for c in range(len(IN_CHUNKS)):
                    split.up_to(b0 + 2 * c + 3)
                    for t in (2, 3):
                        a, bb = in_cols(l, c, t)
                        dve.wait_ge(*sig("acc_ready").at((("in", l, c), t)))
                        nc.vector.tensor_copy(pj[:, t, a:bb], acc[t][:, 0:bb - a]).then_inc(*sig("in_read_dve").did((l, c, t)))
                        sig("in_read_dve").seen[("all", l)] = sig("in_read_dve").count
                    if c in (2, 3):
                        dve.wait_ge(*sig("in_read_dve").at((l, 1, 3)))
                        linked(rope(pj[:, c, C_DQ:C_DV].rearrange("p (h e f) -> p h e f", e=2, f=DA_DIM // 2), 16, DA_DIM // 2, "da", c))
                    if c == 4:
                        for t in (2, 3):
                            dve.wait_ge(*sig("in_read_dve").at((l, 3, t)))
                            linked(rope(pj[:, t, C_KR:C_HQ].rearrange("p (h e f) -> p h e f", h=1, e=2), 1, MLA_ROPE // 2, "mla", t))
                        dve.wait_ge(*sig("c_sq").at(l))
                        a = act_t[0]
                        ts(stats[:, 8 + a:12], stats[:, a:4], 1.0 / MLA_Q, 1e-6, ALU.mult, ALU.add)
                        ts(stats[:, 12:16], stats[:, 4:8], 1.0 / MLA_KV, 1e-6, ALU.mult, ALU.add).then_inc(*sig("c_mean").did(l))
                    if c == 5:
                        dve.wait_ge(*sig("c_root").at(l))
                        linked(nc.vector.reciprocal(stats[:, 24 + act_t[0]:32], stats[:, 16 + act_t[0]:24]))
                        for t in range(TILES):
                            dve.wait_ge(*sig("in_read_act" if t < 2 else "in_read_dve").at((l, 3, t)))
                            if t in act_t:
                                ts(c_tok[:, t, 0:MLA_Q], pj[:, t, C_CQ:C_CKV], stats[:, 24 + t:25 + t], None, ALU.mult)
                            ts(c_tok[:, t, MLA_Q:], pj[:, t, C_CKV:C_KR], stats[:, 28 + t:29 + t], None, ALU.mult).then_inc(*sig("c_tok").did((l, t)))
                split.up_to(slab_at[("out", l, 0, 0) if l else ("mod", 0, MOD_FIRST, 0)] + RING - 1)
                dve.wait_ge(*sig("in_read_dve").last())
                dve.wait_ge(*sig("c_tok").last())
                phase_end(dve, "dve", "in")
                marks[("mla", l)] = marks["dve"]

                for s in range(TILES + 2):
                    if s < TILES:
                        dve.wait_ge(*sig("dakT_ps").at((l, s)))
                        nc.vector.tensor_copy(dakT[:, s, :], tmp[1][:, :]).then_inc(*sig("daT_read_dve").did((l, s)))
                    if 1 <= s <= TILES:
                        t = s - 1
                        dve.wait_ge(*sig("mkv_ps").at((l, t)))
                        if t >= 2:
                            dve.wait_ge(*sig("mkT_ps").at((l, t - 2)))
                        kv = acc[1][:, :].rearrange("p (h d) -> p h d", h=MLA_HEADS)
                        nc.vector.tensor_copy(k_tok[:, t % 2, :, 0:MLA_NOPE], kv[:, :, 0:MLA_NOPE])
                        kr = pj[:, t, C_KR:C_HQ].unsqueeze(1).broadcast_to([P, MLA_HEADS, MLA_ROPE])
                        nc.vector.tensor_copy(k_tok[:, t % 2, :, MLA_NOPE:], kr).then_inc(*sig("mk_roped").did((l, t)))
                        nc.vector.tensor_copy(pj[:, t, C_CQ:C_CQ + 256].rearrange("p (h d) -> p h d", h=MLA_HEADS), kv[:, :, MLA_NOPE:]).then_inc(*sig("kv_tok").did((l, t)))
                        if t >= 2:
                            dve.wait_ge(*sig("q_tok").at((l, t)))
                            src = q_tok[:, t % 2, :, MLA_NOPE:].rearrange("p h (e f) -> p h e f", e=2)
                            rope(src, MLA_HEADS, MLA_ROPE // 2, "mla", t).then_inc(*sig("mq_roped").did((l, t)))
                            dve.wait_ge(*sig("mq_roped").last())
                    if s >= 2:
                        t = s - 2
                        dve.wait_ge(*sig("mkT_ps").at((l, t)))
                        nc.vector.tensor_copy(mkT[:, :, t * P:(t + 1) * P], acc[3][0:MLA_QK, :].rearrange("p (h d) -> p h d", h=MLA_HEADS)).then_inc(*sig("mkT_read").did((l, t)))
                dve.wait_ge(*sig("mkT_read").last())
                phase_end(dve, "dve", "attn_prep")

                us = units(l)

                def finish(u):
                    kind, t, h = us[u]
                    dve.wait_ge(*sig("o_ps").at((l, u)))
                    o = acc[2 + u % 2]
                    s = 48 + 8 * (u % 2)
                    if kind == "mla":
                        ts(pj[:, t, 512 + h * 64:512 + (h + 1) * 64], o[:, 0:64], stats[:, s + 4:s + 5], None, ALU.mult).then_inc(*sig("attended").did((l, u)))
                        return
                    nc.vector.tensor_copy(pj[:, t, h * P:(h + 1) * P], o[:, 0:P]).then_inc(*sig("attended").did((l, u)))

                def maximum(u):
                    kind, t, h = us[u]
                    keys = TOK if t >= 2 else CTX
                    sc = (DA_DIM if kind == "da" else MLA_QK) ** -0.5
                    ng = 2 if kind == "da" else 1
                    o = 8 * (u % 2)
                    dve.wait_ge(*sig("scores").at((l, u)))
                    for g in range(ng):
                        ins = nc.vector.tensor_reduce(small[:, 16 + o + g:17 + o + g], tmp[2 * (u % 2) + g][:, 0:keys], AX.X, ALU.max)
                    linked(ins)
                    ts(stats[:, 32 + o:32 + o + ng], small[:, 16 + o:16 + o + ng], -sc, None, ALU.mult).then_inc(*sig("neg_max").did((l, u)))

                def weights(u):
                    kind, t, h = us[u]
                    keys = TOK if t >= 2 else CTX
                    ng = 2 if kind == "da" else 1
                    o = 8 * (u % 2)
                    s = 48 + o
                    dve.wait_ge(*sig("exp").at((l, u)))
                    if u >= 2:
                        dve.wait_ge(*sig("attended").at((l, u - 2)))
                    linked(nc.vector.reciprocal(stats[:, s + 4:s + 4 + ng] if kind == "mla" else stats[:, s:s + 2], stats[:, 34 + o:34 + o + ng]))
                    if kind == "da":
                        linked(tt(stats[:, s + 2:s + 3], stats[:, s + 1:s + 2], lam[:, l, 4:5], ALU.mult))
                        linked(ts(probs[:, u % 2, 1, 0:keys], probs[:, u % 2, 1, 0:keys], stats[:, s + 2:s + 3], None, ALU.mult))
                        stt(probs[:, u % 2, 0, 0:keys], probs[:, u % 2, 0, 0:keys], stats[:, s:s + 1], probs[:, u % 2, 1, 0:keys], ALU.mult, ALU.add).then_inc(*sig("probs").did((l, u)))

                for u in range(len(us) + 2):
                    if 1 <= u <= len(us):
                        weights(u - 1)
                    if u < len(us):
                        maximum(u)
                    if l == 0 and u >= BESIDE_UNIT:
                        n, kh = divmod(u - BESIDE_UNIT + 2 * MOD_FIRST, 2)
                        if kh == 0 and n > MOD_FIRST + 1:
                            mod_cols_add(0, n - 2, tmp[3])
                        if u <= len(us):
                            split.up_to(slab_at[("mod", 0, MOD_FIRST, 0)] + u - BESIDE_UNIT + 1)
                    if u >= 2:
                        finish(u - 2)
                if l == 0:
                    mod_cols_add(0, MOD_CHUNKS - 1, tmp[3])
                    dve.wait_ge(*sig("mod_cols").last())
                dve.wait_ge(*sig("attended").last())
                phase_end(dve, "dve", "attn")
                marks[("attn", l)] = marks["dve"]

                for i in range(4):
                    dve.wait_ge(*sig("gate_sig").at((l, i)))
                    ts(hkT[:, i, :], hkT[:, i, :], one_less_lb[:, l, i:i + 1], None, ALU.mult).then_inc(*sig("hk").did((l, i)))
                ones = c_("ones").broadcast_to([P, SEQ])
                for i in range(4):
                    dve.wait_ge(*sig("logf").at((l, i)))
                    for sg in range(2):
                        a, bb = sg * SEQ, (sg + 1) * SEQ
                        o, g = cum[:, i, a:bb], sig_f[:, i, a:bb]
                        if i >= 2:
                            o, g = o[:, ::-1], g[:, ::-1]
                        ins = nc.vector.tensor_tensor_scan(o, ones, g, 0.0, ALU.mult, ALU.add)
                    ins.then_inc(*sig("cum").did((l, i)))
                dve.wait_ge(*sig("cum").last())
                dve.wait_ge(*sig("hk").last())
                dve.wait_ge(*sig("gate_sig").at((l, 5)))
                S0 = act_t[0] * P
                T = TOK - S0
                gains = [rows[:, l, o_:o_ + w_] for o_, w_ in (ROW["diff_norm"], ROW["hgrn_norm"])]
                steps = level_steps()
                heads = [slice(0, 64), slice(64, P)]

                def blocks(ap, m):
                    return ap.rearrange("p (b e m) -> p b e m", e=2, m=m)

                def scaled(i):
                    p, n, m = steps[i]
                    f, bk = p, 2 + p
                    buf = n % 2
                    if i >= 2:
                        dve.wait_ge(*sig("s_ps").at((l, i - 2, 1)))
                    done = sig("level").did((l, p, n))
                    if m == 0:
                        tt(lev_k[:, buf, 0, S0:], hkT[:, f, S0:], hkT[:, bk, S0:], ALU.add).then_inc(*done)
                        return
                    d = dec[:, i % DECAYS]
                    dve.wait_ge(*sig("dec_exp").at((l, p, n)))
                    if m <= 128:
                        q_, kf_, kb_ = blocks(hqT[:, p, S0:], m), blocks(hkT[:, f, S0:], m), blocks(hkT[:, bk, S0:], m)
                        dv = [d[:, q, 0:T // 2].rearrange("p (b m) -> p b m", m=m) for q in range(4)]
                        for r, h in zip(heads, range(2)):
                            for e in range(2):
                                tt(lev_q[r, buf, e, h, 0:T // 2].rearrange("p (b m) -> p b m", m=m), q_[r, :, 1 - e], dv[2 * e][r], ALU.mult)
                        lk = [blocks(lev_k[:, buf, q, S0:], m) for q in range(2)]
                        tt(lk[0][:, :, 0], kf_[:, :, 0], dv[1], ALU.mult)
                        tt(lk[1][:, :, 1], kb_[:, :, 1], dv[3], ALU.mult).then_inc(*done)
                    else:
                        for r, h in zip(heads, range(2)):
                            for e in range(2):
                                tt(lev_q[r, buf, e, h, :], hqT[r, p, CTX:], d[r, 2 * e, :], ALU.mult)
                        tt(lev_k[:, buf, 0, 0:CTX], hkT[:, f, 0:CTX], d[:, 1, :], ALU.mult)
                        tt(lev_k[:, buf, 1, 0:CTX], hkT[:, bk, 0:CTX], d[:, 3, :], ALU.mult).then_inc(*done)

                def placed(i):
                    p, n, m = steps[i]
                    if m > 64:
                        return
                    for b in level_banks(l, m):
                        dve.wait_ge(*sig("s_ps").at((l, i, b)))
                        if p and n == 0:
                            dve.wait_ge(*sig("hg_o").at((l, 0)))
                        if m == 0:
                            src = level_bank(i, b)[:, S0:].rearrange("p (t q) -> p t q", q=P)
                            ins = nc.vector.tensor_copy(s_diag[:, b, act_t[0]:, :], src)
                        else:
                            src = level_bank(i, b)[:, :].rearrange("p (t h q) -> p h t q", t=2, h=2)
                            dst = s_diag[:, :, 2 * b:2 * b + 2, :]
                            dve.wait_ge(*sig("s_read").at((l, i - 1, 1)))
                            mk = c_("masks").rearrange("p (v q) -> p v q", q=P)[:, LEVELS.index(m)].bitcast(mybir.dt.int32)
                            ins = nc.vector.copy_predicated(dst, mk.unsqueeze(1).unsqueeze(1).broadcast_to([P, 2, 2, P]), src)
                        ins.then_inc(*sig("s_read").did((l, i, b)))

                dve.wait_ge(*sig("lev_clear").at(l))
                for i in range(len(steps) + 1):
                    if i < len(steps):
                        scaled(i)
                    if l == 0:
                        c, kh = divmod(AHEAD_OF_LEVELS + i, 2)
                        if kh == 0:
                            mod_cols_add(1, c - 2, acc[3])
                    if i:
                        placed(i - 1)
                    if 0 <= i - 1 - SQUARES_AT < len(act_t) // 2:
                        tp = act_t[0] // 2 + i - 1 - SQUARES_AT
                        if i == 1 + SQUARES_AT:
                            linked(nc.vector.memset(stats[:, 0:16], 0.0))
                        dve.wait_ge(*sig("da_sq").at((l, tp)))
                        nc.vector.tensor_reduce(stats[:, 8 * tp:8 * tp + 8], squared[:, :, :].rearrange("p t (h d) -> p (t h) d", d=P), AX.X, ALU.add)\
                            .then_inc(*sig("da_sum").did((l, tp)))
                        if tp == 1:
                            dve.wait_ge(*sig("da_sum").last())
                            ts(stats[:, 16:32], stats[:, 0:16], 1.0 / P, 1e-5, ALU.mult, ALU.add).then_inc(*sig("da_mean").did(l))
                    if i == GAINS_AT:
                        dve.wait_ge(*sig("da_root").at(l))
                        linked(nc.vector.reciprocal(stats[:, 48:64], stats[:, 32:48]))
                    if 0 <= i - GAINS_AT < len(act_t):
                        t = act_t[i - GAINS_AT]
                        da_o = pj[:, t, 0:512].rearrange("p (h d) -> p h d", h=DA_HEADS)
                        linked(tt(da_o, da_o, stats[:, 48 + 4 * t:52 + 4 * t].unsqueeze(2).broadcast_to([P, DA_HEADS, P]), ALU.mult))
                        linked(tt(da_o, da_o, gains[0].unsqueeze(1).broadcast_to([P, DA_HEADS, P]), ALU.mult))
                if l == 0:
                    mod_cols_add(1, MOD_CHUNKS - 1, acc[3])
                    split.up_to(slab_at[("out", l, 0, 0)])
                    dve.wait_ge(*sig("mod_cols").last())
                pairs = range(act_t[0] // 2, 2)
                heads8 = lambda ap: ap.rearrange("p (h d) -> p h d", d=HG_DIM)
                linked(nc.vector.memset(small[:, 0:16], 0.0))
                phase_end(dve, "dve", "hg")

                def mix_rest(k):
                    dve.wait_ge(*sig("oT_hi").at((l, k)))
                    tt(hT_lo[:, k, S0:], tmp[k % 4][:, S0:], hT_hi[:, k, S0:].bitcast(F32), ALU.subtract).then_inc(*sig("oT_lo").did((l, k)))

                for tp in pairs:
                    dve.wait_ge(*sig("hg_sq").at((l, tp)))
                    ins = nc.vector.tensor_reduce(small[:, 8 * tp:8 * tp + 8], heads8(squared[:, tp, :]), AX.X, ALU.add)
                linked(ins)
                ts(small[:, 16:32], small[:, 0:16], 1.0 / HG_DIM, 1e-6, ALU.mult, ALU.add).then_inc(*sig("hg_mean").did(l))
                mix_rest(0)
                mix_rest(1)
                dve.wait_ge(*sig("hg_root").at(l))
                linked(nc.vector.reciprocal(small[:, 48:64], small[:, 32:48]))
                for tp in pairs:
                    ins = tt(heads8(squared[:, tp, :]), heads8(acc[tp][:, :]), small[:, 48 + 8 * tp:56 + 8 * tp].unsqueeze(2).broadcast_to([P, 8, HG_DIM]), ALU.mult)
                linked(ins)
                for tp in pairs:
                    ins = tt(heads8(squared[:, tp, :]), heads8(squared[:, tp, :]), gains[1].unsqueeze(1).broadcast_to([P, 8, HG_DIM]), ALU.mult)
                linked(ins)
                dve.wait_ge(*sig("hg_silu").at(l))
                for tp in pairs:
                    tt(pj[:, 2 * tp:2 * tp + 2, 768:1024], squared[:, tp, :].rearrange("p (t f) -> p t f", t=2), pj[:, 2 * tp:2 * tp + 2, C_HG:C_HG + 256], ALU.mult)\
                        .then_inc(*sig("mixed").did((l, 2 * tp + 1)))
                for k in range(2, KD):
                    mix_rest(k)
                    if l == 0 and k == 4:
                        split.up_to(slab_at[("out", l, 0, 0)] + 1)
                dve.wait_ge(*sig("mixed").last())

                def add_gated(key, t, n):
                    j = 1 - t // 2
                    dve.wait_ge(*sig("acc_ready").at((key, t)))
                    linked(tt(upd[:, 0, :], acc[t][:, :], gate_all[:, j, n * 512:(n + 1) * 512], ALU.mult))
                    return tt(x[:, t, n * 512:(n + 1) * 512], x[:, t, n * 512:(n + 1) * 512], upd[:, 0, :], ALU.add)

                dve.wait_ge(*sig("gate_all").at((l, 0, 3)))
                for n in range(2):
                    split.up_to(slab_at[("out", l, n, 1)] + 2)
                    for t in act_t:
                        add_gated(("out", l, n), t, n).then_inc(*sig("acc_added").did((l, "out", n, t)))
                        dve.wait_ge(*sig("acc_added").last())
                scaled_gain(l, 1)
                normalised(l, 1, act_t)
                phase_end(dve, "dve", "out")
                norm_rest(l, 1, act_t)
                phase_end(dve, "dve", "norm1")
                if l % 2 == 0:
                    for g, (j0, j1) in enumerate(FF_GROUPS):
                        for j in range(j0, j1):
                            split.up_to(slab_at[("gu", l, j, 1)] + 2)
                            for t in range(TILES):
                                n = j * TILES + t
                                dve.wait_ge(*sig("silu").at((l, j, t)))
                                if j:
                                    dve.wait_ge(*sig("aT_ps").at((l, 2 * j - 1)))
                                tt(act_tok[:, t, :], act_gate[:, n % 2, :], acc[t][:, GU:2 * GU], ALU.mult).then_inc(*sig("act_tok").did((l, j, t)))
                            for c in range(2):
                                dve.wait_ge(*sig("aT_hi").at((l, 2 * j + c)))
                                kc = 2 * (j - j0) + c
                                tt(aT_lo[:, kc, :], tmp[(2 * j + c) % 3][:, :], aT_hi[:, kc, :].bitcast(F32), ALU.subtract).then_inc(*sig("aT_lo").did((l, 2 * j + c)))
                        nk = 2 * (j1 - j0)
                        for n in range(2):
                            split.up_to(slab_at[("down", l, g, n, (nk - 1) // 4 * 4)] + 2)
                            for t in range(TILES):
                                add_gated(("down", l, g, n), t, n).then_inc(*sig("acc_added").did((l, "down", g, n, t)))
                                dve.wait_ge(*sig("acc_added").last())
                    scaled_gain(l + 1, 0)
                    normalised(l + 1, 0, range(TILES))
                    phase_end(dve, "dve", "ffn")
                    marks[("layer", l + 1)] = marks["dve"]
                else:
                    experts_dve(dve, linked)

        seen.update({k: s.seen for k, s in signals.items()})
        seen["phases"] = {k: v for k, v in marks.items() if k not in ("pe", "act", "dve")}


def layout(inputs):
    f = lambda k: np.ascontiguousarray(np.asarray(inputs[k]))
    cols = lambda v: v.reshape(-1, P).T
    arrays = {k: f(k) for k in ("x", "ctx", "w_mod", "w_in", "w_out", "mla_w_uq", "mla_w_ukv", "ffn_w_gate",
                                "ffn_w_up", "ffn_w_down", "moe_router", "moe_w_gate", "moe_w_up", "moe_w_down")}
    arrays["consts"] = constants()[0]
    arrays["cond"] = np.stack([cols(f("c")[0]), cols(f("c_ctx"))], 2).reshape(P, -1)
    vecs = np.zeros((P, DEPTH, VEC_COLS), np.float32)
    rows = np.zeros((P, DEPTH, ROW_COLS), np.float32)
    for l in range(DEPTH):
        for name, v in (("norm_mix", f("norm_mix")[l]), ("norm_ffn", f("norm_ffn")[l]), ("q_norm", f("mla_q_norm")[l]),
                        ("kv_norm", f("mla_kv_norm")[l]), ("lb_logits", f("hgrn_lb_logits")[:, l]), ("b_mod", f("b_mod")[l])):
            c = cols(v)
            vecs[:, l, VEC[name]:VEC[name] + c.shape[1]] = c
        for name, v in (("diff_norm", f("diff_norm")[l]), ("hgrn_norm", f("hgrn_norm")[l]), ("diff_lambda", f("diff_lambda")[l])):
            o, w = ROW[name]
            rows[:, l, o:o + w] = v.reshape(-1)
    arrays["vecs"], arrays["rows"] = vecs, rows
    arrays["norm_final"] = np.tile(f("norm_final"), (P, 1))
    return {k: np.ascontiguousarray(v) for k, v in arrays.items()}


def kernel(**inputs):
    import concourse.bacc as bacc
    from concourse.bass_utils import run_bass_kernel_spmd

    arrays = layout(inputs)

    def build(known):
        nc = bacc.Bacc("TRN2", target_bir_lowering=False, num_devices=1)
        dram = {k: nc.dram_tensor(k, v.shape, mybir.dt.from_np(v.dtype), kind="ExternalInput").ap() for k, v in arrays.items()}
        out = nc.dram_tensor("out", (1, SEQ, D), F32, kind="ExternalOutput").ap()
        seen = {}
        program(nc, dram, out, known, seen)
        return nc, seen

    nc, seen = build(build({})[1])
    return run_bass_kernel_spmd(nc, [arrays], core_ids=[0]).results[0]["out"]
```
